# Optimizing a Trainium2 kernel written in Bass

```python
import math
import jax, jax.numpy as jnp
from jax import lax
import numpy as np

D_MODEL = 1024
BATCH = 1
SEQ = 512
DEPTH = 1

D_SSM = 512
SSM_GROUP = 16
N_SSM_GROUPS = D_SSM // SSM_GROUP
SSM_STATE = 64
D_ATTN = 512
HEAD_DIM = 64
N_HEADS = D_ATTN // HEAD_DIM
D_MIX = D_SSM + D_ATTN
D_IN = D_SSM + 3 * D_ATTN
MOBA_BLOCK = 256
MOBA_TOPK = 3
Q_CHUNK = 32
N_BUCKETS = 32
MAX_DISTANCE = 128
N_MEM = 256
X_HEADS = 4
X_HEAD_DIM = 128
D_X = X_HEADS * X_HEAD_DIM
D_FF = 2816
CONV_W = 3
EPS = 1e-6
NEG = -1e30

kernel_name = 'hybrid_s5_moba_memxattn_convffn'

def rms_norm(x, g):
    xf = x.astype(jnp.float32)
    y = xf * lax.rsqrt(jnp.mean(xf * xf, axis=-1, keepdims=True) + EPS)
    return (y * g.astype(jnp.float32)).astype(x.dtype)

def t5_bucket(dist):
    n = jnp.maximum(dist, 0)
    max_exact = N_BUCKETS // 2
    nf = jnp.maximum(n, max_exact).astype(jnp.float32)
    large = max_exact + (jnp.log(nf / max_exact) / math.log(MAX_DISTANCE / max_exact)
                         * (N_BUCKETS - max_exact)).astype(jnp.int32)
    large = jnp.minimum(large, N_BUCKETS - 1)
    return jnp.where(n < max_exact, n, large)

def s5_mixer(u, lam_re, lam_im, log_step, b_re, b_im, c_re, c_im, d_skip, w_glu, b_glu):
    bsz, t = u.shape[0], u.shape[1]
    f32 = jnp.float32
    dt_ = u.dtype
    a_re = jnp.minimum(lam_re.astype(f32), -1e-4)
    a_im = lam_im.astype(f32)
    step = jnp.exp(log_step.astype(f32))[:, None]
    mag = jnp.exp(step * a_re)
    ab_re = mag * jnp.cos(step * a_im)
    ab_im = mag * jnp.sin(step * a_im)
    den = a_re * a_re + a_im * a_im
    p = ab_re - 1.0
    f_re = (p * a_re + ab_im * a_im) / den
    f_im = (ab_im * a_re - p * a_im) / den
    bb_re = f_re[..., None] * b_re - f_im[..., None] * b_im
    bb_im = f_re[..., None] * b_im + f_im[..., None] * b_re
    ug = u.reshape(bsz, t, N_SSM_GROUPS, SSM_GROUP)
    bu_re = jnp.einsum('btgc,gnc->btgn', ug, bb_re.astype(dt_))
    bu_im = jnp.einsum('btgc,gnc->btgn', ug, bb_im.astype(dt_))
    a_re_t = jnp.broadcast_to(ab_re.astype(dt_), (1, t) + ab_re.shape)
    a_im_t = jnp.broadcast_to(ab_im.astype(dt_), (1, t) + ab_im.shape)

    def combine(e1, e2):
        a1r, a1i, b1r, b1i = e1
        a2r, a2i, b2r, b2i = e2
        return (a2r * a1r - a2i * a1i,
                a2r * a1i + a2i * a1r,
                a2r * b1r - a2i * b1i + b2r,
                a2r * b1i + a2i * b1r + b2i)

    _, _, s_re, s_im = lax.associative_scan(combine, (a_re_t, a_im_t, bu_re, bu_im), axis=1)
    y = (jnp.einsum('gcn,btgn->btgc', c_re.astype(dt_), s_re)
         - jnp.einsum('gcn,btgn->btgc', c_im.astype(dt_), s_im))
    y = y.reshape(bsz, t, D_SSM) + d_skip * u
    y = jax.nn.gelu(y)
    return y * jax.nn.sigmoid(y @ w_glu + b_glu)

def moba_attention(q, k, v, rel_bias):
    bsz, t = q.shape[0], q.shape[1]
    f32 = jnp.float32
    nb = -(-t // MOBA_BLOCK)
    t_pad = nb * MOBA_BLOCK
    pad = ((0, 0), (0, t_pad - t), (0, 0), (0, 0))
    qp = jnp.pad(q, pad).transpose(0, 2, 1, 3)
    kb = jnp.pad(k, pad).transpose(0, 2, 1, 3).reshape(bsz, N_HEADS, nb, MOBA_BLOCK, HEAD_DIM)
    vb = jnp.pad(v, pad).transpose(0, 2, 1, 3).reshape(bsz, N_HEADS, nb, MOBA_BLOCK, HEAD_DIM)
    k_mean = jnp.mean(kb.astype(f32), axis=3).astype(q.dtype)
    top_k = min(MOBA_TOPK, nb)
    bias_t = rel_bias.T
    scale = HEAD_DIM ** -0.5
    b_ix = jnp.arange(bsz)[:, None, None, None]
    h_ix = jnp.arange(N_HEADS)[None, :, None, None]
    h_ix5 = h_ix[..., None]
    blk_ar = jnp.arange(MOBA_BLOCK, dtype=jnp.int32)
    blocks = jnp.arange(nb, dtype=jnp.int32)

    def chunk(c):
        q0 = c * Q_CHUNK
        own = q0 // MOBA_BLOCK
        qc = lax.dynamic_slice_in_dim(qp, q0, Q_CHUNK, axis=2)
        qpos = q0 + jnp.arange(Q_CHUNK, dtype=jnp.int32)
        gate = jnp.einsum('bhqd,bhnd->bhqn', qc, k_mean).astype(f32)
        gate = jnp.where(blocks < own, gate, -jnp.inf)
        gval, gidx = lax.top_k(gate, top_k)
        sel_ok = jnp.isfinite(gval)
        ks = kb[b_ix, h_ix, gidx]
        vs = vb[b_ix, h_ix, gidx]
        kpos_sel = gidx[..., None] * MOBA_BLOCK + blk_ar
        s_sel = jnp.einsum('bhqd,bhqskd->bhqsk', qc, ks).astype(f32) * scale
        s_sel = s_sel + bias_t[h_ix5, t5_bucket(qpos[:, None, None] - kpos_sel)].astype(f32)
        s_sel = jnp.where(sel_ok[..., None], s_sel, NEG)
        k_own = lax.dynamic_index_in_dim(kb, own, axis=2, keepdims=False)
        v_own = lax.dynamic_index_in_dim(vb, own, axis=2, keepdims=False)
        dist_own = qpos[:, None] - (own * MOBA_BLOCK + blk_ar)[None, :]
        s_own = jnp.einsum('bhqd,bhkd->bhqk', qc, k_own).astype(f32) * scale
        s_own = s_own + bias_t[:, t5_bucket(dist_own)].astype(f32)
        s_own = jnp.where(dist_own >= 0, s_own, NEG)
        logits = jnp.concatenate(
            [s_sel.reshape(bsz, N_HEADS, Q_CHUNK, top_k * MOBA_BLOCK), s_own], axis=-1)
        prob = jax.nn.softmax(logits, axis=-1).astype(v.dtype)
        p_sel = prob[..., :top_k * MOBA_BLOCK].reshape(bsz, N_HEADS, Q_CHUNK, top_k, MOBA_BLOCK)
        p_own = prob[..., top_k * MOBA_BLOCK:]
        return (jnp.einsum('bhqsk,bhqskd->bhqd', p_sel, vs)
                + jnp.einsum('bhqk,bhkd->bhqd', p_own, v_own))

    outs = lax.map(chunk, jnp.arange(t_pad // Q_CHUNK, dtype=jnp.int32))
    out = outs.transpose(1, 0, 3, 2, 4).reshape(bsz, t_pad, D_ATTN)
    return out[:, :t]

def memory_cross_attention(h, mem_n, w_q, w_kv, w_o, qn, kn):
    bsz, t = h.shape[0], h.shape[1]
    m = mem_n.shape[1]
    q = rms_norm((h @ w_q).reshape(bsz, t, X_HEADS, X_HEAD_DIM), qn)
    kv = mem_n @ w_kv
    k = rms_norm(kv[..., :D_X].reshape(bsz, m, X_HEADS, X_HEAD_DIM), kn)
    v = kv[..., D_X:].reshape(bsz, m, X_HEADS, X_HEAD_DIM)
    s = jnp.einsum('bqhd,bmhd->bhqm', q, k).astype(jnp.float32) * (X_HEAD_DIM ** -0.5)
    prob = jax.nn.softmax(s, axis=-1).astype(v.dtype)
    o = jnp.einsum('bhqm,bmhd->bqhd', prob, v).reshape(bsz, t, D_X)
    return o @ w_o

def conv_ffn(h, w_up, conv_w, conv_b, w_down):
    up = h @ w_up
    upc = lax.conv_general_dilated(
        up, conv_w.astype(up.dtype), window_strides=(1,), padding=[(CONV_W - 1, 0)],
        dimension_numbers=('NWC', 'WIO', 'NWC'), feature_group_count=2 * D_FF) + conv_b
    gate, val = upc[..., :D_FF], upc[..., D_FF:]
    return (jax.nn.silu(gate) * val) @ w_down

def setup_inputs(seed: int = 0) -> dict:
    key = jax.random.key(seed)
    ks = jax.random.split(key, 40)
    f32 = jnp.float32
    L = DEPTH

    def nrm(k, shape, scale):
        return jax.random.normal(k, shape, f32) * scale

    def gain(k, shape):
        return 1.0 + 0.02 * jax.random.normal(k, shape, f32)

    G, N, C = N_SSM_GROUPS, SSM_STATE, SSM_GROUP
    return {
        'x': nrm(ks[0], (BATCH, SEQ, D_MODEL), 1.0),
        'mem': nrm(ks[1], (BATCH, N_MEM, D_MODEL), 1.0),
        'norm_mix': gain(ks[2], (L, D_MODEL)),
        'w_in': nrm(ks[3], (L, D_MODEL, D_IN), D_MODEL ** -0.5),
        'attn_qn': gain(ks[4], (L, HEAD_DIM)),
        'attn_kn': gain(ks[5], (L, HEAD_DIM)),
        'ssm_lam_re': -0.5 + 0.01 * jax.random.normal(ks[6], (L, G, N), f32),
        'ssm_lam_im': jnp.pi * jnp.arange(N, dtype=f32) + 0.01 * jax.random.normal(ks[7], (L, G, N), f32),
        'ssm_log_step': jax.random.uniform(ks[8], (L, G), f32, minval=math.log(1e-3), maxval=math.log(1e-1)),
        'ssm_b_re': nrm(ks[9], (L, G, N, C), (2 * C) ** -0.5),
        'ssm_b_im': nrm(ks[10], (L, G, N, C), (2 * C) ** -0.5),
        'ssm_c_re': nrm(ks[11], (L, G, C, N), (2 * N) ** -0.5),
        'ssm_c_im': nrm(ks[12], (L, G, C, N), (2 * N) ** -0.5),
        'ssm_d': nrm(ks[13], (L, D_SSM), 0.5),
        'ssm_w_glu': nrm(ks[14], (L, D_SSM, D_SSM), D_SSM ** -0.5),
        'ssm_b_glu': nrm(ks[15], (L, D_SSM), 0.01),
        'gnorm_ssm': gain(ks[16], (L, D_SSM)),
        'gnorm_attn': gain(ks[17], (L, D_ATTN)),
        'w_out': nrm(ks[18], (L, D_MIX, D_MODEL), D_MIX ** -0.5),
        'rel_bias': nrm(ks[19], (N_BUCKETS, N_HEADS), 0.5),
        'norm_xattn': gain(ks[20], (L, D_MODEL)),
        'norm_mem': gain(ks[21], (L, D_MODEL)),
        'x_wq': nrm(ks[22], (L, D_MODEL, D_X), D_MODEL ** -0.5),
        'x_wkv': nrm(ks[23], (L, D_MODEL, 2 * D_X), D_MODEL ** -0.5),
        'x_wo': nrm(ks[24], (L, D_X, D_MODEL), D_X ** -0.5),
        'x_qn': gain(ks[25], (L, X_HEAD_DIM)),
        'x_kn': gain(ks[26], (L, X_HEAD_DIM)),
        'norm_ffn': gain(ks[27], (L, D_MODEL)),
        'ffn_w_up': nrm(ks[28], (L, D_MODEL, 2 * D_FF), D_MODEL ** -0.5),
        'ffn_conv_w': nrm(ks[29], (L, CONV_W, 1, 2 * D_FF), CONV_W ** -0.5),
        'ffn_conv_b': nrm(ks[30], (L, 2 * D_FF), 0.01),
        'ffn_w_down': nrm(ks[31], (L, D_FF, D_MODEL), D_FF ** -0.5),
    }

def reference(x, mem, norm_mix, w_in, attn_qn, attn_kn, ssm_lam_re, ssm_lam_im, ssm_log_step,
              ssm_b_re, ssm_b_im, ssm_c_re, ssm_c_im, ssm_d, ssm_w_glu, ssm_b_glu,
              gnorm_ssm, gnorm_attn, w_out, rel_bias, norm_xattn, norm_mem, x_wq, x_wkv, x_wo,
              x_qn, x_kn, norm_ffn, ffn_w_up, ffn_conv_w, ffn_conv_b, ffn_w_down):
    bsz, t = x.shape[0], x.shape[1]
    h = x
    for l in range(DEPTH):
        hn = rms_norm(h, norm_mix[l])
        proj = hn @ w_in[l]
        u_ssm = proj[..., :D_SSM]
        q = proj[..., D_SSM:D_SSM + D_ATTN].reshape(bsz, t, N_HEADS, HEAD_DIM)
        k = proj[..., D_SSM + D_ATTN:D_SSM + 2 * D_ATTN].reshape(bsz, t, N_HEADS, HEAD_DIM)
        v = proj[..., D_SSM + 2 * D_ATTN:].reshape(bsz, t, N_HEADS, HEAD_DIM)
        q = rms_norm(q, attn_qn[l])
        k = rms_norm(k, attn_kn[l])
        y_ssm = s5_mixer(u_ssm, ssm_lam_re[l], ssm_lam_im[l], ssm_log_step[l], ssm_b_re[l],
                         ssm_b_im[l], ssm_c_re[l], ssm_c_im[l], ssm_d[l], ssm_w_glu[l], ssm_b_glu[l])
        y_att = moba_attention(q, k, v, rel_bias)
        mixed = jnp.concatenate([rms_norm(y_ssm, gnorm_ssm[l]), rms_norm(y_att, gnorm_attn[l])], axis=-1)
        h = h + mixed @ w_out[l]
        h = h + memory_cross_attention(rms_norm(h, norm_xattn[l]), rms_norm(mem, norm_mem[l]),
                                       x_wq[l], x_wkv[l], x_wo[l], x_qn[l], x_kn[l])
        h = h + conv_ffn(rms_norm(h, norm_ffn[l]), ffn_w_up[l], ffn_conv_w[l], ffn_conv_b[l], ffn_w_down[l])
    return h


_drawn_inputs = setup_inputs


def setup_inputs(seed=0):
    import zlib

    import numpy as np

    out = dict(_drawn_inputs(seed))
    spreads = {}
    factors = {'attn_qn': 5.674,
     'attn_kn': 4.923,
     'ssm_lam_re': 64.0,
     'ssm_b_glu': 8.0,
     'gnorm_ssm': 5.247,
     'gnorm_attn': 5.437,
     'norm_xattn': 8.0,
     'norm_mem': 8.0,
     'x_qn': 8.0,
     'x_kn': 8.0,
     'norm_ffn': 5.36,
     'ffn_conv_b': 23.117}
    for name, (base, spread) in spreads.items():
        noise = np.random.default_rng([zlib.crc32(name.encode()), seed]).standard_normal(out[name].shape)
        drawn = base * np.exp(spread * noise) if base else spread * noise
        out[name] = __import__('jax').numpy.asarray(drawn.astype(out[name].dtype))
    for name, factor in factors.items():
        out[name] = (out[name] * factor).astype(out[name].dtype)
    return out
```

```python
import math
from contextlib import ExitStack

import numpy as np
import concourse.bass as bass
from concourse import mybir

T = 512
TT = T // 128
D = 1024
KD = D // 128
DS = 512
G, CG, NS = 32, 16, 64
GP = G // 2
H, HD = 8, 64
M = 256
MT = M // 128
XH, XD = 4, 128
DF = 2816
FT = DF // 128
EPS = 1e-6
NEG = -1e30
NB, MAXD = 32, 128
L = 8
NC = T // L
QG = 8
NQ = G // QG
QP = QG // 2

GAINS = [("norm_xattn", 8), ("norm_mem", 8), ("norm_ffn", 8), ("gnorm_ssm", 4),
         ("gnorm_attn", 4), ("ssm_d", 4), ("ssm_b_glu", 4), ("x_qn", 1), ("x_kn", 1),
         ("attn_qn", 1), ("attn_kn", 1)]
N_GAIN = len(GAINS) + 2
COL = {}
_at = 0
for _n, _k in GAINS:
    COL[_n] = _at
    _at += _k
NG = _at

U_SSM, U_Q, U_K, U_V, U_MK, U_MV = 0, 4, 8, 12, 16, 20
U_GLU, U_OUT, U_XQ, U_XO, U_UP, U_DOWN = 24, 26, 34, 38, 42, 86
U_END = U_DOWN + FT


def bucket_table():
    t = np.zeros((NB + 1, 384), np.float32)
    half = NB // 2
    for y in range(384):
        dist = 255 - y
        if dist < 0:
            t[NB, y] = 1.0
            continue
        b = dist
        if dist >= half:
            b = min(half + int(math.log(dist / half) / math.log(MAXD / half) * (NB - half)), NB - 1)
        t[b, y] += 1.0
        t[NB - 1, y] -= 1.0
    return t


def layer(nc, A, out):
    f32, f32r = mybir.dt.float32, mybir.dt.float32r
    ALU, ACT, AX = mybir.AluOpType, mybir.ActivationFunctionType, mybir.AxisListType

    scr_u = nc.dram_tensor("scr_u", (DS, L, NC), f32).ap()
    scr_y = nc.dram_tensor("scr_y", (NQ, 128, QG, NC), f32).ap()
    scr_b = nc.dram_tensor("scr_b", (128 * H * 384,), f32).ap()

    ctx = ExitStack()
    with ctx:
        def sb(name, shape, dt=f32):
            return ctx.enter_context(nc.sbuf_tensor(name, shape, dt))

        def sem(name):
            return ctx.enter_context(nc.semaphore(name))

        wring = sb("wring", [128, 4, 2, 1024], f32r)
        xs = sb("xs", [128, 2, KD, T], f32r)
        bs = sb("bs", [128, 2, 2048], f32r)
        raw = sb("raw", [128, 2, 2048])
        ident = sb("ident", [128, 128])
        ones = sb("ones", [128, 1])
        lsrow = sb("lsrow", [GP, 2])
        relb = sb("relb", [NB + 1, H])
        gcol = sb("gcol", [128, NG])
        ccol = sb("ccol", [128, 4, 2 * FT])
        lam = sb("lam", [128, 3 * GP + KD])
        sp = sb("sp", [128, 24, GP])
        pw = sb("pw", [128, 2, GP, L + 1])
        st = sb("st", [128, 160])
        nmx = sb("nmx", [128, 48])
        lsum = sb("lsum", [128, 48])
        rl = sb("rl", [128, 16])
        F = sb("F", [128, 4096 + 12416 + 2048 + 2048 + 2048 + 4096])

        def region(at, *dims):
            n = int(np.prod(dims))
            v = F[:, at:at + n]
            if len(dims) == 1:
                return v
            names = "abcd"[:len(dims)]
            return v.rearrange(f"p ({' '.join(names)}) -> p {' '.join(names)}",
                               **{k: d for k, d in zip(names, dims)})

        ph = region(0, 2, GP, NC)
        w1 = region(2048, 2, 2, 512)
        bias = region(0, H, 512)
        R0 = 4096
        ca = region(R0, 2, 2, QP * (L + 1) * CG)
        w1p = region(R0 + 2304, 2, 512)
        kt = region(R0 + 3328, QG, 128)
        toep = region(R0 + 4352, QG, 128)
        ub = region(R0 + 5376, G, NC)
        craw = region(R0 + 5376, 2, 4, 128)
        zb = region(R0 + 7424, 2, QP, NC)
        dtmp = region(R0 + 7936, 4, QP, NC)
        ptmp = region(R0 + 8960, 2, 576)
        yb = region(R0 + 10112, 512)
        bmat = region(R0 + 10112, 2, GP, CG)
        yst = region(R0 + 10624, 512)
        cmat = region(R0 + 11136, 3, GP, CG)
        bb = region(R0 + 11904, 2, GP, CG)
        pbuf = region(R0, 2, 512)
        ptb = region(R0 + 1024, 2, 512)
        sg = region(R0, 4, 512)
        yrow = region(R0 + 2048, TT, 512)
        mkrow = region(R0 + 4096, MT, 512)
        kxT = region(R0 + 5120, XH, M)
        xv = region(R0 + 6144, MT, 512)
        hres = region(R0 + 7808, TT, D)
        hff = region(0, FT, T)
        R1 = R0 + 12416
        uT = region(R1, NQ, T)
        grow = region(R1, 128)[0:NG]
        nrow = region(R1 + 768, 128)[0:KD]
        crow = region(R1 + 128, 2, 128)[0:88]
        prow = region(R1 + 384, 3, 128)[0:GP]
        qk = region(R1 + 2048, TT, 512)
        vrow = region(R1 + 4096, TT, 512)
        mrow = region(R1 + 4096, 2048)
        R2 = R1 + 6144
        qT = region(R2, 4, T)
        kT = region(R2 + 2048, 4, T)
        xr = region(R2, TT, D)
        cv = region(R2, 4, T)
        memr = mrow.rearrange("p (t d) -> p t d", t=MT)

        pb = [ctx.enter_context(nc.psum_tensor(f"pb{i}", [128, 512], f32)) for i in range(8)]

        raw_in = [sem("raw_in0"), sem("raw_in1")]
        hi_done, lo_done = sem("hi_done"), sem("lo_done")
        unit_used = sem("unit_used")
        bank_full = [sem(f"bank_full{i}") for i in range(8)]
        bank_free = [sem(f"bank_free{i}") for i in range(8)]
        x_in = [sem(f"x_in{t}") for t in range(TT)]
        mem_in, par_in, gain_in = sem("mem_in"), sem("par_in"), sem("gain_in")
        conv_in, c_in, b_in, relb_in = sem("conv_in"), sem("c_in"), sem("b_in"), sem("relb_in")
        h_in, bias_in = sem("h_in"), sem("bias_in")
        scr_out = sem("scr_out")
        su_out = sem("su_out")
        sy_out = [sem(f"sy_out{q}") for q in range(NQ)]
        u_in = sem("u_in")
        y_in = [sem(f"y_in{q}") for q in range(NQ)]
        t_in = [sem(f"t_in{q}") for q in range(NQ)]
        out_done = sem("out_done")
        ident_ok, zero_ok, ones_ok = sem("ident_ok"), sem("zero_ok"), sem("ones_ok")
        dve_step, act_step, pool_step = sem("dve_step"), sem("act_step"), sem("pool_step")
        step_row, lam_ok = sem("step_row"), sem("lam_ok")
        sq_done = sem("sq_done")
        ms_ready, rs_ready = sem("ms_ready"), sem("rs_ready")
        xn_ready = sem("xn_ready")
        act_hi = sem("act_hi")
        act_lo = sem("act_lo")
        stp_ready, sa_ready, mag_ready = sem("stp_ready"), sem("sa_ready"), sem("mag_ready")
        ang_ready, sin_ready, par_ready = sem("ang_ready"), sem("sin_ready"), sem("par_ready")
        cols_ready, relbv_ready, cmat_ready = sem("cols_ready"), sem("relbv_ready"), sem("cmat_ready")
        ph_ready, w1p_ready, ca_ready = sem("ph_ready"), sem("w1p_ready"), sem("ca_ready")
        w1_ready, kt_ready = sem("w1_ready"), sem("kt_ready")
        uT_ready, z_ready, yb_ready, zz_ready = sem("uT_ready"), sem("z_ready"), sem("yb_ready"), sem("zz_ready")
        row_ready = sem("row_ready")
        qkT_ready = sem("qkT_ready")
        far_zero = sem("far_zero")
        logit_ready, prob_ready, pt_ready, pv_done = (sem("logit_ready"), sem("prob_ready"),
                                                      sem("pt_ready"), sem("pv_done"))
        yrow_ready = sem("yrow_ready")
        gelu_ready, sig_ready, y2_ready, y3_ready = (sem("gelu_ready"), sem("sig_ready"),
                                                     sem("y2_ready"), sem("y3_ready"))
        ysq_ready = sem("ysq_ready")
        h1_ready = sem("h1_ready")
        conv_ready, gate_ready, val_ready = sem("conv_ready"), sem("gate_ready"), sem("val_ready")
        taps_ready, hff_ready = sem("taps_ready"), sem("hff_ready")
        res_ready = sem("res_ready")

        uses, fills = {}, [0] * 8

        def use(bank, name):
            uses[name] = (bank, fills[bank])
            fills[bank] += 1

        def plan():
            use(4, "lam"); use(5, "par"); use(6, "cr"); use(7, "cm"); use(6, "relb")
            for d in range(KD):
                use(4 + d % 4, f"x{d}")
            for m in range(4):
                use(m, f"u{m}")
            for i in range(4):
                use(4 + i, f"m{i}")

            def sa(q):
                use(4, f"w1r{q}"); use(5, f"w1i{q}"); use(6, f"ka{q}"); use(7, f"kb{q}")

            def sbq(q):
                use(4, f"vr{q}"); use(5, f"vi{q}")
            for p in "qkv":
                for t in range(TT):
                    use(t, f"{p}{t}")
            sa(0); sbq(0); sa(1); use(6, "ye0"); use(7, "yo0"); sbq(1)
            for t in range(TT):
                use(4 + t, f"qt{t}")
            sa(2); use(6, "ye1"); use(7, "yo1"); sbq(2); sa(3); use(6, "ye2"); use(7, "yo2"); sbq(3)
            for t in range(TT):
                use(4 + t, f"kt{t}")
            use(6, "ye3"); use(7, "yo3")
            for s in range(32):
                use(4 + s % 2, f"sc{s}"); use(6, f"pt{s}")
            for t in range(TT):
                use(7, f"pv{t}")
            use(0, "mk0"); use(1, "mk1"); use(2, "mv0"); use(3, "mv1")
            use(4, "kx0"); use(5, "kx1")
            for c in range(4):
                use([6, 7, 4, 5][c], f"ya{c}")
            for m in range(4):
                use(m, f"z{m}")
            use(4, "ss"); use(5, "bc")
            for half in range(2):
                for t in range(TT):
                    use(t, f"o{half}{t}")
            for d in range(KD):
                use(4 + d % 4, f"x2{d}")
            for t in range(TT):
                use(t, f"qx{t}")
            for t in range(TT):
                use(4 + t, f"qxt{t}")
            for s in range(16):
                use(4 + s % 2, f"xs{s}"); use(6, f"xp{s}")
            for t in range(TT):
                use(7, f"xpv{t}")
            for c in range(4):
                use(4 + c, f"xo{c}")
            for half in range(2):
                for t in range(TT):
                    use(t, f"w{half}{t}")
            for d in range(KD):
                use(4 + d % 4, f"x3{d}")
            for j in range(2 * FT):
                use(j % 4, f"f{j}")
            for b in range(8):
                use(b, f"d{b}")
        plan()

        DONE = {m: f"u{m}" for m in range(4)}
        DONE.update({U_Q + 3: "q3", U_K + 3: "k3", U_V + 3: "v3", U_MK + 3: "mk1", U_MV + 3: "mv1",
                     U_GLU: "z1", U_GLU + 1: "z3", U_OUT + 3: "o03", U_OUT + 7: "o13",
                     U_XQ + 3: "qx3", U_XO + 1: "w03", U_XO + 3: "w13"})
        DONE.update({U_UP + j: f"f{j}" for j in range(2 * FT)})

        def wait_unit(eng, u):
            if u in DONE:
                bank, n = uses[DONE[u]]
                eng.wait_ge(bank_full[bank], n + 1)
            else:
                eng.wait_ge(unit_used, sum(v not in DONE for v in range(u + 1)))

        def fill(pe, name):
            bank, n = uses[name]
            if n > 0:
                pe.wait_ge(bank_free[bank], n)
            return pb[bank]

        def filled(ins, name):
            ins.then_inc(bank_full[uses[name][0]], 1)

        def read(eng, name):
            bank, n = uses[name]
            eng.wait_ge(bank_full[bank], n + 1)
            return pb[bank]

        def drained(ins, name):
            ins.then_inc(bank_free[uses[name][0]], 1)

        def after_drain(eng, name):
            bank, n = uses[name]
            eng.wait_ge(bank_free[bank], n + 1)

        def wait_values(eng, s, heads, bank, before):
            if s % heads == heads - 1:
                read(eng, f"{bank}{s // heads}")
            else:
                eng.wait_ge(pv_done, before + s + 1 - s // heads)

        def pt_evac(eng, copy, s):
            if s >= 2:
                wait_values(eng, s - 2, H, "pv", 0)
            n = (s // H + 1) * 128
            drained(copy(ptb[:, s % 2, 0:n], read(eng, f"pt{s}")[:, 0:n]), f"pt{s}")

        def xp_evac(eng, copy, s):
            if s >= 2:
                wait_values(eng, s - 2, XH, "xpv", TT * (H - 1))
            drained(copy(ptb[:, s % 2, 0:M], read(eng, f"xp{s}")[:, 0:M]), f"xp{s}")

        def to_tokens(a):
            return a.rearrange("p (k i) -> p i k", i=L)

        w_in = A["w_in"][0].rearrange("(k p) n -> p k n", p=128)
        w_kv = A["x_wkv"][0].rearrange("(k p) n -> p k n", p=128)
        w_glu = A["ssm_w_glu"][0].rearrange("(k p) n -> p k n", p=128)
        w_out = A["w_out"][0].rearrange("(k p) n -> p k n", p=128)
        w_xq = A["x_wq"][0].rearrange("(k p) n -> p k n", p=128)
        w_xo = A["x_wo"][0].rearrange("(k p) n -> p k n", p=128)
        w_up = A["ffn_w_up"][0].rearrange("(k p) n -> p k n", p=128)
        w_dn = A["ffn_w_down"][0].rearrange("(k p) n -> p k n", p=128)

        def chunk_src(c):
            u = 2 * c
            if u < U_Q:
                return w_in[:, :, 256 * c:256 * c + 256]
            if u < U_MK:
                p, j = (u - U_Q) // 4, (u - U_Q) // 2 % 2
                return w_in[:, 4 * j:4 * j + 4, DS * (p + 1):DS * (p + 2)]
            if u < U_GLU:
                p, j = (u - U_MK) // 4, (u - U_MK) // 2 % 2
                return w_kv[:, 4 * j:4 * j + 4, 512 * p:512 * p + 512]
            if u < U_OUT:
                return w_glu
            if u < U_XQ:
                p, j = (u - U_OUT) // 4, (u - U_OUT) // 2 % 2
                return w_out[:, 4 * j:4 * j + 4, 512 * p:512 * p + 512]
            if u < U_XO:
                j = (u - U_XQ) // 2
                return w_xq[:, 4 * j:4 * j + 4, :]
            if u < U_UP:
                p = (u - U_XO) // 2
                return w_xo[:, :, 512 * p:512 * p + 512]
            if u < U_DOWN:
                i, p = (u - U_UP) // 4, (u - U_UP) // 2 % 2
                return w_up[:, :, DF * p + 256 * i:DF * p + 256 * i + 256]
            j = (u - U_DOWN)
            return w_dn[:, j:j + 2, :]

        def unit_dims(u):
            if u < U_Q or U_UP <= u < U_DOWN:
                return 8, 128
            if U_GLU <= u < U_OUT:
                return 4, 256
            if u >= U_DOWN:
                return 1, 1024
            return 2, 512

        def raw_unit(u):
            r = raw[:, u // 2 % 2, :]
            a, b = unit_dims(u)
            if b in (128, 256):
                v = r.rearrange("p (k n) -> p k n", k=a)
                return v[:, :, (u % 2) * b:(u % 2) * b + b]
            return r[:, (u % 2) * 1024:(u % 2) * 1024 + 1024].rearrange("p (k n) -> p k n", k=a)

        def w_unit(u, part):
            a, b = unit_dims(u)
            return wring[:, u % 4, part, :].rearrange("p (k n) -> p k n", k=a)

        def load_chunk(eng, c):
            if c >= 2:
                eng.wait_ge(hi_done, 2 * (c - 1))
                eng.wait_ge(lo_done, 2 * (c - 1))
            src = chunk_src(c)
            eng.dma_start(raw[:, c % 2, :].rearrange("p (k n) -> p k n", k=src.shape[1]), src)\
               .then_inc(raw_in[c % 2], 16)

        def split_hi(act, u):
            act.wait_ge(raw_in[u // 2 % 2], 16 * (u // 4 + 1))
            if u >= 4:
                wait_unit(act, u - 4)
            nc.scalar.activation(w_unit(u, 0), raw_unit(u), ACT.Copy).then_inc(hi_done, 1)

        def split_lo(dve, u):
            dve.wait_ge(hi_done, u + 1)
            nc.vector.tensor_tensor(w_unit(u, 1), raw_unit(u), w_unit(u, 0).bitcast(f32),
                                    ALU.subtract).then_inc(lo_done, 1)

        def mm3(ps, lh, ll, rh, rl_, first, last):
            nc.tensor.matmul(ps, lh, rh, start=first, stop=False)
            nc.tensor.matmul(ps, lh, rl_, start=False, stop=False)
            return nc.tensor.matmul(ps, ll, rh, start=False, stop=last)

        EV = [("x", TT, D), ("mem", MT, D), ("q", TT * H, HD), ("k", TT * H, HD), ("mk", MT * XH, XD),
              ("ya", TT, DS), ("ss", TT, DS), ("x2", TT, D), ("qx", TT * XH, XD), ("x3", TT, D)]
        EVN = {n: i for i, (n, _, _) in enumerate(EV)}
        EVC, at = {}, 0
        for n, k, _ in EV:
            EVC[n] = at
            at += k
        sq = sb("sq", [128, at])
        ms = sb("ms", [128, at])
        rs = sb("rs", [128, at])
        rt = sb("rt", [128, 2, 32])

        def ev(t, name):
            return t[:, EVC[name]:EVC[name] + EV[EVN[name]][1]]

        junk = qk[:, 0:2, :].rearrange("p a b -> p (a b)")
        sqr_s5, sqr_late = region(R0 + 7936, 512), region(R0 + 7168, 512)
        ssr_ready, relb_ok = sem("ssr_ready"), sem("relb_ok")

        n_sq = [0]

        def row_square(act, event, t, row):
            if n_sq[0] > 0:
                act.wait_ge(sq_done, n_sq[0])
            n_sq[0] += 1
            c = EVC[event] + t
            nc.scalar.activation(junk[:, 0:row.shape[1]], row, ACT.Square, accum_out=sq[:, c:c + 1])\
                .then_inc(sq_done, 1)

        block = ctx.enter_context(nc.Block())

        @block.sync
        def _(sync):
            for t in range(TT):
                sync.dma_start(xr[:, t, :], A["x"][0, t * 128:(t + 1) * 128, :]).then_inc(x_in[t], 16)
            lam_rows = [A[n][0].rearrange("(a b) n -> a (b n)", b=2) for n in ("ssm_lam_re", "ssm_lam_im")]
            sync.dma_start(prow[:, 0, :], lam_rows[0]).then_inc(par_in, 16)
            sync.dma_start(prow[:, 1, :], lam_rows[1]).then_inc(par_in, 16)
            sync.dma_start(lsrow[:, :], A["ssm_log_step"][0].rearrange("(a b) -> a b", b=2)).then_inc(par_in, 16)
            sync.dma_start(nrow[:, :], A["norm_mix"][0].rearrange("(a n) -> a n", n=128)).then_inc(par_in, 16)
            load_chunk(sync, 0)
            load_chunk(sync, 1)
            n_gain = 0
            for name, k in GAINS:
                r = COL[name]
                src = A[name][0]
                if name in ("attn_qn", "attn_kn"):
                    for i in range(2):
                        sync.dma_start(grow[r:r + 1, i * HD:(i + 1) * HD], src.rearrange("(a n) -> a n", a=1))\
                            .then_inc(gain_in, 16)
                        n_gain += 1
                else:
                    sync.dma_start(grow[r:r + k, :], src.rearrange("(a n) -> a n", n=128)).then_inc(gain_in, 16)
                    n_gain += 1
            assert n_gain == N_GAIN
            for t in range(MT):
                sync.dma_start(memr[:, t, :], A["mem"][0, t * 128:(t + 1) * 128, :]).then_inc(mem_in, 16)
            cw = A["ffn_conv_w"][0].rearrange("w o (a n) -> w (o a) n", n=128)
            sync.dma_start(crow[0:44, 0, :], cw[0]).then_inc(conv_in, 16)
            sync.dma_start(crow[44:88, 0, :], cw[1]).then_inc(conv_in, 16)
            sync.dma_start(crow[0:44, 1, :], cw[2]).then_inc(conv_in, 16)
            sync.dma_start(crow[44:88, 1, :], A["ffn_conv_b"][0].rearrange("(a n) -> a n", n=128)).then_inc(conv_in, 16)
            load_chunk(sync, 2)
            load_chunk(sync, 3)

            def u_write(q):
                after_drain(sync, f"u{q}")
                sync.dma_start(scr_u[q * 128:(q + 1) * 128].rearrange("p i k -> p (i k)"), uT[:, q, :]).then_inc(su_out, 16)

            def u_read():
                sync.wait_ge(su_out, 16 * NQ)
                after_drain(sync, "cm")
                v = scr_u.rearrange("(g c) i k -> i c g k", c=CG)
                for d in range(L):
                    sync.dma_start(ub[d * CG:(d + 1) * CG, :, :], v[L - 1 - d]).then_inc(u_in, 16)

            def t_load(q):
                after_drain(sync, f"ka{q}")
                after_drain(sync, f"kb{q}")
                if q == 0:
                    sync.wait_ge(zero_ok, 1)
                else:
                    after_drain(sync, f"yo{q - 1}")
                for d in range(L):
                    sync.dma_start(toep[d * CG:(d + 1) * CG, :, (L - 1 - d) * CG:],
                                   kt[0:CG, :, 0:(d + 1) * CG]).then_inc(t_in[q], 16)

            def y_back(q):
                after_drain(sync, f"yo{q}")
                sync.dma_start(scr_y[q].rearrange("p g k -> p (g k)"), yb).then_inc(sy_out[q], 16)
                sync.wait_ge(sy_out[q], 16)
                if q >= 1:
                    sync.wait_ge(zz_ready, q)
                v = scr_y[q].rearrange("(j c) g k -> g c j k", c=CG)
                for g in range(QG):
                    sync.dma_start(yst[g * CG:(g + 1) * CG, :].rearrange("p (j k) -> p j k", j=L), v[g])\
                        .then_inc(y_in[q], 16)

            for q in range(NQ):
                u_write(q)
            u_read()
            load_chunk(sync, 4)
            load_chunk(sync, 5)
            after_drain(sync, "relb")
            sync.dma_start(scr_b.rearrange("(p h y) -> h p y", p=128, h=H),
                           yst[0:H, 0:384].unsqueeze(1).to_broadcast([H, 128, 384])).then_inc(scr_out, 16)
            t_load(0)
            load_chunk(sync, 6)
            sync.wait_ge(scr_out, 16)
            y_back(0)
            t_load(1)
            load_chunk(sync, 7)
            load_chunk(sync, 8)
            y_back(1)
            t_load(2)
            load_chunk(sync, 9)
            y_back(2)
            t_load(3)
            load_chunk(sync, 10)
            y_back(3)
            load_chunk(sync, 11)
            sync.wait_ge(z_ready, NQ)
            skew = bass.AP(tensor=scr_b.tensor, offset=127,
                           ap=[[H * 384 - 1, 128], [384, H], [1, 256]])
            sync.dma_start(bias[:, :, 256:512], skew).then_inc(bias_in, 16)
            sync.wait_ge(zz_ready, NQ)
            for t in range(TT):
                sync.dma_start(hres[:, t, :], A["x"][0, t * 128:(t + 1) * 128, :]).then_inc(h_in, 16)
            for c in range(12, U_END // 2):
                load_chunk(sync, c)
            for t in range(TT):
                for half in range(2):
                    sync.wait_ge(res_ready, 2 * t + half + 1)
                    sync.dma_start(out[0, t * 128:(t + 1) * 128, half * 512:half * 512 + 512],
                                   hres[:, t, half * 512:half * 512 + 512]).then_inc(out_done, 16)
            sync.wait_ge(out_done, 16 * 2 * TT)

        @block.gpsimd
        def _(pool):
            n_step = [0]

            def link(ins):
                n_step[0] += 1
                ins.then_inc(pool_step, 1)
                pool.wait_ge(pool_step, n_step[0])

            def mul(o, a, b):
                return nc.gpsimd.tensor_tensor(o, a, b, ALU.mult)

            def cmul(o_re, o_im, a_re, a_im, b_re, b_im, t1, t2, sign=ALU.add):
                mul(t1, a_re, b_re)
                link(mul(t2, a_im, b_im))
                link(nc.gpsimd.tensor_tensor(o_re, t1, t2, ALU.subtract))
                mul(t1, a_re, b_im)
                link(mul(t2, a_im, b_re))
                return nc.gpsimd.tensor_tensor(o_im, t1, t2, sign)

            for i, part in enumerate(("ssm_b_re", "ssm_b_im")):
                pool.dma_start(bmat[:, i], A[part][0].rearrange("(a b) n c -> (b n) a c", b=2)).then_inc(b_in, 16)
            for i, part in enumerate(("ssm_c_re", "ssm_c_im")):
                for half in range(2):
                    pool.dma_start(craw[:, i, :, half * NS:(half + 1) * NS],
                                   A[part][0].rearrange("(a g) c n -> (g c) a n", a=4)).then_inc(c_in, 16)
            pool.dma_start(relb[0:NB, :], A["rel_bias"]).then_inc(relb_in, 16)
            pool.dma_start(qk[0:NB + 1, 3, 0:384], A["buckets"]).then_inc(relb_in, 16)
            link(nc.gpsimd.memset(ident[:, :], 0.0))
            nc.gpsimd.affine_select(out=ident[:, :], in_=ident[:, :], compare_op=ALU.not_equal,
                                    fill=1.0, base=0, pattern=[[-1, 128]], channel_multiplier=1)\
                .then_inc(ident_ok, 1)
            nc.gpsimd.memset(toep[:, :, :], 0.0).then_inc(zero_ok, 1)
            nc.gpsimd.memset(pw[:, 0, :, 0:1], 1.0)
            nc.gpsimd.memset(pw[:, 1, :, 0:1], 0.0)
            nc.gpsimd.memset(ph[:, 0, :, 0:1], 1.0)
            link(nc.gpsimd.memset(ph[:, 1, :, 0:1], 0.0))

            def view(t, *dims):
                n = int(np.prod(dims))
                names = "abcd"[:len(dims)]
                return t[:, 0:n].rearrange(f"p ({' '.join(names)}) -> p {' '.join(names)}",
                                           **{k: d for k, d in zip(names, dims)})

            def powers(tab, top):
                m = 1
                while m < top:
                    k = min(m, top - m)
                    t1, t2 = view(ptmp[:, 0, :], GP, k), view(ptmp[:, 1, :], GP, k)
                    b = [tab[:, i, :, m:m + 1].to_broadcast([128, GP, k]) for i in range(2)]
                    link(cmul(tab[:, 0, :, m + 1:m + 1 + k], tab[:, 1, :, m + 1:m + 1 + k],
                              tab[:, 0, :, 1:1 + k], tab[:, 1, :, 1:1 + k], b[0], b[1], t1, t2))
                    m *= 2

            pool.wait_ge(par_ready, 1)
            pool.wait_ge(b_in, 32)
            t1, t2 = view(ptmp[:, 0, :], GP, CG), view(ptmp[:, 1, :], GP, CG)
            fb = [sp[:, i, :].unsqueeze(2).to_broadcast([128, GP, CG]) for i in (0, 1)]
            link(cmul(bb[:, 0], bb[:, 1], fb[0], fb[1], bmat[:, 0], bmat[:, 1], t1, t2))
            powers(pw, L)

            def quarter(q):
                g0 = q * QP
                if q >= 1:
                    bank, n = uses[f"w1i{q - 1}"]
                    pool.wait_ge(bank_full[bank], n + 1)
                shape = [128, QP, L, CG]
                t1, t2 = view(ptmp[:, 0, :], QP, L, CG), view(ptmp[:, 1, :], QP, L, CG)
                p = [pw[:, i, g0:g0 + QP, 0:L].unsqueeze(3).to_broadcast(shape) for i in range(2)]
                b = [bb[:, i, g0:g0 + QP, :].unsqueeze(2).to_broadcast(shape) for i in range(2)]
                o = [view(w1p[:, i, :], QP, L, CG) for i in range(2)]
                cmul(o[0], o[1], p[0], p[1], b[0], b[1], t1, t2).then_inc(w1p_ready, 1)
                pool.wait_ge(w1p_ready, q + 1)
                if q == 0:
                    after_drain(pool, "cr")
                    after_drain(pool, "cm")
                if q >= 2:
                    after_drain(pool, f"yo{q - 2}")
                shape = [128, QP, L + 1, CG]
                t1, t2 = view(ptmp[:, 0, :], QP, L + 1, CG), view(ptmp[:, 1, :], QP, L + 1, CG)
                p = [pw[:, i, g0:g0 + QP, :].unsqueeze(3).to_broadcast(shape) for i in range(2)]
                c_re, c_im, nc_re = [cmat[:, i, g0:g0 + QP, :].unsqueeze(2).to_broadcast(shape)
                                     for i in range(3)]
                o = [view(ca[:, q % 2, i, :], QP, L + 1, CG) for i in range(2)]
                mul(t1, c_re, p[0])
                link(mul(t2, c_im, p[1]))
                link(nc.gpsimd.tensor_tensor(o[0], t1, t2, ALU.subtract))
                mul(t1, nc_re, p[1])
                link(mul(t2, c_im, p[0]))
                nc.gpsimd.tensor_tensor(o[1], t1, t2, ALU.subtract).then_inc(ca_ready, 1)
                pool.wait_ge(ca_ready, q + 1)

            quarter(0)
            powers(ph, NC - 1)
            nc.gpsimd.memset(rt[:, 1, 31:32], 0.0).then_inc(ph_ready, 1)
            for q in range(1, NQ):
                quarter(q)

        @block.scalar
        def _(act):
            n_step = [0]

            def link(ins):
                n_step[0] += 1
                ins.then_inc(act_step, 1)
                act.wait_ge(act_step, n_step[0])

            def A_(o, i, f, **k):
                return nc.scalar.activation(o, i, f, **k)

            def inv_root(name):
                act.wait_ge(ms_ready, EVN[name] + 1)
                if EVN[name] > 0:
                    act.wait_ge(rs_ready, EVN[name])
                w = EV[EVN[name]][1]
                link(A_(rt[:, 0, 0:w], ev(ms, name), ACT.Ln))
                A_(ev(rs, name), rt[:, 0, 0:w], ACT.Exp, scale=-0.5).then_inc(rs_ready, 1)

            def act_split(name, dst, gain=1.0):
                A_(dst, read(act, name)[:, :], ACT.Copy, scale=gain).then_inc(act_hi, 1)

            def col(name, i=0):
                return gcol[:, COL[name] + i:COL[name] + i + 1]

            for t in range(TT):
                act.wait_ge(x_in[t], 16)
                row_square(act, "x", t, xr[:, t, :])
            after_drain(act, "lam")
            A_(sp[:, 2, :], lam[:, 2 * GP:3 * GP], ACT.Exp).then_inc(stp_ready, 1)
            inv_root("x")
            split_hi(act, 0)
            split_hi(act, 1)
            act.wait_ge(sa_ready, 1)
            A_(sp[:, 5, :], sp[:, 3, :], ACT.Exp)
            A_(sp[:, 6, :], sp[:, 3, :], ACT.Exp, scale=float(L)).then_inc(mag_ready, 1)
            act.wait_ge(ang_ready, 1)
            A_(sp[:, 8, :], sp[:, 7, :], ACT.Sin)
            A_(sp[:, 10, :], sp[:, 9, :], ACT.Sin).then_inc(sin_ready, 1)
            p = read(act, "par")
            A_(gcol[:, :], p[:, 0:NG], ACT.Copy)
            drained(A_(ccol[:, :, :], p[:, 64:64 + 176].rearrange("p (a b) -> p a b", a=4), ACT.Copy), "par")
            for i, name in enumerate(("cr", "cm")):
                p = read(act, name)
                for half in range(2):
                    rows = slice(half * NS, (half + 1) * NS)
                    src = p[rows, :].rearrange("p (a b c) -> p a b c", b=2, c=CG)[:, :, half, :]
                    ins = A_(cmat[rows, i], src, ACT.Copy)
                    if i == 0:
                        ins = A_(cmat[rows, 2], src, ACT.Copy, scale=-1.0)
                drained(ins, name)
            p = read(act, "relb")
            drained(A_(yst[0:H, 0:384], p[0:H, 0:384], ACT.Copy), "relb")
            after_drain(act, "par")
            for d in range(KD):
                act_split(f"x{d}", xs[:, 0, d, :], lam[:, 3 * GP + d:3 * GP + d + 1])
                if d == 3:
                    split_hi(act, 2)
                    split_hi(act, 3)
            act.wait_ge(mem_in, 16 * MT)
            for t in range(MT):
                row_square(act, "mem", t, memr[:, t, :])
            inv_root("mem")
            for m in range(4):
                p = read(act, f"u{m}")
                drained(A_(uT[:, m, :].rearrange("p (i k) -> p i k", i=L),
                           p[:, :].rearrange("p (k i) -> p i k", i=L), ACT.Copy), f"u{m}")
                split_hi(act, U_Q + m)
            for i in range(4):
                p = read(act, f"m{i}")
                for j in range(2):
                    c = COL["norm_mem"] + 2 * i + j
                    A_(bs[:, 0, i * 512 + j * M:i * 512 + (j + 1) * M], p[:, j * M:(j + 1) * M], ACT.Copy,
                       scale=gcol[:, c:c + 1]).then_inc(act_hi, 1)

            def evac(name, dst, src=lambda p: p[:, :]):
                drained(A_(dst, src(read(act, name)), ACT.Copy), name)

            def weights_in(q):
                if q >= 2:
                    read(act, f"vi{q - 2}")
                evac(f"w1i{q}", w1[:, q % 2, 1, :])
                if q >= 1:
                    act.wait_ge(t_in[q - 1], 16 * L)
                for b, n in enumerate("ab"):
                    evac(f"k{n}{q}", kt[0:CG].rearrange("p (a b) n -> p a b n", b=2)[:, :, b, :],
                         lambda p: p[0:CG, :].rearrange("p (a n) -> p a n", a=QP))

            def y_out(q):
                if q >= 1:
                    act.wait_ge(sy_out[q - 1], 16)
                for b, n in enumerate("eo"):
                    drained(A_(yb.rearrange("p (a b k) -> p a b k", b=2, k=NC)[:, :, b, :],
                               read(act, f"y{n}{q}")[:, 0:QP * NC].rearrange("p (a k) -> p a k", a=QP), ACT.Copy),
                            f"y{n}{q}")

            def rows(p, dst):
                for t in range(TT):
                    evac(f"{p}{t}", dst[:, t, :])

            split_hi(act, 8)
            split_hi(act, 9)
            weights_in(0)
            split_hi(act, 10)
            rows("q", qk)
            split_hi(act, 11)
            weights_in(1)
            inv_root("q")
            split_hi(act, 12)
            y_out(0)
            split_hi(act, 13)
            weights_in(2)
            split_hi(act, 14)
            y_out(1)
            for t in range(TT):
                read(act, f"qt{t}")
            rows("k", qk)
            split_hi(act, 15)
            weights_in(3)
            inv_root("k")
            split_hi(act, 16)
            y_out(2)
            split_hi(act, 17)
            split_hi(act, 18)
            y_out(3)
            rows("v", vrow)
            split_hi(act, 19)

            for s in range(TT * H):
                n = (s // H + 1) * 128
                if s >= 2:
                    read(act, f"pt{s - 2}")
                p = read(act, f"sc{s}")
                act.wait_ge(logit_ready, s + 1)
                drained(A_(pbuf[:, s % 2, 0:n], p[:, 0:n], ACT.Exp, scale=-1.0, bias=nmx[:, s:s + 1],
                           accum_out=lsum[:, s:s + 1]), f"sc{s}")
                if s % 2 == 1:
                    pt_evac(act, lambda o, i: A_(o, i, ACT.Copy), s - 1)
                if s >= 4 and (s - 4) % 3 == 0 and (s - 4) // 3 < 8:
                    split_hi(act, 20 + (s - 4) // 3)
                if s == 2:
                    for q in range(NQ):
                        act.wait_ge(zz_ready, q + 1)
                        A_(uT[:, q, :], uT[:, q, :], ACT.Gelu_apprx_tanh).then_inc(gelu_ready, 1)
                if s == 14:
                    evac("mk0", mkrow[:, 0, :])
                    evac("mk1", mkrow[:, 1, :])
                if s == 18:
                    inv_root("mk")
                if s == 26:
                    evac("mv0", xv[:, 0, :])
                    evac("mv1", xv[:, 1, :])
                if s == 28:
                    wait_unit(act, U_MV + 3)
                    act.wait_ge(gelu_ready, NQ)
                    for q in range(NQ):
                        A_(bs[:, 0, q * 512:(q + 1) * 512], uT[:, q, :], ACT.Copy).then_inc(act_hi, 1)
                if s in (12, 20, 28):
                    t = (s - 12) // 8
                    after_drain(act, f"pv{t}")
                    row_square(act, "ya", t, yrow[:, t, :])
            after_drain(act, f"pv{TT - 1}")
            row_square(act, "ya", TT - 1, yrow[:, TT - 1, :])
            inv_root("ya")
            for i in range(2):
                drained(A_(kxT[:, 2 * i:2 * i + 2, :].rearrange("p h m -> p (h m)"), read(act, f"kx{i}")[:, :],
                           ACT.Copy, scale=gcol[:, COL["x_kn"]:COL["x_kn"] + 1]), f"kx{i}")
            for m in range(4):
                b = COL["ssm_b_glu"] + m
                drained(A_(sg[:, m, :], read(act, f"z{m}")[:, :], ACT.Sigmoid, bias=gcol[:, b:b + 1]), f"z{m}")
                if m % 2 == 1:
                    split_hi(act, 28 + m // 2)
            for c in range(4):
                act.wait_ge(y2_ready, c + 1)
                A_(sg[:, c, :], uT[:, c, :], ACT.Square).then_inc(ysq_ready, 1)
            for c in range(4):
                act_split(f"ya{c}", xs[:, 0, 4 + c, :], col("gnorm_attn", c))
            inv_root("ss")
            for c in range(4):
                act.wait_ge(y3_ready, c + 1)
                g = COL["gnorm_ssm"] + c
                A_(to_tokens(xs[:, 0, c, :]), uT[:, c, :].rearrange("p (i k) -> p i k", i=L),
                   ACT.Copy, scale=gcol[:, g:g + 1]).then_inc(act_hi, 1)
            for u in range(U_OUT, U_OUT + 8):
                split_hi(act, u + 4)

            def norm_rows(name, last_add, gain):
                for t in range(TT):
                    after_drain(act, f"{last_add}{t}")
                    row_square(act, name, t, hres[:, t, :])
                inv_root(name)
                for d in range(KD):
                    act_split(f"{name}{d}", xs[:, 0, d, :], col(gain, d))

            norm_rows("x2", "o1", "norm_xattn")
            for u in range(U_XQ, U_XQ + 4):
                split_hi(act, u + 4)
            rows("qx", qk)
            inv_root("qx")
            for s in range(TT * XH):
                if s >= 2:
                    read(act, f"xp{s - 2}")
                p = read(act, f"xs{s}")
                act.wait_ge(logit_ready, TT * H + s + 1)
                drained(A_(pbuf[:, s % 2, 0:M], p[:, 0:M], ACT.Exp, bias=nmx[:, 32 + s:33 + s],
                           accum_out=lsum[:, 32 + s:33 + s]), f"xs{s}")
                if s % 2 == 1:
                    xp_evac(act, lambda o, i: A_(o, i, ACT.Copy), s - 1)
            for c in range(4):
                act_split(f"xo{c}", bs[:, 0, c * 512:(c + 1) * 512])
            for u in range(U_XO, U_XO + 4):
                split_hi(act, u + 4)
            norm_rows("x3", "w1", "norm_ffn")
            for i in range(FT // 2):
                for j in range(4):
                    k = 4 * i + j
                    tile = 2 * i + j if j < 2 else FT + 2 * i + j - 2
                    p = read(act, f"f{k}")
                    if i >= 1:
                        act.wait_ge(hff_ready, 2 * i - 1 + j % 2)
                    A_(cv[:, j, :], p[:, :], ACT.Identity, scale=ccol[:, 2, tile:tile + 1],
                       bias=ccol[:, 3, tile:tile + 1]).then_inc(conv_ready, 1)
                    split_hi(act, U_UP + k + 4)
                    if j < 2:
                        after_drain(act, f"f{k}")
                        A_(cv[:, j, :], cv[:, j, :], ACT.Silu).then_inc(gate_ready, 1)
            for n in range(FT):
                act.wait_ge(hff_ready, n + 1)
                if n >= 4:
                    wait_unit(act, U_DOWN + n - 4)
                A_(bs[:, 0, n % 4 * 512:n % 4 * 512 + 512], hff[:, n, :], ACT.Copy).then_inc(act_hi, 1)
                if n >= 1 and U_DOWN + n + 3 < U_END:
                    split_hi(act, U_DOWN + n + 3)

        @block.vector
        def _(dve):
            n_step, n_hi = [0], [0]

            def link(ins):
                n_step[0] += 1
                ins.then_inc(dve_step, 1)
                dve.wait_ge(dve_step, n_step[0])

            V = nc.vector

            def tt(o, a, b, op):
                return V.tensor_tensor(o, a, b, op)

            def ts(o, a, s1, s2, o1, o2):
                return V.tensor_scalar(o, a, s1, s2, o1, o2)

            def stt(o, a, s1, b, o1, o2):
                return V.scalar_tensor_tensor(out=o, in0=a, scalar=s1, in1=b, op0=o1, op1=o2)

            def lo_of(src, hi, lo, g=1.0):
                n_hi[0] += 1
                dve.wait_ge(act_hi, n_hi[0])
                return stt(lo, src, g, hi.bitcast(f32), ALU.mult, ALU.subtract)

            def mean_sq(name):
                n = EV[EVN[name]][2]
                ts(ev(ms, name), ev(sq, name), 1.0 / n, EPS, ALU.mult, ALU.add).then_inc(ms_ready, 1)

            def root(name, ready=None):
                w = EV[EVN[name]][1]
                dve.wait_ge(rs_ready, EVN[name] + 1)
                r, t = ev(rs, name), rt[:, 1, 0:w]
                link(tt(t, r, r, ALU.mult))
                link(tt(t, t, ev(ms, name), ALU.mult))
                link(ts(t, t, -0.5, 1.5, ALU.mult, ALU.add))
                last = tt(r, r, t, ALU.mult)
                if ready is None:
                    link(last)
                else:
                    last.then_inc(ready, 1)

            def scale_rows(name, dst, src, tiles):
                for t in range(tiles):
                    c = EVC[name] + t
                    V.tensor_scalar_mul(dst[:, t, :], src[:, t, :], rs[:, c:c + 1]).then_inc(xn_ready, 1)

            def head_event(name, src, tiles, heads, pre):
                for t in range(tiles):
                    after_drain(dve, f"{pre}{t}")
                    sqr = sqr_s5 if name in "qk" else sqr_late
                    link(tt(sqr, src[:, t, :], src[:, t, :], ALU.mult))
                    c = EVC[name] + t * heads
                    link(V.reduce_sum(sq[:, c:c + heads], sqr.rearrange("p (h n) -> p h n", h=heads), AX.X))
                mean_sq(name)

            def head_rows(name, src, tiles, heads, width):
                root(name)
                for t in range(tiles):
                    c = EVC[name] + t * heads
                    v = src[:, t, :].rearrange("p (h n) -> p h n", h=heads)
                    tt(v, v, rs[:, c:c + heads].unsqueeze(2).to_broadcast([128, heads, width]), ALU.mult)\
                        .then_inc(xn_ready, 1)

            V.memset(ones[:, :], 1.0).then_inc(ones_ok, 1)
            V.memset(relb[NB:NB + 1, :], NEG).then_inc(relb_ok, 1)
            dve.wait_ge(par_in, 64)
            V.tensor_copy(prow[:, 2, :].rearrange("p (b n) -> p b n", b=2),
                          lsrow[:, :].unsqueeze(2).to_broadcast([GP, 2, NS])).then_inc(step_row, 1)
            p = read(dve, "lam")
            drained(V.tensor_copy(lam[:, :], p[:, 0:3 * GP + KD]), "lam")
            after_drain(dve, "lam")
            c = lambda i: sp[:, i, :]
            dve.wait_ge(stp_ready, 1)
            link(V.tensor_scalar_min(c(11), lam[:, 0:GP], -1e-4))
            tt(c(3), c(11), c(2), ALU.mult).then_inc(sa_ready, 1)
            link(tt(c(4), lam[:, GP:2 * GP], c(2), ALU.mult))
            MAGIC = 12582912.0
            C1 = 6.28125
            C2 = round((2 * math.pi - C1) * 2 ** 22) / 2 ** 22
            C3 = 2 * math.pi - C1 - C2
            TOP = 3.141592
            link(ts(c(12), c(4), 1 / (2 * math.pi), MAGIC, ALU.mult, ALU.add))
            link(V.tensor_scalar_sub(c(12), c(12), MAGIC))
            link(stt(c(7), c(12), -C1, c(4), ALU.mult, ALU.add))
            link(stt(c(7), c(12), -C2, c(7), ALU.mult, ALU.add))
            link(stt(c(7), c(12), -C3, c(7), ALU.mult, ALU.add))
            link(ts(c(7), c(7), TOP, -TOP, ALU.min, ALU.max))
            link(V.tensor_scalar_mul(c(13), c(7), -1.0))
            link(tt(c(13), c(13), c(7), ALU.max))
            ts(c(9), c(13), -1.0, math.pi / 2, ALU.mult, ALU.add).then_inc(ang_ready, 1)
            dve.wait_ge(sq_done, TT)
            mean_sq("x")
            root("x")
            scale_rows("x", xr, xr, TT)
            split_lo(dve, 0)
            split_lo(dve, 1)
            dve.wait_ge(sin_ready, 1)
            dve.wait_ge(mag_ready, 1)
            tt(pw[:, 0, :, 1], c(5), c(10), ALU.mult)
            tt(pw[:, 1, :, 1], c(5), c(8), ALU.mult)
            tt(c(12), c(11), c(11), ALU.mult)
            link(tt(c(13), lam[:, GP:2 * GP], lam[:, GP:2 * GP], ALU.mult))
            link(tt(c(12), c(12), c(13), ALU.add))
            link(V.reciprocal(c(12), c(12)))
            link(V.tensor_scalar_add(c(14), pw[:, 0, :, 1], -1.0))
            tt(c(15), c(14), c(11), ALU.mult)
            tt(c(16), pw[:, 1, :, 1], lam[:, GP:2 * GP], ALU.mult)
            tt(c(17), pw[:, 1, :, 1], c(11), ALU.mult)
            link(tt(c(18), c(14), lam[:, GP:2 * GP], ALU.mult))
            tt(c(15), c(15), c(16), ALU.add)
            link(tt(c(17), c(17), c(18), ALU.subtract))
            tt(c(0), c(15), c(12), ALU.mult)
            link(tt(c(1), c(17), c(12), ALU.mult))
            a_, b_ = c(10), c(8)
            for i in range(3):
                n0, n1 = (ph[:, 0, :, 1], ph[:, 1, :, 1]) if i == 2 else (c(19 + 2 * i), c(20 + 2 * i))
                tt(c(14), a_, a_, ALU.mult)
                tt(c(15), b_, b_, ALU.mult)
                link(tt(c(16), a_, b_, ALU.mult))
                tt(n0, c(14), c(15), ALU.subtract)
                last = V.tensor_scalar_mul(n1, c(16), 2.0)
                if i < 2:
                    link(last)
                else:
                    last.then_inc(par_ready, 1)
                a_, b_ = n0, n1
            after_drain(dve, "par")
            for d in range(KD):
                g = lam[:, 3 * GP + d:3 * GP + d + 1]
                p = read(dve, f"x{d}")
                drained(lo_of(p[:, :], xs[:, 0, d, :], xs[:, 1, d, :], g), f"x{d}")
                if d == 3:
                    split_lo(dve, 2)
                    split_lo(dve, 3)
            dve.wait_ge(sq_done, TT + MT)
            mean_sq("mem")
            root("mem")
            scale_rows("mem", memr, memr, MT)
            for m in range(4):
                split_lo(dve, U_Q + m)
            for i in range(4):
                p = read(dve, f"m{i}")
                dve.wait_ge(act_hi, n_hi[0] + 2)
                for j in range(2):
                    cc = COL["norm_mem"] + 2 * i + j
                    at = slice(i * 512 + j * M, i * 512 + (j + 1) * M)
                    ins = lo_of(p[:, j * M:(j + 1) * M], bs[:, 0, at], bs[:, 1, at], gcol[:, cc:cc + 1])
                drained(ins, f"m{i}")

            def weights_in(q):
                if q >= 2:
                    read(dve, f"vr{q - 2}")
                drained(V.tensor_copy(w1[:, q % 2, 0, :], read(dve, f"w1r{q}")[:, :]), f"w1r{q}")

            def scan(q):
                if q == 0:
                    dve.wait_ge(ph_ready, 1)
                else:
                    dve.wait_ge(z_ready, q)
                if q >= 1:
                    read(dve, f"yo{q - 1}")
                vr = read(dve, f"vr{q}")[:, 0:QP * NC].rearrange("p (g k) -> p g k", g=QP)
                vi = read(dve, f"vi{q}")[:, 0:QP * NC].rearrange("p (g k) -> p g k", g=QP)
                co, si = (ph[:, i, q * QP:(q + 1) * QP, :] for i in range(2))
                t = [dtmp[:, i] for i in range(4)]
                zr, zi = zb[:, 0], zb[:, 1]
                tt(t[0], vr, co, ALU.mult)
                drained(tt(t[3], vr, si, ALU.mult), f"vr{q}")
                tt(t[1], vi, si, ALU.mult)
                drained(tt(t[2], vi, co, ALU.mult), f"vi{q}")
                after_drain(dve, f"vr{q}")
                after_drain(dve, f"vi{q}")
                tt(zr, t[0], t[1], ALU.add)
                link(tt(zi, t[2], t[3], ALU.subtract))
                for g in range(QP):
                    decay = sp[:, 6, q * QP + g:q * QP + g + 1].to_broadcast([128, NC])
                    V.tensor_tensor_scan(t[0][:, g, :], decay, zr[:, g, :], 0.0, ALU.mult, ALU.add)
                    last = V.tensor_tensor_scan(t[1][:, g, :], decay, zi[:, g, :], 0.0, ALU.mult, ALU.add)
                link(last)
                tt(t[2], t[0], co, ALU.mult)
                link(tt(t[3], t[1], si, ALU.mult))
                link(tt(zr, t[2], t[3], ALU.subtract))
                tt(t[2], t[0], si, ALU.mult)
                link(tt(t[3], t[1], co, ALU.mult))
                tt(zi, t[2], t[3], ALU.add).then_inc(z_ready, 1)

            def skip_in(q):
                dve.wait_ge(y_in[q], 16 * QG)
                g = gcol[:, COL["ssm_d"] + q:COL["ssm_d"] + q + 1]
                stt(uT[:, q, :], uT[:, q, :], g, yst, ALU.mult, ALU.add).then_inc(zz_ready, 1)

            def transposed(pre, dst, gain, scale):
                for t in range(TT):
                    p = read(dve, f"{pre}{t}")
                    drained(ts(dst[:, :, t * 128:(t + 1) * 128], p[:, :].rearrange("p (a b) -> p a b", a=4),
                               gcol[:, COL[gain]:COL[gain] + 1], scale, ALU.mult, ALU.mult), f"{pre}{t}")

            split_lo(dve, 8)
            split_lo(dve, 9)
            weights_in(0)
            split_lo(dve, 10)
            scan(0)
            head_event("q", qk, TT, H, "q")
            split_lo(dve, 11)
            weights_in(1)
            head_rows("q", qk, TT, H, HD)
            split_lo(dve, 12)
            scan(1)
            split_lo(dve, 13)
            transposed("qt", qT, "attn_qn", HD ** -0.5)
            weights_in(2)
            skip_in(0)
            split_lo(dve, 14)
            scan(2)
            head_event("k", qk, TT, H, "k")
            split_lo(dve, 15)
            weights_in(3)
            head_rows("k", qk, TT, H, HD)
            skip_in(1)
            split_lo(dve, 16)
            scan(3)
            split_lo(dve, 17)
            transposed("kt", kT, "attn_kn", 1.0)
            skip_in(2)
            split_lo(dve, 18)
            V.memset(bias[:, :, 0:256], 0.0).then_inc(far_zero, 1)
            skip_in(3)
            split_lo(dve, 19)
            dve.wait_ge(far_zero, 1)
            dve.wait_ge(bias_in, 16)

            def normalise(bank, l0, heads, width, t):
                p = read(dve, bank)
                link(V.reciprocal(rl[:, 0:heads], lsum[:, l0:l0 + heads]))
                drained(tt(yrow[:, t, :].rearrange("p (h n) -> p h n", h=heads),
                           p[:, :].rearrange("p (h n) -> p h n", h=heads),
                           rl[:, 0:heads].unsqueeze(2).to_broadcast([128, heads, width]), ALU.mult), bank)
                after_drain(dve, bank)

            for s in range(TT * H):
                h, n = s % H, (s // H + 1) * 128
                p = read(dve, f"sc{s}")
                V.tensor_tensor_reduce(out=p[:, 0:n], in0=p[:, 0:n], in1=bias[:, h, 512 - n:512], scale=-1.0,
                                       scalar=3.0e38, op0=ALU.add, op1=ALU.min,
                                       accum_out=nmx[:, s:s + 1]).then_inc(logit_ready, 1)
                if s >= 2 and s % 2 == 0:
                    pt_evac(dve, V.tensor_copy, s - 1)
                if s >= 4 and (s - 4) % 3 == 0 and (s - 4) // 3 < 8:
                    split_lo(dve, 20 + (s - 4) // 3)
                if s == 16:
                    head_event("mk", mkrow, MT, XH, "mk")
                if s == 19:
                    head_rows("mk", mkrow, MT, XH, XD)
                if s in (10, 18, 26):
                    qd = (s - 10) // 8
                    normalise(f"pv{qd}", H * qd, H, HD, qd)
                if s == 29:
                    for q in range(NQ):
                        lo_of(uT[:, q, :], bs[:, 0, q * 512:(q + 1) * 512], bs[:, 1, q * 512:(q + 1) * 512])\
                            .then_inc(act_lo, 1)
            pt_evac(dve, V.tensor_copy, TT * H - 1)
            normalise(f"pv{TT - 1}", H * (TT - 1), H, HD, TT - 1)
            dve.wait_ge(sq_done, TT + MT + TT)
            mean_sq("ya")
            root("ya")
            scale_rows("ya", yrow, yrow, TT)
            for m in range(4):
                after_drain(dve, f"z{m}")
                tt(uT[:, m, :], uT[:, m, :], sg[:, m, :], ALU.mult).then_inc(y2_ready, 1)
                if m % 2 == 1:
                    split_lo(dve, 28 + m // 2)
            for cc in range(4):
                g = gcol[:, COL["gnorm_attn"] + cc:COL["gnorm_attn"] + cc + 1]
                p = read(dve, f"ya{cc}")
                drained(lo_of(p[:, :], xs[:, 0, 4 + cc, :], xs[:, 1, 4 + cc, :], g), f"ya{cc}")
            p = read(dve, "ss")
            drained(V.tensor_copy(ev(sq, "ss"), p[:, 0:TT]), "ss")
            after_drain(dve, "ss")
            mean_sq("ss")
            root("ss", ssr_ready)
            p = read(dve, "bc")
            for cc in range(4):
                tt(uT[:, cc, :], uT[:, cc, :], p[:, :], ALU.mult).then_inc(y3_ready, 1)
            for cc in range(4):
                g = gcol[:, COL["gnorm_ssm"] + cc:COL["gnorm_ssm"] + cc + 1]
                dve.wait_ge(y3_ready, cc + 1)
                ins = lo_of(uT[:, cc, :].rearrange("p (i k) -> p i k", i=L), to_tokens(xs[:, 0, cc, :]),
                            to_tokens(xs[:, 1, cc, :]), g)
            drained(ins, "bc")

            def residual(pre, half):
                for t in range(TT):
                    p = read(dve, f"{pre}{half}{t}")
                    o = hres[:, t, half * 512:(half + 1) * 512]
                    drained(tt(o, o, p[:, :], ALU.add), f"{pre}{half}{t}")

            def norm_rows(name, squares, gain):
                dve.wait_ge(sq_done, squares)
                mean_sq(name)
                root(name)
                scale_rows(name, xr, hres, TT)
                for d in range(KD):
                    g = gcol[:, COL[gain] + d:COL[gain] + d + 1]
                    p = read(dve, f"{name}{d}")
                    drained(lo_of(p[:, :], xs[:, 0, d, :], xs[:, 1, d, :], g), f"{name}{d}")

            for u in range(U_OUT, U_OUT + 4):
                split_lo(dve, u + 4)
            dve.wait_ge(h_in, 16 * TT)
            residual("o", 0)
            for u in range(U_OUT + 4, U_OUT + 8):
                split_lo(dve, u + 4)
            residual("o", 1)
            norm_rows("x2", 2 * TT + MT + TT, "norm_xattn")
            for u in range(U_XQ, U_XQ + 4):
                split_lo(dve, u + 4)
            head_event("qx", qk, TT, XH, "qx")
            head_rows("qx", qk, TT, XH, XD)
            transposed("qxt", qT, "x_qn", XD ** -0.5)
            for s in range(TT * XH):
                p = read(dve, f"xs{s}")
                V.tensor_reduce(nmx[:, 32 + s:33 + s], p[:, 0:M], AX.X, ALU.max, negate=True)\
                    .then_inc(logit_ready, 1)
                if s >= 2 and s % 2 == 0:
                    xp_evac(dve, V.tensor_copy, s - 1)
                if s % XH == 2 and s > XH:
                    normalise(f"xpv{s // XH - 1}", 32 + XH * (s // XH - 1), XH, XD, s // XH - 1)
            xp_evac(dve, V.tensor_copy, TT * XH - 1)
            normalise(f"xpv{TT - 1}", 32 + XH * (TT - 1), XH, XD, TT - 1)
            for cc in range(4):
                p = read(dve, f"xo{cc}")
                at = slice(cc * 512, (cc + 1) * 512)
                drained(lo_of(p[:, :], bs[:, 0, at], bs[:, 1, at]), f"xo{cc}")
            split_lo(dve, U_XO + 4)
            split_lo(dve, U_XO + 5)
            residual("w", 0)
            split_lo(dve, U_XO + 6)
            split_lo(dve, U_XO + 7)
            residual("w", 1)
            norm_rows("x3", 2 * TT + MT + 2 * TT, "norm_ffn")
            for i in range(FT // 2):
                for j in range(4):
                    k = 4 * i + j
                    tile = 2 * i + j if j < 2 else FT + 2 * i + j - 2
                    p = read(dve, f"f{k}")
                    dve.wait_ge(conv_ready, k + 1)
                    o = cv[:, j, :]
                    link(stt(o[:, 1:], p[:, 0:T - 1], ccol[:, 1, tile:tile + 1], o[:, 1:], ALU.mult, ALU.add))
                    drained(stt(o[:, 2:], p[:, 0:T - 2], ccol[:, 0, tile:tile + 1], o[:, 2:], ALU.mult, ALU.add), f"f{k}")
                    split_lo(dve, U_UP + k + 4)
                    if j >= 2:
                        after_drain(dve, f"f{k}")
                        dve.wait_ge(gate_ready, 2 * i + j - 1)
                        tt(hff[:, 2 * i + j - 2, :], cv[:, j - 2, :], o, ALU.mult).then_inc(hff_ready, 1)
            for n in range(FT):
                at = slice(n % 4 * 512, n % 4 * 512 + 512)
                lo_of(hff[:, n, :], bs[:, 0, at], bs[:, 1, at]).then_inc(act_lo, 1)
                if n >= 1 and U_DOWN + n + 3 < U_END:
                    split_lo(dve, U_DOWN + n + 3)
            for b in range(8):
                t, half = b // 2, b % 2
                o = hres[:, t, half * 512:(half + 1) * 512]
                tt(o, o, read(dve, f"d{b}")[:, :], ALU.add).then_inc(res_ready, 1)

        @block.tensor
        def _(pe):
            def mm(o, l, r, start=True, stop=True):
                return nc.tensor.matmul(o, l, r, start=start, stop=stop)

            def tr(o, i):
                return nc.tensor.transpose(o, i, ident[0:i.shape[0], 0:i.shape[0]])

            def used(ins, u):
                if u in DONE:
                    filled(ins, DONE[u])
                else:
                    ins.then_inc(unit_used, 1)

            def cols_unit(u, kts, xhi, bank_names):
                pe.wait_ge(lo_done, u + 1)
                wh, wl = w_unit(u, 0), w_unit(u, 1)
                for i, name in enumerate(bank_names):
                    p = fill(pe, name)
                    for k in range(kts):
                        at = slice(i * 128, (i + 1) * 128)
                        last = mm3(p[:, :], wh[:, k, at], wl[:, k, at], xhi(0, k), xhi(1, k), k == 0, k == kts - 1)
                    filled(last, name)

            def rows_unit(u, u0, units, act_tile, tiles, names):
                pe.wait_ge(lo_done, u + 1)
                j = u - u0
                for t in range(tiles):
                    if j == 0:
                        fill(pe, names[t])
                    p = pb[uses[names[t]][0]]
                    for k in range(2):
                        kk = 2 * j + k
                        last = mm3(p[:, :], act_tile(0, kk, t), act_tile(1, kk, t), w_unit(u, 0)[:, k, :],
                                   w_unit(u, 1)[:, k, :], kk == 0, kk == 2 * units - 1)
                    if j == units - 1:
                        filled(last, names[t])
                if j < units - 1:
                    last.then_inc(unit_used, 1)

            x_tile = lambda part, k, t: xs[:, part, k, t * 128:(t + 1) * 128]
            m_tile = lambda part, k, t: bs[:, part, k * M + t * 128:k * M + (t + 1) * 128]
            o_tile = lambda part, k, t: bs[:, part, k * 512 + t * 128:k * 512 + (t + 1) * 128]
            names = lambda pre, n: [f"{pre}{t}" for t in range(n)]

            def proj(u, u0, pre):
                rows_unit(u, u0, 4, x_tile, TT, names(pre, TT))

            pe.wait_ge(ident_ok, 1)
            pe.wait_ge(par_in, 64)
            pe.wait_ge(step_row, 1)
            p = fill(pe, "lam")
            for i in range(3):
                tr(p[:, i * GP:(i + 1) * GP], prow[:, i, :])
            filled(tr(p[:, 3 * GP:3 * GP + KD], nrow[:, :]), "lam")
            pe.wait_ge(gain_in, 16 * N_GAIN)
            pe.wait_ge(conv_in, 16 * 4)
            p = fill(pe, "par")
            tr(p[:, 0:NG], grow[:, :])
            tr(p[:, 64:152], crow[:, 0, :])
            filled(tr(p[:, 152:240], crow[:, 1, :]), "par")
            pe.wait_ge(c_in, 16 * 4)
            for i, name in enumerate(("cr", "cm")):
                p = fill(pe, name)
                for a in range(4):
                    last = tr(p[:, a * 128:(a + 1) * 128], craw[:, i, a, :])
                filled(last, name)
            pe.wait_ge(relb_in, 32)
            pe.wait_ge(relb_ok, 1)
            p = fill(pe, "relb")
            filled(mm(p[0:H, 0:384], relb[:, :], qk[0:NB + 1, 3, 0:384]), "relb")

            def transposes(pre, count, base, src, tiles=TT):
                pe.wait_ge(xn_ready, base)
                for d in range(count):
                    p = fill(pe, f"{pre}{d}")
                    for t in range(tiles):
                        last = tr(p[:, t * 128:(t + 1) * 128], src(d, t))
                    filled(last, f"{pre}{d}")

            transposes("x", KD, TT, lambda d, t: xr[:, t, d * 128:(d + 1) * 128])
            after_drain(pe, f"x{KD - 1}")
            for d in range(KD):
                after_drain(pe, f"x{d}")
            for m in range(4):
                cols_unit(U_SSM + m, KD, lambda part, k: xs[:, part, k, :], [f"u{m}"])
            transposes("m", 4, TT + MT, lambda i, j: memr[:, j % 2, (2 * i + j // 2) * 128:(2 * i + j // 2 + 1) * 128])

            def weights_in(q):
                pe.wait_ge(w1p_ready, q + 1)
                for i, n in enumerate("ri"):
                    p = fill(pe, f"w1{n}{q}")
                    for g in range(QP):
                        last = tr(p[:, g * 128:(g + 1) * 128], w1p[:, i, g * 128:(g + 1) * 128])
                    filled(last, f"w1{n}{q}")
                pe.wait_ge(ca_ready, q + 1)
                p = [fill(pe, f"k{n}{q}") for n in "ab"]
                for a in range(QP):
                    at = slice(a * (L + 1) * CG, a * (L + 1) * CG + L * CG)
                    for part in range(2):
                        for b in range(2):
                            rows = slice(b * NS, (b + 1) * NS)
                            last = mm(p[b][0:CG, a * 128:(a + 1) * 128], bb[rows, part, q * QP + a, :],
                                      ca[rows, q % 2, part, at], part == 0, part == 1)
                            if a == QP - 1 and part == 1:
                                filled(last, f"k{'ab'[b]}{q}")

            def states_in(q):
                pe.wait_ge(u_in, 16 * L)
                after_drain(pe, f"w1r{q}")
                after_drain(pe, f"w1i{q}")
                for i, n in enumerate("ri"):
                    p = fill(pe, f"v{n}{q}")
                    for g in range(QG):
                        rows, gp = slice(g % 2 * NS, g % 2 * NS + NS), g // 2
                        last = mm(p[rows, gp * NC:(gp + 1) * NC],
                                  w1[:, q % 2, i, gp * 128 + g % 2 * NS:gp * 128 + g % 2 * NS + NS],
                                  ub[:, q * QG + g, :])
                    filled(last, f"v{n}{q}")

            def outputs(q):
                pe.wait_ge(t_in[q], 16 * L)
                pe.wait_ge(z_ready, q + 1)
                p = [fill(pe, f"y{n}{q}") for n in "eo"]
                for a in range(QP):
                    for b in range(2):
                        g = 2 * a + b
                        mm(p[b][:, a * NC:(a + 1) * NC], toep[:, g, :], ub[:, q * QG + g, :], True, False)
                    at = slice((a * (L + 1) + 1) * CG, (a + 1) * (L + 1) * CG)
                    for part in range(2):
                        for b in range(2):
                            rows = slice(b * NS, (b + 1) * NS)
                            last = mm(p[b][:, a * NC + 1:(a + 1) * NC], ca[rows, q % 2, part, at],
                                      zb[rows, part, a, 0:NC - 1], False, part == 1)
                            if a == QP - 1 and part == 1:
                                filled(last, f"y{'eo'[b]}{q}")

            def head_transposes(pre, base, src, tiles=TT):
                for t in range(tiles):
                    pe.wait_ge(xn_ready, base + t + 1)
                    p = fill(pe, f"{pre}{t}")
                    for a in range(4):
                        last = tr(p[:, a * 128:(a + 1) * 128], src[:, t, a * 128:(a + 1) * 128])
                    filled(last, f"{pre}{t}")

            proj(4, U_Q, "q")
            proj(5, U_Q, "q")
            weights_in(0)
            proj(6, U_Q, "q")
            states_in(0)
            proj(7, U_Q, "q")
            weights_in(1)
            proj(8, U_K, "k")
            outputs(0)
            states_in(1)
            proj(9, U_K, "k")
            N0 = TT + MT
            head_transposes("qt", N0, qk)
            weights_in(2)
            proj(10, U_K, "k")
            outputs(1)
            states_in(2)
            proj(11, U_K, "k")
            weights_in(3)
            proj(12, U_V, "v")
            outputs(2)
            states_in(3)
            proj(13, U_V, "v")
            head_transposes("kt", N0 + TT, qk)
            proj(14, U_V, "v")
            outputs(3)
            proj(15, U_V, "v")

            def scores(s):
                qt, h = s // H, s % H
                rows = slice(h % 2 * HD, h % 2 * HD + HD)
                p = fill(pe, f"sc{s}")
                n = (qt + 1) * 128
                filled(mm(p[:, 0:n], qT[rows, h // 2, qt * 128:(qt + 1) * 128], kT[rows, h // 2, 0:n]), f"sc{s}")

            def prob_transposes(pre, sc, s, tiles):
                after_drain(pe, f"{sc}{s}")
                p = fill(pe, f"{pre}{s}")
                for a in range(tiles):
                    last = tr(p[:, a * 128:(a + 1) * 128], pbuf[:, s % 2, a * 128:(a + 1) * 128])
                filled(last, f"{pre}{s}")

            def values(s, heads, width, pt, bank, tiles, v):
                t, h = s // heads, s % heads
                after_drain(pe, f"{pt}{s}")
                p = fill(pe, f"{bank}{t}") if h == 0 else pb[uses[f"{bank}{t}"][0]]
                for a in range(tiles):
                    last = mm(p[:, h * width:(h + 1) * width], ptb[:, s % 2, a * 128:(a + 1) * 128],
                              v[:, a, h * width:(h + 1) * width], a == 0, a == tiles - 1)
                if h == heads - 1:
                    filled(last, f"{bank}{t}")
                else:
                    last.then_inc(pv_done, 1)

            for t in range(TT):
                after_drain(pe, f"qt{t}")
                after_drain(pe, f"kt{t}")
                after_drain(pe, f"v{t}")
            scores(0)
            for s in range(TT * H):
                if s + 1 < TT * H:
                    scores(s + 1)
                if s >= 2 and (s - 2) % 3 == 0 and (s - 2) // 3 < 8:
                    u = U_MK + (s - 2) // 3
                    if u < U_MV:
                        rows_unit(u, U_MK, 4, m_tile, MT, names("mk", MT))
                    else:
                        rows_unit(u, U_MV, 4, m_tile, MT, names("mv", MT))
                prob_transposes("pt", "sc", s, s // H + 1)
                if s >= 1:
                    values(s - 1, H, HD, "pt", "pv", (s - 1) // H + 1, vrow)
            values(TT * H - 1, H, HD, "pt", "pv", TT, vrow)
            N1 = N0 + 2 * TT
            pe.wait_ge(xn_ready, N1 + MT)
            for i in range(2):
                p = fill(pe, f"kx{i}")
                for h in range(2):
                    for t in range(MT):
                        last = tr(p[:, h * M + t * 128:h * M + (t + 1) * 128],
                                  mkrow[:, t, (2 * i + h) * XD:(2 * i + h + 1) * XD])
                filled(last, f"kx{i}")
            pe.wait_ge(act_lo, NQ)
            for i in range(2):
                cols_unit(U_GLU + i, 4, lambda part, k: bs[:, part, k * 512:(k + 1) * 512], [f"z{2 * i}", f"z{2 * i + 1}"])
            transposes("ya", 4, N1 + MT + TT, lambda d, t: yrow[:, t, d * 128:(d + 1) * 128])
            pe.wait_ge(ones_ok, 1)
            pe.wait_ge(ysq_ready, 4)
            p = fill(pe, "ss")
            for t in range(TT):
                for c in range(4):
                    last = mm(p[:, t:t + 1], sg[:, c, t * 128:(t + 1) * 128], ones[:, 0:1], c == 0, c == 3)
            filled(last, "ss")
            pe.wait_ge(ssr_ready, 1)
            p = fill(pe, "bc")
            for t in range(TT):
                cc = EVC["ss"] + t
                last = mm(p[:, t * 128:(t + 1) * 128], rs[:, cc:cc + 1].to_broadcast([128, 128]), ident[:, :])
            filled(last, "bc")
            for c in range(4):
                after_drain(pe, f"ya{c}")
            after_drain(pe, "bc")
            for u in range(U_OUT, U_OUT + 8):
                half = (u - U_OUT) // 4
                proj(u, U_OUT + 4 * half, f"o{half}")
            N2 = N1 + MT + TT
            transposes("x2", KD, N2 + TT, lambda d, t: xr[:, t, d * 128:(d + 1) * 128])
            for d in range(KD):
                after_drain(pe, f"x2{d}")
            for u in range(U_XQ, U_XQ + 4):
                proj(u, U_XQ, "qx")
            head_transposes("qxt", N2 + TT, qk)

            def x_scores(s):
                t, h = s // XH, s % XH
                p = fill(pe, f"xs{s}")
                filled(mm(p[:, 0:M], qT[:, h, t * 128:(t + 1) * 128], kxT[:, h, :]), f"xs{s}")

            for t in range(TT):
                after_drain(pe, f"qxt{t}")
            after_drain(pe, "kx0")
            after_drain(pe, "kx1")
            after_drain(pe, "mv0")
            after_drain(pe, "mv1")
            x_scores(0)
            for s in range(TT * XH):
                if s + 1 < TT * XH:
                    x_scores(s + 1)
                prob_transposes("xp", "xs", s, MT)
                if s >= 1:
                    values(s - 1, XH, XD, "xp", "xpv", MT, xv)
            values(TT * XH - 1, XH, XD, "xp", "xpv", MT, xv)
            for c in range(4):
                for t in range(TT):
                    after_drain(pe, f"xpv{t}")
                p = fill(pe, f"xo{c}")
                for t in range(TT):
                    last = tr(p[:, t * 128:(t + 1) * 128], yrow[:, t, c * 128:(c + 1) * 128])
                filled(last, f"xo{c}")
            for c in range(4):
                after_drain(pe, f"xo{c}")
            for u in range(U_XO, U_XO + 4):
                half = (u - U_XO) // 2
                rows_unit(u, U_XO + 2 * half, 2, o_tile, TT, names(f"w{half}", TT))
            transposes("x3", KD, N2 + 3 * TT, lambda d, t: xr[:, t, d * 128:(d + 1) * 128])
            for d in range(KD):
                after_drain(pe, f"x3{d}")
            for k in range(2 * FT):
                cols_unit(U_UP + k, KD, lambda part, kk: xs[:, part, kk, :], [f"f{k}"])
            for n in range(FT):
                u = U_DOWN + n
                pe.wait_ge(lo_done, u + 1)
                pe.wait_ge(act_lo, NQ + n + 1)
                for b in range(8):
                    t, half = b // 2, b % 2
                    p = fill(pe, f"d{b}") if n == 0 else pb[b]
                    at = slice(n % 4 * 512 + t * 128, n % 4 * 512 + (t + 1) * 128)
                    cols = slice(half * 512, (half + 1) * 512)
                    last = mm3(p[:, :], bs[:, 0, at], bs[:, 1, at], w_unit(u, 0)[:, 0, cols], w_unit(u, 1)[:, 0, cols],
                               n == 0, n == FT - 1)
                    if n == FT - 1:
                        filled(last, f"d{b}")
                if n < FT - 1:
                    last.then_inc(unit_used, 1)


INPUTS = ["x", "mem", "norm_mix", "w_in", "attn_qn", "attn_kn", "ssm_lam_re", "ssm_lam_im", "ssm_log_step",
          "ssm_b_re", "ssm_b_im", "ssm_c_re", "ssm_c_im", "ssm_d", "ssm_w_glu", "ssm_b_glu", "gnorm_ssm",
          "gnorm_attn", "w_out", "rel_bias", "norm_xattn", "norm_mem", "x_wq", "x_wkv", "x_wo", "x_qn",
          "x_kn", "norm_ffn", "ffn_w_up", "ffn_conv_w", "ffn_conv_b", "ffn_w_down"]


def kernel(**inputs):
    import concourse.bacc as bacc
    from concourse.bass_utils import run_bass_kernel_spmd

    nc = bacc.Bacc("TRN2", target_bir_lowering=False, num_devices=1)
    arrays, aps = {}, {}
    for name in INPUTS:
        a = np.ascontiguousarray(inputs[name])
        arrays[f"in_{name}"] = a
        aps[name] = nc.dram_tensor(f"in_{name}", a.shape, mybir.dt.from_np(a.dtype), kind="ExternalInput").ap()
    arrays["in_buckets"] = bucket_table()
    aps["buckets"] = nc.dram_tensor("in_buckets", (NB + 1, 384), mybir.dt.float32, kind="ExternalInput").ap()
    out = nc.dram_tensor("out_0", (1, T, D), mybir.dt.float32, kind="ExternalOutput").ap()
    layer(nc, aps, out)
    r = run_bass_kernel_spmd(nc, [arrays], core_ids=[0])
    return r.results[0]["out_0"]
```

```python
import math
from contextlib import ExitStack

import numpy as np
import concourse.bass as bass
from concourse import mybir

T = 512
TT = T // 128
D = 1024
KD = D // 128
DS = 512
G, CG, NS = 32, 16, 64
GP = G // 2
H, HD = 8, 64
M = 256
MT = M // 128
XH, XD = 4, 128
DF = 2816
FT = DF // 128
EPS = 1e-6
NEG = -1e30
NB, MAXD = 32, 128
L = 8
NC = T // L
QG = 8
NQ = G // QG
QP = QG // 2

GAINS = [("norm_xattn", 8), ("norm_mem", 8), ("norm_ffn", 8), ("gnorm_ssm", 4),
         ("gnorm_attn", 4), ("ssm_d", 4), ("ssm_b_glu", 4), ("x_qn", 1), ("x_kn", 1),
         ("attn_qn", 1), ("attn_kn", 1)]
N_GAIN = len(GAINS) + 2
COL = {}
_at = 0
for _n, _k in GAINS:
    COL[_n] = _at
    _at += _k
NG = _at

U_SSM, U_Q, U_K, U_V, U_MK, U_MV = 0, 4, 8, 12, 16, 20
U_GLU, U_OUT, U_XQ, U_XO, U_UP, U_DOWN = 24, 26, 34, 38, 42, 86
U_OA = U_OUT + 4
U_END = U_DOWN + FT


MK_AT = [0, 1, 2, 3]
MV_AT = [5, 6, 7, 8]
GLU_AT = [9, 10, 11, 12]
SOUT_AT = [23, 23, 24, 24, 25, 25, 26, 26, 27, 27, 28, 28, 29, 30, 31, 31]
SPLIT_AT = {2: 20, 3: 21, 4: 22, 5: 23, 7: 24, 8: 25, 9: 26, 10: 27, 12: 28, 14: 29, 31: 30}
YA_AT = [13, 18, 26]


def bucket_table():
    t = np.zeros((NB + 1, 384), np.float32)
    half = NB // 2
    for y in range(384):
        dist = 255 - y
        if dist < 0:
            t[NB, y] = 1.0
            continue
        b = dist
        if dist >= half:
            b = min(half + int(math.log(dist / half) / math.log(MAXD / half) * (NB - half)), NB - 1)
        t[b, y] += 1.0
        t[NB - 1, y] -= 1.0
    return t


def layer(nc, A, out):
    f32, f32r = mybir.dt.float32, mybir.dt.float32r
    ALU, ACT, AX = mybir.AluOpType, mybir.ActivationFunctionType, mybir.AxisListType

    scr_u = nc.dram_tensor("scr_u", (DS, L, NC), f32).ap()
    scr_y = nc.dram_tensor("scr_y", (NQ, 128, QG, NC), f32).ap()
    scr_b = nc.dram_tensor("scr_b", (128 * H * 384,), f32).ap()

    ctx = ExitStack()
    with ctx:
        def sb(name, shape, dt=f32):
            return ctx.enter_context(nc.sbuf_tensor(name, shape, dt))

        def sem(name):
            return ctx.enter_context(nc.semaphore(name))

        wring = sb("wring", [128, 4, 2, 1024], f32r)
        xs = sb("xs", [128, 2, KD, T], f32r)
        bs = sb("bs", [128, 2, 2048], f32r)
        raw = sb("raw", [128, 2, 2048])
        ident = sb("ident", [128, 128])
        ones = sb("ones", [128, 1])
        lsrow = sb("lsrow", [GP, 2])
        relb = sb("relb", [NB + 1, H])
        gcol = sb("gcol", [128, NG])
        ccol = sb("ccol", [128, 4, 2 * FT])
        lam = sb("lam", [128, 3 * GP + KD])
        sp = sb("sp", [128, 24, GP])
        pw = sb("pw", [128, 2, GP, L + 1])
        st = sb("st", [128, 160])
        nmx = sb("nmx", [128, 48])
        lsum = sb("lsum", [128, 48])
        rl = sb("rl", [128, 16])
        F = sb("F", [128, 4096 + 12416 + 2048 + 2048 + 2048 + 4096])

        def region(at, *dims):
            n = int(np.prod(dims))
            v = F[:, at:at + n]
            if len(dims) == 1:
                return v
            names = "abcd"[:len(dims)]
            return v.rearrange(f"p ({' '.join(names)}) -> p {' '.join(names)}",
                               **{k: d for k, d in zip(names, dims)})

        ph = region(0, 2, GP, NC)
        w1 = region(2048, 2, 2, 512)
        bias = region(0, H, 512)
        R0 = 4096
        ca = region(R0, 2, 2, QP * (L + 1) * CG)
        w1p = region(R0 + 2304, 2, 512)
        kt = region(R0 + 3328, QG, 128)
        toep = region(R0 + 4352, QG, 128)
        ub = region(R0 + 5376, G, NC)
        craw = region(R0 + 5376, 2, 4, 128)
        zb = region(R0 + 7424, 2, QP, NC)
        dtmp = region(R0 + 7936, 4, QP, NC)
        ptmp = region(R0 + 8960, 2, 576)
        yb = region(R0 + 10112, 512)
        bmat = region(R0 + 10112, 2, GP, CG)
        yst = region(R0 + 10624, 512)
        cmat = region(R0 + 11136, 3, GP, CG)
        bb = region(R0 + 11904, 2, GP, CG)
        pbuf = region(R0, 2, 512)
        ptb = region(R0 + 1024, 2, 512)
        yrow = region(R0 + 2048, TT, 512)
        mkrow = region(R0 + 4096, MT, 512)
        kxT = region(R0 + 5120, XH, M)
        xv = region(R0 + 6144, MT, 512)
        hres = region(R0 + 7808, TT, D)
        hff = region(0, FT, T)
        R1 = R0 + 12416
        uT = region(R1, NQ, T)
        grow = region(R0 + 7936, 128)[0:NG]
        nrow = region(R0 + 8832, 128)[0:KD]
        crow = region(R0 + 8064, 2, 128)[0:88]
        prow = region(R0 + 8320, 3, 128)[0:GP]
        qk = region(R1 + 2048, TT, 512)
        sg = region(R1 + 2048, 4, 512)
        gffn = region(0, D)
        xbc = qk[:, 2, :]
        x3row = region(R1 + 4096, 2, D)
        vrow = region(R1 + 4096, TT, 512)
        mrow = region(R1 + 4096, 2048)
        R2 = R1 + 6144
        qT = region(R2, 4, T)
        kT = region(R2 + 2048, 4, T)
        xr = region(R2, TT, D)
        cv = region(R2, 4, T)
        memr = mrow.rearrange("p (t d) -> p t d", t=MT)

        pb = [ctx.enter_context(nc.psum_tensor(f"pb{i}", [128, 512], f32)) for i in range(8)]

        raw_in = [sem("raw_in0"), sem("raw_in1")]
        hi_done, lo_done = sem("hi_done"), sem("lo_done")
        unit_used = sem("unit_used")
        bank_full = [sem(f"bank_full{i}") for i in range(8)]
        bank_free = [sem(f"bank_free{i}") for i in range(8)]
        x_in = [sem(f"x_in{t}") for t in range(TT)]
        mem_in, par_in, gain_in = sem("mem_in"), sem("par_in"), sem("gain_in")
        conv_in, c_in, b_in, relb_in = sem("conv_in"), sem("c_in"), sem("b_in"), sem("relb_in")
        h_in, bias_in = sem("h_in"), sem("bias_in")
        scr_out = sem("scr_out")
        su_out = sem("su_out")
        sy_out = [sem(f"sy_out{q}") for q in range(NQ)]
        u_in = sem("u_in")
        y_in = [sem(f"y_in{q}") for q in range(NQ)]
        t_in = [sem(f"t_in{q}") for q in range(NQ)]
        out_done = sem("out_done")
        ident_ok, zero_ok, ones_ok = sem("ident_ok"), sem("zero_ok"), sem("ones_ok")
        dve_step, act_step, pool_step = sem("dve_step"), sem("act_step"), sem("pool_step")
        step_row, lam_ok = sem("step_row"), sem("lam_ok")
        sq_done = sem("sq_done")
        ms_ready, rs_ready = sem("ms_ready"), sem("rs_ready")
        xn_ready = sem("xn_ready")
        act_hi = sem("act_hi")
        act_lo = sem("act_lo")
        stp_ready, sa_ready, mag_ready = sem("stp_ready"), sem("sa_ready"), sem("mag_ready")
        ang_ready, sin_ready, par_ready = sem("ang_ready"), sem("sin_ready"), sem("par_ready")
        cols_ready, relbv_ready, cmat_ready = sem("cols_ready"), sem("relbv_ready"), sem("cmat_ready")
        ph_ready, w1p_ready, ca_ready = sem("ph_ready"), sem("w1p_ready"), sem("ca_ready")
        w1_ready, kt_ready = sem("w1_ready"), sem("kt_ready")
        uT_ready, z_ready, yb_ready, zz_ready = sem("uT_ready"), sem("z_ready"), sem("yb_ready"), sem("zz_ready")
        row_ready = sem("row_ready")
        qkT_ready = sem("qkT_ready")
        far_zero = sem("far_zero")
        logit_ready, prob_ready, pt_ready, pv_done = (sem("logit_ready"), sem("prob_ready"),
                                                      sem("pt_ready"), sem("pv_done"))
        yrow_ready = sem("yrow_ready")
        gelu_ready, sig_ready, y2_ready, y3_ready = (sem("gelu_ready"), sem("sig_ready"),
                                                     sem("y2_ready"), sem("y3_ready"))
        ysq_ready = sem("ysq_ready")
        h1_ready = sem("h1_ready")
        conv_ready, gate_ready, val_ready = sem("conv_ready"), sem("gate_ready"), sem("val_ready")
        taps_ready, hff_ready = sem("taps_ready"), sem("hff_ready")
        res_ready = sem("res_ready")

        uses, fills = {}, [0] * 8

        def use(bank, name):
            uses[name] = (bank, fills[bank])
            fills[bank] += 1

        def plan():
            use(4, "lam")
            for d in range(KD):
                use(d, f"x{d}")
            use(4, "xb"); use(5, "par"); use(6, "cr"); use(7, "cm"); use(6, "relb")
            for m in range(4):
                use(m, f"u{m}")
            for i in range(4):
                use(4 + i, f"m{i}")

            def sa(q):
                use(4, f"w1r{q}"); use(5, f"w1i{q}"); use(6, f"ka{q}"); use(7, f"kb{q}")

            def sbq(q):
                use(4, f"vr{q}"); use(5, f"vi{q}")
            for p in "qkv":
                for t in range(TT):
                    use(t, f"{p}{t}")
            sa(0); sbq(0); sa(1); use(6, "ye0"); use(7, "yo0"); sbq(1)
            for t in range(TT):
                use(4 + t, f"qt{t}")
            sa(2); use(6, "ye1"); use(7, "yo1"); sbq(2); sa(3); use(6, "ye2"); use(7, "yo2"); sbq(3)
            for t in range(TT):
                use(4 + t, f"kt{t}")
            use(6, "ye3"); use(7, "yo3")
            for s in range(TT * H):
                use(3 + s % 3, f"sc{s}"); use(6, f"pt{s}")
                if s in YA_AT:
                    use(6, f"ya{YA_AT.index(s)}")
            use(6, "ya3")
            for t in range(TT):
                use(7, f"pv{t}")
            use(0, "mk0"); use(1, "mk1")
            use(2, "mv0"); use(0, "mv1")
            use(1, "z0"); use(0, "z1"); use(2, "z2"); use(1, "z3")
            use(0, "ss"); use(1, "kx0"); use(2, "kx1"); use(0, "bc")
            for t in range(TT):
                for half in range(2):
                    use((2 * t + half) % 3, f"g{t}{half}")
            for t in range(TT):
                for half in range(2):
                    use((2 * t + half) % 4, f"o{t}{half}")
                    use(4 + (2 * t + half) % 4, f"x2{t}{half}")
            for t in range(TT):
                use(t, f"qx{t}"); use(t, f"qxt{t}")
            for s in range(TT * XH):
                use(4 + s % 2, f"xs{s}"); use(6, f"xp{s}")
                if s in (6, 10, 14):
                    use(6, f"xo{(s - 6) // 4}")
            use(6, "xo3")
            for t in range(TT):
                use(7, f"xpv{t}")
                for half in range(2):
                    use((2 * t + half) % 4, f"w{t}{half}")
            for t in range(TT):
                for half in range(2):
                    use(4 + (2 * t + half) % 4, f"x3{t}{half}")
            for j in range(2 * FT):
                use(j % 4, f"f{j}")
            for b in range(8):
                use(b, f"d{b}")
        plan()

        DONE = {m: f"u{m}" for m in range(4)}
        DONE.update({U_Q + 3: "q3", U_K + 3: "k3", U_V + 3: "v3", U_MK + 3: "mk1", U_MV + 3: "mv1",
                     U_GLU: "z1", U_GLU + 1: "z3", U_OUT + 1: "g30", U_OUT + 3: "g31",
                     U_OA + 1: "o30", U_OA + 3: "o31", U_XQ + 3: "qx3", U_XO + 1: "w30", U_XO + 3: "w31"})
        DONE.update({U_UP + j: f"f{j}" for j in range(2 * FT)})

        def wait_unit(eng, u):
            if u in DONE:
                bank, n = uses[DONE[u]]
                eng.wait_ge(bank_full[bank], n + 1)
            else:
                eng.wait_ge(unit_used, sum(v not in DONE for v in range(u + 1)))

        def fill(pe, name):
            bank, n = uses[name]
            if n > 0:
                pe.wait_ge(bank_free[bank], n)
            return pb[bank]

        def filled(ins, name):
            ins.then_inc(bank_full[uses[name][0]], 1)

        def read(eng, name):
            bank, n = uses[name]
            eng.wait_ge(bank_full[bank], n + 1)
            return pb[bank]

        def drained(ins, name):
            ins.then_inc(bank_free[uses[name][0]], 1)

        def after_drain(eng, name):
            bank, n = uses[name]
            eng.wait_ge(bank_free[bank], n + 1)

        def wait_values(eng, s, heads, bank, before):
            if s % heads == heads - 1:
                read(eng, f"{bank}{s // heads}")
            else:
                eng.wait_ge(pv_done, before + s + 1 - s // heads)

        def pt_evac(eng, copy, s):
            if s >= 2:
                wait_values(eng, s - 2, H, "pv", 0)
            n = (s // H + 1) * 128
            drained(copy(ptb[:, s % 2, 0:n], read(eng, f"pt{s}")[:, 0:n]), f"pt{s}")

        def xp_evac(eng, copy, s):
            if s >= 2:
                wait_values(eng, s - 2, XH, "xpv", TT * (H - 1))
            drained(copy(ptb[:, s % 2, 0:M], read(eng, f"xp{s}")[:, 0:M]), f"xp{s}")

        def to_tokens(a):
            return a.rearrange("p (k i) -> p i k", i=L)

        w_in = A["w_in"][0].rearrange("(k p) n -> p k n", p=128)
        w_kv = A["x_wkv"][0].rearrange("(k p) n -> p k n", p=128)
        w_glu = A["ssm_w_glu"][0].rearrange("(k p) n -> p k n", p=128)
        w_out = A["w_out"][0].rearrange("(k p) n -> p k n", p=128)
        w_xq = A["x_wq"][0].rearrange("(k p) n -> p k n", p=128)
        w_xo = A["x_wo"][0].rearrange("(k p) n -> p k n", p=128)
        w_up = A["ffn_w_up"][0].rearrange("(k p) n -> p k n", p=128)
        w_dn = A["ffn_w_down"][0].rearrange("(k p) n -> p k n", p=128)

        def chunk_src(c):
            u = 2 * c
            if u < U_Q:
                return w_in[:, :, 256 * c:256 * c + 256]
            if u < U_MK:
                p, j = (u - U_Q) // 4, (u - U_Q) // 2 % 2
                return w_in[:, 4 * j:4 * j + 4, DS * (p + 1):DS * (p + 2)]
            if u < U_GLU:
                p, j = (u - U_MK) // 4, (u - U_MK) // 2 % 2
                return w_kv[:, 4 * j:4 * j + 4, 512 * p:512 * p + 512]
            if u < U_OUT:
                return w_glu
            if u < U_XQ:
                j, p = (u - U_OUT) // 4, (u - U_OUT) // 2 % 2
                return w_out[:, 4 * j:4 * j + 4, 512 * p:512 * p + 512]
            if u < U_XO:
                j = (u - U_XQ) // 2
                return w_xq[:, 4 * j:4 * j + 4, :]
            if u < U_UP:
                p = (u - U_XO) // 2
                return w_xo[:, :, 512 * p:512 * p + 512]
            if u < U_DOWN:
                i, p = (u - U_UP) // 4, (u - U_UP) // 2 % 2
                return w_up[:, :, DF * p + 256 * i:DF * p + 256 * i + 256]
            j = (u - U_DOWN)
            return w_dn[:, j:j + 2, :]

        def unit_dims(u):
            if u < U_Q or U_UP <= u < U_DOWN:
                return 8, 128
            if U_GLU <= u < U_OUT:
                return 4, 256
            if u >= U_DOWN:
                return 1, 1024
            return 2, 512

        def raw_unit(u):
            r = raw[:, u // 2 % 2, :]
            a, b = unit_dims(u)
            if b in (128, 256):
                v = r.rearrange("p (k n) -> p k n", k=a)
                return v[:, :, (u % 2) * b:(u % 2) * b + b]
            return r[:, (u % 2) * 1024:(u % 2) * 1024 + 1024].rearrange("p (k n) -> p k n", k=a)

        def w_unit(u, part):
            a, b = unit_dims(u)
            return wring[:, u % 4, part, :].rearrange("p (k n) -> p k n", k=a)

        def load_chunk(eng, c):
            if c >= 2:
                eng.wait_ge(hi_done, 2 * (c - 1))
                eng.wait_ge(lo_done, 2 * (c - 1))
            src = chunk_src(c)
            eng.dma_start(raw[:, c % 2, :].rearrange("p (k n) -> p k n", k=src.shape[1]), src)\
               .then_inc(raw_in[c % 2], 16)

        def unit_gain(u):
            if U_OA <= u < U_XQ:
                return COL["gnorm_attn"] + 2 * ((u - U_OA) % 2)
            if U_XQ <= u < U_XO:
                return COL["norm_xattn"] + 2 * (u - U_XQ)
            return None

        def split_hi(act, u):
            act.wait_ge(raw_in[u // 2 % 2], 16 * (u // 4 + 1))
            if u >= 4:
                wait_unit(act, u - 4)
            g = unit_gain(u)
            if g is None:
                ins = nc.scalar.activation(w_unit(u, 0), raw_unit(u), ACT.Copy)
            else:
                for k in range(2):
                    ins = nc.scalar.activation(w_unit(u, 0)[:, k, :], raw_unit(u)[:, k, :], ACT.Copy,
                                               scale=gcol[:, g + k:g + k + 1])
            ins.then_inc(hi_done, 1)

        def split_lo(dve, u):
            dve.wait_ge(hi_done, u + 1)
            g = unit_gain(u)
            if g is None:
                ins = nc.vector.tensor_tensor(w_unit(u, 1), raw_unit(u), w_unit(u, 0).bitcast(f32), ALU.subtract)
            else:
                for k in range(2):
                    ins = nc.vector.scalar_tensor_tensor(
                        out=w_unit(u, 1)[:, k, :], in0=raw_unit(u)[:, k, :], scalar=gcol[:, g + k:g + k + 1],
                        in1=w_unit(u, 0)[:, k, :].bitcast(f32), op0=ALU.mult, op1=ALU.subtract)
            ins.then_inc(lo_done, 1)

        def mm3(ps, lh, ll, rh, rl_, first, last):
            nc.tensor.matmul(ps, lh, rh, start=first, stop=False)
            nc.tensor.matmul(ps, lh, rl_, start=False, stop=False)
            return nc.tensor.matmul(ps, ll, rh, start=False, stop=last)

        EV = [("x", TT, D), ("mem", MT, D), ("q", TT * H, HD), ("k", TT * H, HD), ("mk", MT * XH, XD),
              ("ss", TT, DS), ("ya", TT, DS), ("x2", TT, D)]
        EV += [(f"qx{t}", XH, XD) for t in range(TT)] + [(f"x3{t}", 1, D) for t in range(TT)]
        EVN = {n: i for i, (n, _, _) in enumerate(EV)}
        EVC, at = {}, 0
        for n, k, _ in EV:
            EVC[n] = at
            at += k
        sq = sb("sq", [128, at])
        ms = sb("ms", [128, at])
        rs = sb("rs", [128, at])
        rt = sb("rt", [128, 2, 32])

        def ev(t, name):
            return t[:, EVC[name]:EVC[name] + EV[EVN[name]][1]]

        junk = qk[:, 0:2, :].rearrange("p a b -> p (a b)")
        junk_ya, junk_late = region(R0 + 11904, 512), region(R1, 1024)
        sqr_s5, sqr_late = region(R0 + 7936, 512), region(R0 + 7168, 512)
        ssr_ready, relb_ok, x2r_ready, xr_ready = sem("ssr_ready"), sem("relb_ok"), sem("x2r_ready"), sem("xr_ready")
        pow_ready, gffn_in, half_ok = sem("pow_ready"), sem("gffn_in"), sem("half_ok")
        mhalf = sb("mhalf", [128, 8])
        hbglu = sb("hbglu", [128, 4])
        glu_in, hb_ready = sem("glu_in"), sem("hb_ready")


        n_sq = [0]

        def row_square(act, event, t, row):
            if n_sq[0] > 0:
                act.wait_ge(sq_done, n_sq[0])
            n_sq[0] += 1
            c = EVC[event] + t
            to = {"x": junk, "me": junk, "ya": junk_ya}.get(event[0:2], junk_late)
            nc.scalar.activation(to[:, 0:row.shape[1]], row, ACT.Square, accum_out=sq[:, c:c + 1])\
                .then_inc(sq_done, 1)

        block = ctx.enter_context(nc.Block())

        @block.sync
        def _(sync):
            lam_rows = [A[n][0].rearrange("(a b) n -> a (b n)", b=2) for n in ("ssm_lam_re", "ssm_lam_im")]
            sync.dma_start(prow[:, 0, :], lam_rows[0]).then_inc(par_in, 16)
            sync.dma_start(prow[:, 1, :], lam_rows[1]).then_inc(par_in, 16)
            sync.dma_start(lsrow[:, :], A["ssm_log_step"][0].rearrange("(a b) -> a b", b=2)).then_inc(par_in, 16)
            sync.dma_start(nrow[:, :], A["norm_mix"][0].rearrange("(a n) -> a n", n=128)).then_inc(par_in, 16)
            for t in range(TT):
                sync.dma_start(xr[:, t, :], A["x"][0, t * 128:(t + 1) * 128, :]).then_inc(x_in[t], 16)
            load_chunk(sync, 0)
            load_chunk(sync, 1)
            for i, part in enumerate(("ssm_c_re", "ssm_c_im")):
                for half in range(2):
                    sync.dma_start(craw[:, i, :, half * NS:(half + 1) * NS],
                                   A[part][0].rearrange("(a g) c n -> (g c) a n", a=4)).then_inc(c_in, 16)
            sync.dma_start(relb[0:NB, :], A["rel_bias"]).then_inc(relb_in, 16)
            sync.dma_start(qk[0:NB + 1, 3, 0:384], A["buckets"]).then_inc(relb_in, 16)
            n_gain = 0
            for name, k in GAINS:
                r = COL[name]
                src = A[name][0]
                if name in ("attn_qn", "attn_kn"):
                    for i in range(2):
                        sync.dma_start(grow[r:r + 1, i * HD:(i + 1) * HD], src.rearrange("(a n) -> a n", a=1))\
                            .then_inc(gain_in, 16)
                        n_gain += 1
                else:
                    sync.dma_start(grow[r:r + k, :], src.rearrange("(a n) -> a n", n=128)).then_inc(gain_in, 16)
                    n_gain += 1
            assert n_gain == N_GAIN
            for t in range(MT):
                sync.dma_start(memr[:, t, :], A["mem"][0, t * 128:(t + 1) * 128, :]).then_inc(mem_in, 16)
            cw = A["ffn_conv_w"][0].rearrange("w o (a n) -> w (o a) n", n=128)
            sync.dma_start(crow[0:44, 0, :], cw[0]).then_inc(conv_in, 16)
            sync.dma_start(crow[44:88, 0, :], cw[1]).then_inc(conv_in, 16)
            sync.dma_start(crow[0:44, 1, :], cw[2]).then_inc(conv_in, 16)
            sync.dma_start(crow[44:88, 1, :], A["ffn_conv_b"][0].rearrange("(a n) -> a n", n=128)).then_inc(conv_in, 16)
            load_chunk(sync, 2)
            load_chunk(sync, 3)

            def u_write(q):
                after_drain(sync, f"u{q}")
                sync.dma_start(scr_u[q * 128:(q + 1) * 128].rearrange("p i k -> p (i k)"), uT[:, q, :]).then_inc(su_out, 16)

            def u_read():
                sync.wait_ge(su_out, 16 * NQ)
                after_drain(sync, "cm")
                v = scr_u.rearrange("(g c) i k -> i c g k", c=CG)
                for d in range(L):
                    sync.dma_start(ub[d * CG:(d + 1) * CG, :, :], v[L - 1 - d]).then_inc(u_in, 16)

            def t_load(q):
                after_drain(sync, f"ka{q}")
                after_drain(sync, f"kb{q}")
                if q == 0:
                    sync.wait_ge(zero_ok, 1)
                else:
                    after_drain(sync, f"yo{q - 1}")
                for d in range(L):
                    sync.dma_start(toep[d * CG:(d + 1) * CG, :, (L - 1 - d) * CG:],
                                   kt[0:CG, :, 0:(d + 1) * CG]).then_inc(t_in[q], 16)

            def y_back(q):
                after_drain(sync, f"yo{q}")
                sync.dma_start(scr_y[q].rearrange("p g k -> p (g k)"), yb).then_inc(sy_out[q], 16)
                sync.wait_ge(sy_out[q], 16)
                if q >= 1:
                    sync.wait_ge(zz_ready, q)
                v = scr_y[q].rearrange("(j c) g k -> g c j k", c=CG)
                for g in range(QG):
                    sync.dma_start(yst[g * CG:(g + 1) * CG, :].rearrange("p (j k) -> p j k", j=L), v[g])\
                        .then_inc(y_in[q], 16)

            for q in range(NQ):
                u_write(q)
            u_read()
            load_chunk(sync, 4)
            load_chunk(sync, 5)
            after_drain(sync, "relb")
            sync.dma_start(scr_b.rearrange("(p h y) -> h p y", p=128, h=H),
                           yst[0:H, 0:384].unsqueeze(1).to_broadcast([H, 128, 384])).then_inc(scr_out, 16)
            t_load(0)
            load_chunk(sync, 6)
            sync.wait_ge(scr_out, 16)
            y_back(0)
            t_load(1)
            load_chunk(sync, 7)
            load_chunk(sync, 8)
            y_back(1)
            t_load(2)
            load_chunk(sync, 9)
            y_back(2)
            t_load(3)
            load_chunk(sync, 10)
            sync.wait_ge(z_ready, NQ)
            skew = bass.AP(tensor=scr_b.tensor, offset=127,
                           ap=[[H * 384 - 1, 128], [384, H], [1, 256]])
            sync.dma_start(bias[:, :, 256:512], skew).then_inc(bias_in, 16)
            y_back(3)
            load_chunk(sync, 11)
            sync.wait_ge(zz_ready, NQ)
            for t in range(TT):
                sync.dma_start(hres[:, t, :], A["x"][0, t * 128:(t + 1) * 128, :]).then_inc(h_in, 16)
            for c in range(12, U_END // 2):
                load_chunk(sync, c)
                if c == U_XQ // 2 + 1:
                    sync.wait_ge(logit_ready, TT * H)
                    sync.dma_start(gffn, A["norm_ffn"].to_broadcast([128, D])).then_inc(gffn_in, 16)
            for t in range(TT):
                for half in range(2):
                    sync.wait_ge(res_ready, 2 * t + half + 1)
                    sync.dma_start(out[0, t * 128:(t + 1) * 128, half * 512:half * 512 + 512],
                                   hres[:, t, half * 512:half * 512 + 512]).then_inc(out_done, 16)
            sync.wait_ge(out_done, 16 * 2 * TT)

        @block.gpsimd
        def _(pool):
            n_step = [0]

            def link(ins):
                n_step[0] += 1
                ins.then_inc(pool_step, 1)
                pool.wait_ge(pool_step, n_step[0])

            def mul(o, a, b):
                return nc.gpsimd.tensor_tensor(o, a, b, ALU.mult)

            def cmul(o_re, o_im, a_re, a_im, b_re, b_im, t1, t2, sign=ALU.add):
                mul(t1, a_re, b_re)
                link(mul(t2, a_im, b_im))
                link(nc.gpsimd.tensor_tensor(o_re, t1, t2, ALU.subtract))
                mul(t1, a_re, b_im)
                link(mul(t2, a_im, b_re))
                return nc.gpsimd.tensor_tensor(o_im, t1, t2, sign)

            link(nc.gpsimd.memset(ident[:, :], 0.0))
            nc.gpsimd.affine_select(out=ident[:, :], in_=ident[:, :], compare_op=ALU.not_equal,
                                    fill=1.0, base=0, pattern=[[-1, 128]], channel_multiplier=1)\
                .then_inc(ident_ok, 1)
            for i, part in enumerate(("ssm_b_re", "ssm_b_im")):
                pool.dma_start(bmat[:, i], A[part][0].rearrange("(a b) n c -> (b n) a c", b=2)).then_inc(b_in, 16)
            nc.gpsimd.memset(toep[:, :, :], 0.0).then_inc(zero_ok, 1)
            nc.gpsimd.memset(pw[:, 0, :, 0:1], 1.0)
            nc.gpsimd.memset(pw[:, 1, :, 0:1], 0.0)
            nc.gpsimd.memset(ph[:, 0, :, 0:1], 1.0)
            link(nc.gpsimd.memset(ph[:, 1, :, 0:1], 0.0))

            def view(t, *dims):
                n = int(np.prod(dims))
                names = "abcd"[:len(dims)]
                return t[:, 0:n].rearrange(f"p ({' '.join(names)}) -> p {' '.join(names)}",
                                           **{k: d for k, d in zip(names, dims)})

            def powers(tab, top):
                m = 1
                while m < top:
                    k = min(m, top - m)
                    t1, t2 = view(ptmp[:, 0, :], GP, k), view(ptmp[:, 1, :], GP, k)
                    b = [tab[:, i, :, m:m + 1].to_broadcast([128, GP, k]) for i in range(2)]
                    link(cmul(tab[:, 0, :, m + 1:m + 1 + k], tab[:, 1, :, m + 1:m + 1 + k],
                              tab[:, 0, :, 1:1 + k], tab[:, 1, :, 1:1 + k], b[0], b[1], t1, t2))
                    m *= 2

            pool.wait_ge(par_ready, 1)
            pool.wait_ge(b_in, 32)
            t1, t2 = view(ptmp[:, 0, :], GP, CG), view(ptmp[:, 1, :], GP, CG)
            fb = [sp[:, i, :].unsqueeze(2).to_broadcast([128, GP, CG]) for i in (0, 1)]
            link(cmul(bb[:, 0], bb[:, 1], fb[0], fb[1], bmat[:, 0], bmat[:, 1], t1, t2))
            powers(pw, L)

            def quarter(q):
                g0 = q * QP
                if q >= 1:
                    bank, n = uses[f"w1i{q - 1}"]
                    pool.wait_ge(bank_full[bank], n + 1)
                shape = [128, QP, L, CG]
                t1, t2 = view(ptmp[:, 0, :], QP, L, CG), view(ptmp[:, 1, :], QP, L, CG)
                p = [pw[:, i, g0:g0 + QP, 0:L].unsqueeze(3).to_broadcast(shape) for i in range(2)]
                b = [bb[:, i, g0:g0 + QP, :].unsqueeze(2).to_broadcast(shape) for i in range(2)]
                o = [view(w1p[:, i, :], QP, L, CG) for i in range(2)]
                cmul(o[0], o[1], p[0], p[1], b[0], b[1], t1, t2).then_inc(w1p_ready, 1)
                pool.wait_ge(w1p_ready, q + 1)
                if q == 0:
                    after_drain(pool, "cr")
                    after_drain(pool, "cm")
                if q >= 2:
                    after_drain(pool, f"yo{q - 2}")
                shape = [128, QP, L + 1, CG]
                t1, t2 = view(ptmp[:, 0, :], QP, L + 1, CG), view(ptmp[:, 1, :], QP, L + 1, CG)
                p = [pw[:, i, g0:g0 + QP, :].unsqueeze(3).to_broadcast(shape) for i in range(2)]
                c_re, c_im, nc_re = [cmat[:, i, g0:g0 + QP, :].unsqueeze(2).to_broadcast(shape)
                                     for i in range(3)]
                o = [view(ca[:, q % 2, i, :], QP, L + 1, CG) for i in range(2)]
                mul(t1, c_re, p[0])
                link(mul(t2, c_im, p[1]))
                link(nc.gpsimd.tensor_tensor(o[0], t1, t2, ALU.subtract))
                mul(t1, nc_re, p[1])
                link(mul(t2, c_im, p[0]))
                nc.gpsimd.tensor_tensor(o[1], t1, t2, ALU.subtract).then_inc(ca_ready, 1)
                pool.wait_ge(ca_ready, q + 1)

            quarter(0)
            powers(ph, NC - 1)
            nc.gpsimd.memset(rt[:, 1, 31:32], 0.0).then_inc(ph_ready, 1)
            for q in range(1, NQ):
                quarter(q)

            nc.gpsimd.memset(mhalf[:, :], -0.5).then_inc(half_ok, 1)
            pool.wait_ge(half_ok, 1)
            after_drain(pool, "v3")
            for q in range(NQ):
                pool.wait_ge(gelu_ready, q + 1)
                link(nc.gpsimd.tensor_copy(xs[:, 0, 4 + q, :], uT[:, q, :]))
                nc.gpsimd.tensor_tensor(xs[:, 1, 4 + q, :], uT[:, q, :], xs[:, 0, 4 + q, :].bitcast(f32), ALU.subtract)\
                    .then_inc(glu_in, 1)
            for i in range(EVN["mk"], len(EV)):
                name, w, _ = EV[i]
                pool.wait_ge(ms_ready, i + 1)
                nc.gpsimd.tensor_tensor(ev(rs, name), ev(ms, name), mhalf[:, 0:w], ALU.pow).then_inc(pow_ready, 1)

        @block.scalar
        def _(act):
            n_step = [0]

            def link(ins):
                n_step[0] += 1
                ins.then_inc(act_step, 1)
                act.wait_ge(act_step, n_step[0])

            def A_(o, i, f, **k):
                return nc.scalar.activation(o, i, f, **k)

            def inv_root(name):
                act.wait_ge(ms_ready, EVN[name] + 1)
                if EVN[name] > 0:
                    act.wait_ge(rs_ready, EVN[name])
                w = EV[EVN[name]][1]
                link(A_(rt[:, 0, 0:w], ev(ms, name), ACT.Ln))
                A_(ev(rs, name), rt[:, 0, 0:w], ACT.Exp, scale=-0.5).then_inc(rs_ready, 1)

            def act_split(name, dst, gain=1.0):
                A_(dst, read(act, name)[:, :], ACT.Copy, scale=gain).then_inc(act_hi, 1)

            def col(name, i=0):
                return gcol[:, COL[name] + i:COL[name] + i + 1]


            def x_square(t):
                act.wait_ge(x_in[t], 16)
                row_square(act, "x", t, xr[:, t, :])

            after_drain(act, "lam")
            A_(sp[:, 2, :], lam[:, 2 * GP:3 * GP], ACT.Exp).then_inc(stp_ready, 1)
            x_square(0)
            act.wait_ge(sa_ready, 1)
            A_(sp[:, 5, :], sp[:, 3, :], ACT.Exp)
            A_(sp[:, 6, :], sp[:, 3, :], ACT.Exp, scale=float(L)).then_inc(mag_ready, 1)
            act.wait_ge(ang_ready, 1)
            A_(sp[:, 8, :], sp[:, 7, :], ACT.Sin)
            A_(sp[:, 10, :], sp[:, 9, :], ACT.Sin).then_inc(sin_ready, 1)
            for t in range(1, TT):
                x_square(t)
            for d in range(KD):
                act_split(f"x{d}", xs[:, 0, d, :], lam[:, 3 * GP + d:3 * GP + d + 1])
                if d == 3:
                    split_hi(act, 0)
            split_hi(act, 1)
            inv_root("x")
            split_hi(act, 2)
            split_hi(act, 3)
            p = read(act, "par")
            A_(gcol[:, :], p[:, 0:NG], ACT.Copy)
            drained(A_(ccol[:, :, :], p[:, 64:64 + 176].rearrange("p (a b) -> p a b", a=4), ACT.Copy), "par")
            for i, name in enumerate(("cr", "cm")):
                p = read(act, name)
                for half in range(2):
                    rows = slice(half * NS, (half + 1) * NS)
                    src = p[rows, :].rearrange("p (a b c) -> p a b c", b=2, c=CG)[:, :, half, :]
                    ins = A_(cmat[rows, i], src, ACT.Copy)
                    if i == 0:
                        ins = A_(cmat[rows, 2], src, ACT.Copy, scale=-1.0)
                drained(ins, name)
            p = read(act, "relb")
            drained(A_(yst[0:H, 0:384], p[0:H, 0:384], ACT.Copy), "relb")
            after_drain(act, "par")
            act.wait_ge(mem_in, 16 * MT)
            for t in range(MT):
                row_square(act, "mem", t, memr[:, t, :])
            inv_root("mem")
            for m in range(4):
                split_hi(act, U_Q + m)
            for i in range(4):
                p = read(act, f"m{i}")
                for j in range(2):
                    c = COL["norm_mem"] + 2 * i + j
                    A_(bs[:, 0, i * 512 + j * M:i * 512 + (j + 1) * M], p[:, j * M:(j + 1) * M], ACT.Copy,
                       scale=gcol[:, c:c + 1]).then_inc(act_hi, 1)

            def evac(name, dst, src=lambda p: p[:, :]):
                drained(A_(dst, src(read(act, name)), ACT.Copy), name)

            def weights_in(q):
                if q >= 2:
                    read(act, f"vi{q - 2}")
                evac(f"w1i{q}", w1[:, q % 2, 1, :])
                if q >= 1:
                    act.wait_ge(t_in[q - 1], 16 * L)
                for b, n in enumerate("ab"):
                    evac(f"k{n}{q}", kt[0:CG].rearrange("p (a b) n -> p a b n", b=2)[:, :, b, :],
                         lambda p: p[0:CG, :].rearrange("p (a n) -> p a n", a=QP))

            def y_out(q):
                if q >= 1:
                    act.wait_ge(sy_out[q - 1], 16)
                for b, n in enumerate("eo"):
                    drained(A_(yb.rearrange("p (a b k) -> p a b k", b=2, k=NC)[:, :, b, :],
                               read(act, f"y{n}{q}")[:, 0:QP * NC].rearrange("p (a k) -> p a k", a=QP), ACT.Copy),
                            f"y{n}{q}")

            def rows(name, dst):
                for t in range(TT):
                    c = EVC["x"] + t
                    drained(A_(dst[:, t, :], read(act, f"{name}{t}")[:, :], ACT.Copy, scale=rs[:, c:c + 1]), f"{name}{t}")

            split_hi(act, 8)
            split_hi(act, 9)
            weights_in(0)
            split_hi(act, 10)
            after_drain(act, "u3")
            rows("q", qk)
            split_hi(act, 11)
            weights_in(1)
            inv_root("q")
            split_hi(act, 12)
            y_out(0)
            split_hi(act, 13)
            weights_in(2)
            split_hi(act, 14)
            y_out(1)
            for t in range(TT):
                read(act, f"qt{t}")
            rows("k", qk)
            split_hi(act, 15)
            weights_in(3)
            inv_root("k")
            split_hi(act, 16)
            y_out(2)
            split_hi(act, 17)
            split_hi(act, 18)
            y_out(3)

            def gelu(q):
                act.wait_ge(zz_ready, q + 1)
                A_(uT[:, q, :], uT[:, q, :], ACT.Gelu_apprx_tanh).then_inc(gelu_ready, 1)

            for q in range(3):
                gelu(q)
            rows("v", vrow)
            split_hi(act, 19)

            def tile_hi(name, dst):
                A_(dst, read(act, name)[:, :].rearrange("p (a n) -> p a n", a=4), ACT.Copy).then_inc(act_hi, 1)

            def ya_hi(t):
                tile_hi(f"ya{t}", xs[:, 0, 4:8, t * 128:(t + 1) * 128])

            def ya_square(t):
                after_drain(act, f"pv{t}")
                row_square(act, "ya", t, yrow[:, t, :])

            for s in range(TT * H):
                n = (s // H + 1) * 128
                if s >= 2:
                    read(act, f"pt{s - 2}")
                p = read(act, f"sc{s}")
                act.wait_ge(logit_ready, s + 1)
                drained(A_(pbuf[:, s % 2, 0:n], p[:, 0:n], ACT.Exp, scale=-1.0, bias=nmx[:, s:s + 1],
                           accum_out=lsum[:, s:s + 1]), f"sc{s}")
                if s % 2 == 1:
                    pt_evac(act, lambda o, i: A_(o, i, ACT.Copy), s - 1)
                if s in SPLIT_AT:
                    split_hi(act, SPLIT_AT[s])
                if s == 5:
                    gelu(3)
                if s == 4:
                    evac("mk0", mkrow[:, 0, :])
                    evac("mk1", mkrow[:, 1, :])
                if s - 1 in GLU_AT:
                    m = GLU_AT.index(s - 1)
                    drained(A_(sg[:, m, :], read(act, f"z{m}")[:, :], ACT.Tanh, scale=0.5, bias=hbglu[:, m:m + 1]), f"z{m}")
                if s - 3 in GLU_AT:
                    c = GLU_AT.index(s - 3)
                    act.wait_ge(y2_ready, c + 1)
                    A_(sg[:, c, :], uT[:, c, :], ACT.Square).then_inc(ysq_ready, 1)
                if s in YA_AT:
                    ya_square(YA_AT.index(s))
                if s - 1 in YA_AT:
                    ya_hi(YA_AT.index(s - 1))
                if s == 9:
                    evac("mv0", xv[:, 0, :])
                    evac("mv1", xv[:, 1, :])
                if s == 18:
                    for i in range(2):
                        drained(A_(kxT[:, 2 * i:2 * i + 2, :].rearrange("p h m -> p (h m)"), read(act, f"kx{i}")[:, :],
                                   ACT.Copy, scale=gcol[:, COL["x_kn"]:COL["x_kn"] + 1]), f"kx{i}")
                if s in (21, 22):
                    for c in (2 * (s - 21), 2 * (s - 21) + 1):
                        act.wait_ge(y3_ready, c + 1)
                        g = COL["gnorm_ssm"] + c
                        A_(to_tokens(xs[:, 0, c, :]), uT[:, c, :].rearrange("p (i k) -> p i k", i=L),
                           ACT.Copy, scale=gcol[:, g:g + 1]).then_inc(act_hi, 1)
            ya_square(TT - 1)
            ya_hi(TT - 1)
            split_hi(act, 31)
            split_hi(act, 32)
            split_hi(act, 33)

            def x_hi(name, t):
                for half in range(2):
                    tile_hi(f"{name}{t}{half}", xs[:, 0, 4 * half:4 * half + 4, t * 128:(t + 1) * 128])

            def h_square(name, last_add, event, i, t):
                after_drain(act, f"{last_add}{t}1")
                row_square(act, event, i, hres[:, t, :])

            for t in range(TT):
                if t == TT - 1:
                    split_hi(act, U_XQ)
                    split_hi(act, U_XQ + 1)
                h_square("x2", "o", "x2", t, t)
                if t >= 1:
                    x_hi("x2", t - 1)
            split_hi(act, U_XQ + 2)
            split_hi(act, U_XQ + 3)
            x_hi("x2", TT - 1)
            act.wait_ge(x2r_ready, 1)

            def qx_rows(t):
                c = EVC["x2"] + t
                drained(A_(qk[:, t, :], read(act, f"qx{t}")[:, :], ACT.Copy, scale=rs[:, c:c + 1]), f"qx{t}")

            def xo_hi(t):
                tile_hi(f"xo{t}", bs[:, 0, :].rearrange("p (a n) -> p a n", a=4)[:, :, t * 128:(t + 1) * 128])

            qx_rows(0)
            qx_rows(1)
            for s in range(TT * XH):
                if s >= 2:
                    read(act, f"xp{s - 2}")
                p = read(act, f"xs{s}")
                act.wait_ge(logit_ready, TT * H + s + 1)
                drained(A_(pbuf[:, s % 2, 0:M], p[:, 0:M], ACT.Exp, bias=nmx[:, 32 + s:33 + s],
                           accum_out=lsum[:, 32 + s:33 + s]), f"xs{s}")
                if s % 2 == 1:
                    xp_evac(act, lambda o, i: A_(o, i, ACT.Copy), s - 1)
                if s in (4, 8):
                    qx_rows(1 + s // 4)
                if 6 <= s < 10:
                    split_hi(act, U_XO + s - 6)
                if s in (7, 11, 15):
                    xo_hi((s - 7) // 4)
                if s == 13:
                    h_square("x3", "w", "x30", 0, 0)
            h_square("x3", "w", "x31", 0, 1)
            xo_hi(TT - 1)
            x_hi("x3", 0)
            x_hi("x3", 1)
            h_square("x3", "w", "x32", 0, 2)
            for i in range(4):
                split_hi(act, U_UP + i)
            h_square("x3", "w", "x33", 0, 3)
            x_hi("x3", 2)
            x_hi("x3", 3)
            for i in range(FT // 2):
                for j in range(4):
                    k = 4 * i + j
                    tile = 2 * i + j if j < 2 else FT + 2 * i + j - 2
                    p = read(act, f"f{k}")
                    if i >= 1:
                        act.wait_ge(hff_ready, 2 * i - 1 + j % 2)
                    A_(cv[:, j, :], p[:, :], ACT.Identity, scale=ccol[:, 2, tile:tile + 1],
                       bias=ccol[:, 3, tile:tile + 1]).then_inc(conv_ready, 1)
                    split_hi(act, U_UP + k + 4)
                    if j < 2:
                        after_drain(act, f"f{k}")
                        A_(cv[:, j, :], cv[:, j, :], ACT.Silu).then_inc(gate_ready, 1)
            for n in range(FT):
                act.wait_ge(hff_ready, n + 1)
                if n >= 4:
                    wait_unit(act, U_DOWN + n - 4)
                A_(bs[:, 0, n % 4 * 512:n % 4 * 512 + 512], hff[:, n, :], ACT.Copy).then_inc(act_hi, 1)
                if n >= 1 and U_DOWN + n + 3 < U_END:
                    split_hi(act, U_DOWN + n + 3)

        @block.vector
        def _(dve):
            n_step, n_hi = [0], [0]

            def link(ins):
                n_step[0] += 1
                ins.then_inc(dve_step, 1)
                dve.wait_ge(dve_step, n_step[0])

            V = nc.vector

            def tt(o, a, b, op):
                return V.tensor_tensor(o, a, b, op)

            def ts(o, a, s1, s2, o1, o2):
                return V.tensor_scalar(o, a, s1, s2, o1, o2)

            def stt(o, a, s1, b, o1, o2):
                return V.scalar_tensor_tensor(out=o, in0=a, scalar=s1, in1=b, op0=o1, op1=o2)

            def lo_of(src, hi, lo, g=1.0):
                n_hi[0] += 1
                dve.wait_ge(act_hi, n_hi[0])
                return stt(lo, src, g, hi.bitcast(f32), ALU.mult, ALU.subtract)

            def mean_sq(name):
                n = EV[EVN[name]][2]
                ts(ev(ms, name), ev(sq, name), 1.0 / n, EPS, ALU.mult, ALU.add).then_inc(ms_ready, 1)

            def root(name, ready=None):
                w = EV[EVN[name]][1]
                if EVN[name] < EVN["mk"]:
                    dve.wait_ge(rs_ready, EVN[name] + 1)
                else:
                    dve.wait_ge(pow_ready, EVN[name] - EVN["mk"] + 1)
                r, t = ev(rs, name), rt[:, 1, 0:w]
                link(tt(t, r, r, ALU.mult))
                link(tt(t, t, ev(ms, name), ALU.mult))
                link(ts(t, t, -0.5, 1.5, ALU.mult, ALU.add))
                last = tt(r, r, t, ALU.mult)
                if ready is None:
                    link(last)
                else:
                    last.then_inc(ready, 1)

            def scale_rows(name, dst, src, tiles):
                for t in range(tiles):
                    c = EVC[name] + t
                    V.tensor_scalar_mul(dst[:, t, :], src[:, t, :], rs[:, c:c + 1]).then_inc(xn_ready, 1)

            def head_event(name, src, tiles, heads, pre):
                for t in tiles:
                    after_drain(dve, f"{pre}{t}")
                    sqr = sqr_s5 if name in "qk" else sqr_late
                    at = t - tiles[0]
                    link(tt(sqr, src[:, t, :], src[:, t, :], ALU.mult))
                    c = EVC[name] + at * heads
                    link(V.reduce_sum(sq[:, c:c + heads], sqr.rearrange("p (h n) -> p h n", h=heads), AX.X))
                mean_sq(name)

            def head_rows(name, src, tiles, heads, width):
                root(name)
                for t in tiles:
                    c = EVC[name] + (t - tiles[0]) * heads
                    v = src[:, t, :].rearrange("p (h n) -> p h n", h=heads)
                    tt(v, v, rs[:, c:c + heads].unsqueeze(2).to_broadcast([128, heads, width]), ALU.mult)\
                        .then_inc(xn_ready, 1)

            V.memset(ones[:, :], 1.0).then_inc(ones_ok, 1)
            V.memset(relb[NB:NB + 1, :], NEG).then_inc(relb_ok, 1)
            dve.wait_ge(par_in, 64)
            V.tensor_copy(prow[:, 2, :].rearrange("p (b n) -> p b n", b=2),
                          lsrow[:, :].unsqueeze(2).to_broadcast([GP, 2, NS])).then_inc(step_row, 1)
            p = read(dve, "lam")
            drained(V.tensor_copy(lam[:, :], p[:, 0:3 * GP + KD]), "lam")
            after_drain(dve, "lam")
            c = lambda i: sp[:, i, :]
            dve.wait_ge(stp_ready, 1)
            link(V.tensor_scalar_min(c(11), lam[:, 0:GP], -1e-4))
            tt(c(3), c(11), c(2), ALU.mult).then_inc(sa_ready, 1)
            link(tt(c(4), lam[:, GP:2 * GP], c(2), ALU.mult))
            MAGIC = 12582912.0
            C1 = 6.28125
            C2 = round((2 * math.pi - C1) * 2 ** 22) / 2 ** 22
            C3 = 2 * math.pi - C1 - C2
            TOP = 3.141592
            link(ts(c(12), c(4), 1 / (2 * math.pi), MAGIC, ALU.mult, ALU.add))
            link(V.tensor_scalar_sub(c(12), c(12), MAGIC))
            link(stt(c(7), c(12), -C1, c(4), ALU.mult, ALU.add))
            link(stt(c(7), c(12), -C2, c(7), ALU.mult, ALU.add))
            link(stt(c(7), c(12), -C3, c(7), ALU.mult, ALU.add))
            link(ts(c(7), c(7), TOP, -TOP, ALU.min, ALU.max))
            link(V.tensor_scalar_mul(c(13), c(7), -1.0))
            link(tt(c(13), c(13), c(7), ALU.max))
            ts(c(9), c(13), -1.0, math.pi / 2, ALU.mult, ALU.add).then_inc(ang_ready, 1)
            dve.wait_ge(sin_ready, 1)
            dve.wait_ge(mag_ready, 1)
            tt(pw[:, 0, :, 1], c(5), c(10), ALU.mult)
            tt(pw[:, 1, :, 1], c(5), c(8), ALU.mult)
            tt(c(12), c(11), c(11), ALU.mult)
            link(tt(c(13), lam[:, GP:2 * GP], lam[:, GP:2 * GP], ALU.mult))
            link(tt(c(12), c(12), c(13), ALU.add))
            link(V.reciprocal(c(12), c(12)))
            link(V.tensor_scalar_add(c(14), pw[:, 0, :, 1], -1.0))
            tt(c(15), c(14), c(11), ALU.mult)
            tt(c(16), pw[:, 1, :, 1], lam[:, GP:2 * GP], ALU.mult)
            tt(c(17), pw[:, 1, :, 1], c(11), ALU.mult)
            link(tt(c(18), c(14), lam[:, GP:2 * GP], ALU.mult))
            tt(c(15), c(15), c(16), ALU.add)
            link(tt(c(17), c(17), c(18), ALU.subtract))
            tt(c(0), c(15), c(12), ALU.mult)
            link(tt(c(1), c(17), c(12), ALU.mult))
            a_, b_ = c(10), c(8)
            for i in range(3):
                n0, n1 = (ph[:, 0, :, 1], ph[:, 1, :, 1]) if i == 2 else (c(19 + 2 * i), c(20 + 2 * i))
                tt(c(14), a_, a_, ALU.mult)
                tt(c(15), b_, b_, ALU.mult)
                link(tt(c(16), a_, b_, ALU.mult))
                tt(n0, c(14), c(15), ALU.subtract)
                last = V.tensor_scalar_mul(n1, c(16), 2.0)
                if i < 2:
                    link(last)
                else:
                    last.then_inc(par_ready, 1)
                a_, b_ = n0, n1
            for d in range(KD):
                g = lam[:, 3 * GP + d:3 * GP + d + 1]
                p = read(dve, f"x{d}")
                drained(lo_of(p[:, :], xs[:, 0, d, :], xs[:, 1, d, :], g), f"x{d}")
                if d == 3:
                    split_lo(dve, 0)
            split_lo(dve, 1)
            dve.wait_ge(sq_done, TT)
            mean_sq("x")
            root("x", xr_ready)
            split_lo(dve, 2)
            p = read(dve, "xb")
            drained(V.tensor_copy(xbc, p[:, :]), "xb")
            after_drain(dve, "xb")
            by_step = lambda a: a.rearrange("p (k i) -> p i k", i=L)

            def u_evac(m):
                p = read(dve, f"u{m}")
                drained(tt(uT[:, m, :].rearrange("p (i k) -> p i k", i=L), by_step(p[:, :]), by_step(xbc), ALU.mult),
                        f"u{m}")

            u_evac(0)
            split_lo(dve, 3)
            u_evac(1)
            after_drain(dve, "par")
            dve.wait_ge(sq_done, TT + MT)
            mean_sq("mem")
            root("mem")
            scale_rows("mem", memr, memr, MT)
            b = COL["ssm_b_glu"]
            V.tensor_scalar_mul(hbglu[:, :], gcol[:, b:b + 4], 0.5).then_inc(hb_ready, 1)
            for m in range(4):
                split_lo(dve, U_Q + m)
                if m in (0, 1):
                    u_evac(2 + m)
            for i in range(4):
                p = read(dve, f"m{i}")
                dve.wait_ge(act_hi, n_hi[0] + 2)
                for j in range(2):
                    cc = COL["norm_mem"] + 2 * i + j
                    at = slice(i * 512 + j * M, i * 512 + (j + 1) * M)
                    ins = lo_of(p[:, j * M:(j + 1) * M], bs[:, 0, at], bs[:, 1, at], gcol[:, cc:cc + 1])
                drained(ins, f"m{i}")

            def weights_in(q):
                if q >= 2:
                    read(dve, f"vr{q - 2}")
                drained(V.tensor_copy(w1[:, q % 2, 0, :], read(dve, f"w1r{q}")[:, :]), f"w1r{q}")

            def scan(q):
                if q == 0:
                    dve.wait_ge(ph_ready, 1)
                else:
                    dve.wait_ge(z_ready, q)
                if q >= 1:
                    read(dve, f"yo{q - 1}")
                vr = read(dve, f"vr{q}")[:, 0:QP * NC].rearrange("p (g k) -> p g k", g=QP)
                vi = read(dve, f"vi{q}")[:, 0:QP * NC].rearrange("p (g k) -> p g k", g=QP)
                co, si = (ph[:, i, q * QP:(q + 1) * QP, :] for i in range(2))
                t = [dtmp[:, i] for i in range(4)]
                zr, zi = zb[:, 0], zb[:, 1]
                tt(t[0], vr, co, ALU.mult)
                drained(tt(t[3], vr, si, ALU.mult), f"vr{q}")
                tt(t[1], vi, si, ALU.mult)
                drained(tt(t[2], vi, co, ALU.mult), f"vi{q}")
                after_drain(dve, f"vr{q}")
                after_drain(dve, f"vi{q}")
                tt(zr, t[0], t[1], ALU.add)
                link(tt(zi, t[2], t[3], ALU.subtract))
                for g in range(QP):
                    decay = sp[:, 6, q * QP + g:q * QP + g + 1].to_broadcast([128, NC])
                    V.tensor_tensor_scan(t[0][:, g, :], decay, zr[:, g, :], 0.0, ALU.mult, ALU.add)
                    last = V.tensor_tensor_scan(t[1][:, g, :], decay, zi[:, g, :], 0.0, ALU.mult, ALU.add)
                link(last)
                tt(t[2], t[0], co, ALU.mult)
                link(tt(t[3], t[1], si, ALU.mult))
                link(tt(zr, t[2], t[3], ALU.subtract))
                tt(t[2], t[0], si, ALU.mult)
                link(tt(t[3], t[1], co, ALU.mult))
                tt(zi, t[2], t[3], ALU.add).then_inc(z_ready, 1)

            def skip_in(q):
                dve.wait_ge(y_in[q], 16 * QG)
                g = gcol[:, COL["ssm_d"] + q:COL["ssm_d"] + q + 1]
                stt(uT[:, q, :], uT[:, q, :], g, yst, ALU.mult, ALU.add).then_inc(zz_ready, 1)

            def transposed(pre, dst, gain, scale, tiles=range(TT)):
                for t in tiles:
                    p = read(dve, f"{pre}{t}")
                    drained(ts(dst[:, :, t * 128:(t + 1) * 128], p[:, :].rearrange("p (a b) -> p a b", a=4),
                               gcol[:, COL[gain]:COL[gain] + 1], scale, ALU.mult, ALU.mult), f"{pre}{t}")

            split_lo(dve, 8)
            split_lo(dve, 9)
            weights_in(0)
            split_lo(dve, 10)
            scan(0)
            head_event("q", qk, range(TT), H, "q")
            split_lo(dve, 11)
            weights_in(1)
            head_rows("q", qk, range(TT), H, HD)
            split_lo(dve, 12)
            scan(1)
            split_lo(dve, 13)
            transposed("qt", qT, "attn_qn", HD ** -0.5)
            weights_in(2)
            skip_in(0)
            split_lo(dve, 14)
            scan(2)
            head_event("k", qk, range(TT), H, "k")
            split_lo(dve, 15)
            weights_in(3)
            head_rows("k", qk, range(TT), H, HD)
            skip_in(1)
            split_lo(dve, 16)
            scan(3)
            split_lo(dve, 17)
            transposed("kt", kT, "attn_kn", 1.0)
            skip_in(2)
            split_lo(dve, 18)
            V.memset(bias[:, :, 0:256], 0.0).then_inc(far_zero, 1)
            split_lo(dve, 19)
            dve.wait_ge(far_zero, 1)
            dve.wait_ge(bias_in, 16)

            def normalise(bank, l0, heads, width, t):
                p = read(dve, bank)
                link(V.reciprocal(rl[:, 0:heads], lsum[:, l0:l0 + heads]))
                drained(tt(yrow[:, t, :].rearrange("p (h n) -> p h n", h=heads),
                           p[:, :].rearrange("p (h n) -> p h n", h=heads),
                           rl[:, 0:heads].unsqueeze(2).to_broadcast([128, heads, width]), ALU.mult), bank)
                after_drain(dve, bank)

            def tile_lo(name, hi, lo, last=True):
                ins = lo_of(read(dve, name)[:, :].rearrange("p (a n) -> p a n", a=4), hi, lo)
                drained(ins, name)

            def ya_lo(t):
                at = slice(t * 128, (t + 1) * 128)
                tile_lo(f"ya{t}", xs[:, 0, 4:8, at], xs[:, 1, 4:8, at])

            def residual(name, t, half, factor=1.0):
                o = hres[:, t, half * 512:(half + 1) * 512]
                drained(stt(o, read(dve, name)[:, :], factor, o, ALU.mult, ALU.add), name)

            for s in range(TT * H):
                h, n = s % H, (s // H + 1) * 128
                p = read(dve, f"sc{s}")
                V.tensor_tensor_reduce(out=p[:, 0:n], in0=p[:, 0:n], in1=bias[:, h, 512 - n:512], scale=-1.0,
                                       scalar=3.0e38, op0=ALU.add, op1=ALU.min,
                                       accum_out=nmx[:, s:s + 1]).then_inc(logit_ready, 1)
                if s in (9, 17, 25):
                    qd = (s - 9) // 8
                    normalise(f"pv{qd}", H * qd, H, HD, qd)
                if s >= 2 and s % 2 == 0:
                    pt_evac(dve, V.tensor_copy, s - 1)
                if s in SPLIT_AT:
                    split_lo(dve, SPLIT_AT[s])
                if s == 4:
                    skip_in(3)
                if s == 8:
                    head_event("mk", mkrow, range(MT), XH, "mk")
                if s == 10:
                    head_rows("mk", mkrow, range(MT), XH, XD)
                if s - 1 in YA_AT:
                    ya_lo(YA_AT.index(s - 1))
                if s - 2 in GLU_AT:
                    m = GLU_AT.index(s - 2)
                    after_drain(dve, f"z{m}")
                    link(ts(sg[:, m, :], sg[:, m, :], 0.5, 0.5, ALU.mult, ALU.add))
                    tt(uT[:, m, :], uT[:, m, :], sg[:, m, :], ALU.mult).then_inc(y2_ready, 1)
                if s == 17:
                    p = read(dve, "ss")
                    drained(V.tensor_copy(ev(sq, "ss"), p[:, 0:TT]), "ss")
                    after_drain(dve, "ss")
                    mean_sq("ss")
                if s == 18:
                    root("ss", ssr_ready)
                if s in (20, 21):
                    p = read(dve, "bc")
                    for cc in (2 * (s - 20), 2 * (s - 20) + 1):
                        tt(uT[:, cc, :], uT[:, cc, :], p[:, :], ALU.mult).then_inc(y3_ready, 1)
                if s in (22, 23):
                    for cc in (2 * (s - 22), 2 * (s - 22) + 1):
                        g = gcol[:, COL["gnorm_ssm"] + cc:COL["gnorm_ssm"] + cc + 1]
                        dve.wait_ge(y3_ready, cc + 1)
                        ins = lo_of(uT[:, cc, :].rearrange("p (i k) -> p i k", i=L), to_tokens(xs[:, 0, cc, :]),
                                    to_tokens(xs[:, 1, cc, :]), g)
                        if cc == 3:
                            drained(ins, "bc")
                if s == 23:
                    dve.wait_ge(h_in, 16 * TT)
                for n in range(2 * TT):
                    if s == SOUT_AT[2 * n + 1] + 1:
                        residual(f"g{n // 2}{n % 2}", n // 2, n % 2)
            pt_evac(dve, V.tensor_copy, TT * H - 1)
            normalise(f"pv{TT - 1}", H * (TT - 1), H, HD, TT - 1)
            ya_lo(TT - 1)
            split_lo(dve, 31)
            split_lo(dve, 32)
            split_lo(dve, 33)
            residual("g31", TT - 1, 1)
            dve.wait_ge(sq_done, TT + MT + TT)
            mean_sq("ya")
            root("ya")

            def x_lo(name, t):
                for half in range(2):
                    at = (slice(4 * half, 4 * half + 4), slice(t * 128, (t + 1) * 128))
                    tile_lo(f"{name}{t}{half}", xs[:, 0, at[0], at[1]], xs[:, 1, at[0], at[1]])

            for half in range(2):
                for t in range(TT):
                    after_drain(dve, f"g{t}{half}")
            for t in range(TT):
                for half in range(2):
                    c = EVC["ya"] + t
                    if t == TT - 1:
                        split_lo(dve, U_XQ + half)
                    residual(f"o{t}{half}", t, half, rs[:, c:c + 1])
                if t >= 1:
                    x_lo("x2", t - 1)
            split_lo(dve, U_XQ + 2)
            dve.wait_ge(sq_done, TT + MT + TT + TT)
            mean_sq("x2")
            split_lo(dve, U_XQ + 3)
            x_lo("x2", TT - 1)
            root("x2", x2r_ready)

            def qx_event(t):
                head_event(f"qx{t}", qk, [t], XH, "qx")

            def qx_rows(t):
                head_rows(f"qx{t}", qk, [t], XH, XD)

            def xo_lo(t):
                v = [bs[:, i, :].rearrange("p (a n) -> p a n", a=4)[:, :, t * 128:(t + 1) * 128] for i in range(2)]
                tile_lo(f"xo{t}", v[0], v[1])

            def w_residual(t):
                for half in range(2):
                    if t == 0:
                        after_drain(dve, f"o{t}{half}")
                    residual(f"w{t}{half}", t, half)

            def x3_mean(t):
                dve.wait_ge(sq_done, 3 * TT + MT + t + 1)
                mean_sq(f"x3{t}")

            def x3_rows(t):
                root(f"x3{t}")
                if t == 0:
                    dve.wait_ge(gffn_in, 16)
                c = EVC[f"x3{t}"]
                stt(x3row[:, t % 2, :], hres[:, t, :], rs[:, c:c + 1], gffn, ALU.mult, ALU.mult).then_inc(xn_ready, 1)

            qx_event(0)
            qx_rows(0)
            qx_event(1)
            transposed("qxt", qT, "x_qn", XD ** -0.5, [0])
            qx_rows(1)
            for s in range(TT * XH):
                p = read(dve, f"xs{s}")
                V.tensor_reduce(nmx[:, 32 + s:33 + s], p[:, 0:M], AX.X, ALU.max, negate=True)\
                    .then_inc(logit_ready, 1)
                if s in (5, 9, 13):
                    t = (s - 5) // 4
                    normalise(f"xpv{t}", 32 + XH * t, XH, XD, t)
                if s >= 2 and s % 2 == 0:
                    xp_evac(dve, V.tensor_copy, s - 1)
                if s == 2:
                    transposed("qxt", qT, "x_qn", XD ** -0.5, [1])
                if s in (4, 8):
                    qx_event(1 + s // 4)
                if s in (5, 9):
                    qx_rows(1 + s // 4)
                if s in (6, 10):
                    transposed("qxt", qT, "x_qn", XD ** -0.5, [1 + s // 4])
                if 6 <= s < 10:
                    split_lo(dve, U_XO + s - 6)
                if s in (7, 11, 15):
                    xo_lo((s - 7) // 4)
                if s == 13:
                    w_residual(0)
                if s == 14:
                    x3_mean(0)
                if s == 15:
                    x3_rows(0)
            xp_evac(dve, V.tensor_copy, TT * XH - 1)
            normalise(f"xpv{TT - 1}", 32 + XH * (TT - 1), XH, XD, TT - 1)
            w_residual(1)
            x3_mean(1)
            xo_lo(TT - 1)
            x3_rows(1)
            x_lo("x3", 0)
            w_residual(2)
            x3_mean(2)
            x_lo("x3", 1)
            x3_rows(2)
            for i in range(4):
                split_lo(dve, U_UP + i)
            w_residual(3)
            x3_mean(3)
            x3_rows(3)
            x_lo("x3", 2)
            x_lo("x3", 3)
            for i in range(FT // 2):
                for j in range(4):
                    k = 4 * i + j
                    tile = 2 * i + j if j < 2 else FT + 2 * i + j - 2
                    p = read(dve, f"f{k}")
                    dve.wait_ge(conv_ready, k + 1)
                    o = cv[:, j, :]
                    link(stt(o[:, 1:], p[:, 0:T - 1], ccol[:, 1, tile:tile + 1], o[:, 1:], ALU.mult, ALU.add))
                    drained(stt(o[:, 2:], p[:, 0:T - 2], ccol[:, 0, tile:tile + 1], o[:, 2:], ALU.mult, ALU.add), f"f{k}")
                    split_lo(dve, U_UP + k + 4)
                    if j >= 2:
                        after_drain(dve, f"f{k}")
                        dve.wait_ge(gate_ready, 2 * i + j - 1)
                        tt(hff[:, 2 * i + j - 2, :], cv[:, j - 2, :], o, ALU.mult).then_inc(hff_ready, 1)
            for n in range(FT):
                at = slice(n % 4 * 512, n % 4 * 512 + 512)
                lo_of(hff[:, n, :], bs[:, 0, at], bs[:, 1, at]).then_inc(act_lo, 1)
                if n >= 1 and U_DOWN + n + 3 < U_END:
                    split_lo(dve, U_DOWN + n + 3)
            for b in range(8):
                t, half = b // 2, b % 2
                o = hres[:, t, half * 512:(half + 1) * 512]
                tt(o, o, read(dve, f"d{b}")[:, :], ALU.add).then_inc(res_ready, 1)

        @block.tensor
        def _(pe):
            def mm(o, l, r, start=True, stop=True):
                return nc.tensor.matmul(o, l, r, start=start, stop=stop)

            def tr(o, i):
                return nc.tensor.transpose(o, i, ident[0:i.shape[0], 0:i.shape[0]])

            def used(ins, u):
                if u in DONE:
                    filled(ins, DONE[u])
                else:
                    ins.then_inc(unit_used, 1)

            def cols_unit(u, kts, xhi, bank_names):
                pe.wait_ge(lo_done, u + 1)
                wh, wl = w_unit(u, 0), w_unit(u, 1)
                for i, name in enumerate(bank_names):
                    p = fill(pe, name)
                    for k in range(kts):
                        at = slice(i * 128, (i + 1) * 128)
                        last = mm3(p[:, :], wh[:, k, at], wl[:, k, at], xhi(0, k), xhi(1, k), k == 0, k == kts - 1)
                    filled(last, name)

            def rows_unit(u, u0, units, act_tile, tiles, names):
                pe.wait_ge(lo_done, u + 1)
                j = u - u0
                for t in range(tiles):
                    if j == 0:
                        fill(pe, names[t])
                    p = pb[uses[names[t]][0]]
                    for k in range(2):
                        kk = 2 * j + k
                        last = mm3(p[:, :], act_tile(0, kk, t), act_tile(1, kk, t), w_unit(u, 0)[:, k, :],
                                   w_unit(u, 1)[:, k, :], kk == 0, kk == 2 * units - 1)
                    if j == units - 1:
                        filled(last, names[t])
                if j < units - 1:
                    last.then_inc(unit_used, 1)

            x_tile = lambda part, k, t: xs[:, part, k, t * 128:(t + 1) * 128]
            m_tile = lambda part, k, t: bs[:, part, k * M + t * 128:k * M + (t + 1) * 128]
            o_tile = lambda part, k, t: bs[:, part, k * 512 + t * 128:k * 512 + (t + 1) * 128]
            names = lambda pre, n: [f"{pre}{t}" for t in range(n)]

            def proj(u, u0, pre):
                rows_unit(u, u0, 4, x_tile, TT, names(pre, TT))

            pe.wait_ge(ident_ok, 1)
            pe.wait_ge(par_in, 64)
            pe.wait_ge(step_row, 1)
            p = fill(pe, "lam")
            for i in range(3):
                tr(p[:, i * GP:(i + 1) * GP], prow[:, i, :])
            filled(tr(p[:, 3 * GP:3 * GP + KD], nrow[:, :]), "lam")
            for t in range(TT):
                pe.wait_ge(x_in[t], 16)
                for d in range(KD):
                    p = fill(pe, f"x{d}") if t == 0 else pb[d]
                    last = tr(p[:, t * 128:(t + 1) * 128], xr[:, t, d * 128:(d + 1) * 128])
                    if t == TT - 1:
                        filled(last, f"x{d}")
            pe.wait_ge(lo_done, 1)
            p = fill(pe, "u0")
            for d in range(KD):
                after_drain(pe, f"x{d}")
                last = mm3(p[:, :], w_unit(0, 0)[:, d, :], w_unit(0, 1)[:, d, :], xs[:, 0, d, :], xs[:, 1, d, :],
                           d == 0, d == KD - 1)
            filled(last, "u0")

            def u_unit(m):
                cols_unit(U_SSM + m, KD, lambda part, k: xs[:, part, k, :], [f"u{m}"])

            def token_factors(name, event):
                p = fill(pe, name)
                for t in range(TT):
                    cc = EVC[event] + t
                    last = mm(p[:, t * 128:(t + 1) * 128], rs[:, cc:cc + 1].to_broadcast([128, 128]), ident[:, :])
                filled(last, name)

            u_unit(1)
            pe.wait_ge(xr_ready, 1)
            token_factors("xb", "x")
            pe.wait_ge(gain_in, 16 * N_GAIN)
            pe.wait_ge(conv_in, 16 * 4)
            p = fill(pe, "par")
            tr(p[:, 0:NG], grow[:, :])
            tr(p[:, 64:152], crow[:, 0, :])
            filled(tr(p[:, 152:240], crow[:, 1, :]), "par")
            pe.wait_ge(c_in, 16 * 4)
            for i, name in enumerate(("cr", "cm")):
                p = fill(pe, name)
                for a in range(4):
                    last = tr(p[:, a * 128:(a + 1) * 128], craw[:, i, a, :])
                filled(last, name)
            pe.wait_ge(relb_in, 32)
            pe.wait_ge(relb_ok, 1)
            p = fill(pe, "relb")
            filled(mm(p[0:H, 0:384], relb[:, :], qk[0:NB + 1, 3, 0:384]), "relb")

            def transposes(pre, count, base, src, tiles=TT):
                pe.wait_ge(xn_ready, base)
                for d in range(count):
                    p = fill(pe, f"{pre}{d}")
                    for t in range(tiles):
                        last = tr(p[:, t * 128:(t + 1) * 128], src(d, t))
                    filled(last, f"{pre}{d}")

            u_unit(2)
            u_unit(3)
            transposes("m", 4, MT, lambda i, j: memr[:, j % 2, (2 * i + j // 2) * 128:(2 * i + j // 2 + 1) * 128])

            def weights_in(q):
                pe.wait_ge(w1p_ready, q + 1)
                for i, n in enumerate("ri"):
                    p = fill(pe, f"w1{n}{q}")
                    for g in range(QP):
                        last = tr(p[:, g * 128:(g + 1) * 128], w1p[:, i, g * 128:(g + 1) * 128])
                    filled(last, f"w1{n}{q}")
                pe.wait_ge(ca_ready, q + 1)
                p = [fill(pe, f"k{n}{q}") for n in "ab"]
                for a in range(QP):
                    at = slice(a * (L + 1) * CG, a * (L + 1) * CG + L * CG)
                    for part in range(2):
                        for b in range(2):
                            rows = slice(b * NS, (b + 1) * NS)
                            last = mm(p[b][0:CG, a * 128:(a + 1) * 128], bb[rows, part, q * QP + a, :],
                                      ca[rows, q % 2, part, at], part == 0, part == 1)
                            if a == QP - 1 and part == 1:
                                filled(last, f"k{'ab'[b]}{q}")

            def states_in(q):
                pe.wait_ge(u_in, 16 * L)
                after_drain(pe, f"w1r{q}")
                after_drain(pe, f"w1i{q}")
                for i, n in enumerate("ri"):
                    p = fill(pe, f"v{n}{q}")
                    for g in range(QG):
                        rows, gp = slice(g % 2 * NS, g % 2 * NS + NS), g // 2
                        last = mm(p[rows, gp * NC:(gp + 1) * NC],
                                  w1[:, q % 2, i, gp * 128 + g % 2 * NS:gp * 128 + g % 2 * NS + NS],
                                  ub[:, q * QG + g, :])
                    filled(last, f"v{n}{q}")

            def outputs(q):
                pe.wait_ge(t_in[q], 16 * L)
                pe.wait_ge(z_ready, q + 1)
                p = [fill(pe, f"y{n}{q}") for n in "eo"]
                for a in range(QP):
                    for b in range(2):
                        g = 2 * a + b
                        mm(p[b][:, a * NC:(a + 1) * NC], toep[:, g, :], ub[:, q * QG + g, :], True, False)
                    at = slice((a * (L + 1) + 1) * CG, (a + 1) * (L + 1) * CG)
                    for part in range(2):
                        for b in range(2):
                            rows = slice(b * NS, (b + 1) * NS)
                            last = mm(p[b][:, a * NC + 1:(a + 1) * NC], ca[rows, q % 2, part, at],
                                      zb[rows, part, a, 0:NC - 1], False, part == 1)
                            if a == QP - 1 and part == 1:
                                filled(last, f"y{'eo'[b]}{q}")

            def head_transposes(pre, base, src, tiles=TT):
                for t in range(tiles):
                    pe.wait_ge(xn_ready, base + t + 1)
                    p = fill(pe, f"{pre}{t}")
                    for a in range(4):
                        last = tr(p[:, a * 128:(a + 1) * 128], src[:, t, a * 128:(a + 1) * 128])
                    filled(last, f"{pre}{t}")

            proj(4, U_Q, "q")
            proj(5, U_Q, "q")
            weights_in(0)
            proj(6, U_Q, "q")
            states_in(0)
            proj(7, U_Q, "q")
            weights_in(1)
            proj(8, U_K, "k")
            outputs(0)
            states_in(1)
            proj(9, U_K, "k")
            N0 = MT
            head_transposes("qt", N0, qk)
            weights_in(2)
            proj(10, U_K, "k")
            outputs(1)
            states_in(2)
            proj(11, U_K, "k")
            weights_in(3)
            proj(12, U_V, "v")
            outputs(2)
            states_in(3)
            proj(13, U_V, "v")
            head_transposes("kt", N0 + TT, qk)
            proj(14, U_V, "v")
            outputs(3)
            proj(15, U_V, "v")

            def scores(s):
                qt, h = s // H, s % H
                rows = slice(h % 2 * HD, h % 2 * HD + HD)
                p = fill(pe, f"sc{s}")
                n = (qt + 1) * 128
                filled(mm(p[:, 0:n], qT[rows, h // 2, qt * 128:(qt + 1) * 128], kT[rows, h // 2, 0:n]), f"sc{s}")

            def prob_transposes(pre, sc, s, tiles):
                after_drain(pe, f"{sc}{s}")
                p = fill(pe, f"{pre}{s}")
                for a in range(tiles):
                    last = tr(p[:, a * 128:(a + 1) * 128], pbuf[:, s % 2, a * 128:(a + 1) * 128])
                filled(last, f"{pre}{s}")

            def values(s, heads, width, pt, bank, tiles, v):
                t, h = s // heads, s % heads
                after_drain(pe, f"{pt}{s}")
                p = fill(pe, f"{bank}{t}") if h == 0 else pb[uses[f"{bank}{t}"][0]]
                for a in range(tiles):
                    last = mm(p[:, h * width:(h + 1) * width], ptb[:, s % 2, a * 128:(a + 1) * 128],
                              v[:, a, h * width:(h + 1) * width], a == 0, a == tiles - 1)
                if h == heads - 1:
                    filled(last, f"{bank}{t}")
                else:
                    last.then_inc(pv_done, 1)

            for t in range(TT):
                after_drain(pe, f"qt{t}")
                after_drain(pe, f"kt{t}")
                after_drain(pe, f"v{t}")
            NMK = N0 + 2 * TT + MT

            def glu_tile(m):
                u, at = U_GLU + m // 2, slice(m % 2 * 128, m % 2 * 128 + 128)
                pe.wait_ge(lo_done, u + 1)
                p = fill(pe, f"z{m}")
                for k in range(4):
                    last = mm3(p[:, :], w_unit(u, 0)[:, k, at], w_unit(u, 1)[:, k, at], xs[:, 0, 4 + k, :],
                               xs[:, 1, 4 + k, :], k == 0, k == 3)
                filled(last, f"z{m}")

            def piece(t, i, u0, units, act_tile, name):
                u, (half, j) = u0 + i, divmod(i, units)
                if t == 0:
                    pe.wait_ge(lo_done, u + 1)
                p = fill(pe, name(t, half)) if j == 0 else pb[uses[name(t, half)][0]]
                for k in range(2):
                    kk = 2 * j + k
                    last = mm3(p[:, :], act_tile(0, kk, t), act_tile(1, kk, t), w_unit(u, 0)[:, k, :],
                               w_unit(u, 1)[:, k, :], kk == 0, kk == 2 * units - 1)
                if j == units - 1:
                    filled(last, name(t, half))
                elif t == TT - 1:
                    last.then_inc(unit_used, 1)

            def sout_piece(n):
                piece(n // 4, n % 4, U_OUT, 2, x_tile, lambda t, half: f"g{t}{half}")

            def tile_transposes(name, src):
                p = fill(pe, name)
                for a in range(4):
                    last = tr(p[:, a * 128:(a + 1) * 128], src[:, a * 128:(a + 1) * 128])
                filled(last, name)

            def ya_transposes(t):
                after_drain(pe, f"pv{t}")
                tile_transposes(f"ya{t}", yrow[:, t, :])

            scores(0)
            scores(1)
            for s in range(TT * H):
                if s + 2 < TT * H:
                    scores(s + 2)
                if s in MK_AT:
                    rows_unit(U_MK + MK_AT.index(s), U_MK, 4, m_tile, MT, names("mk", MT))
                if s in GLU_AT:
                    if s == GLU_AT[0]:
                        pe.wait_ge(glu_in, NQ)
                    glu_tile(GLU_AT.index(s))
                if s in MV_AT:
                    rows_unit(U_MV + MV_AT.index(s), U_MV, 4, m_tile, MT, names("mv", MT))
                if s == SOUT_AT[0]:
                    after_drain(pe, "bc")
                for n in range(4 * TT):
                    if SOUT_AT[n] == s:
                        sout_piece(n)
                prob_transposes("pt", "sc", s, s // H + 1)
                if s >= 1:
                    values(s - 1, H, HD, "pt", "pv", (s - 1) // H + 1, vrow)
                if s in YA_AT:
                    ya_transposes(YA_AT.index(s))
                if s == 16:
                    pe.wait_ge(ones_ok, 1)
                    pe.wait_ge(ysq_ready, 4)
                    p = fill(pe, "ss")
                    for t in range(TT):
                        for c in range(4):
                            last = mm(p[:, t:t + 1], sg[:, c, t * 128:(t + 1) * 128], ones[:, 0:1], c == 0, c == 3)
                    filled(last, "ss")
                if s == 17:
                    pe.wait_ge(xn_ready, NMK)
                    for i in range(2):
                        p = fill(pe, f"kx{i}")
                        for h in range(2):
                            for t in range(MT):
                                last = tr(p[:, h * M + t * 128:h * M + (t + 1) * 128],
                                          mkrow[:, t, (2 * i + h) * XD:(2 * i + h + 1) * XD])
                        filled(last, f"kx{i}")
                if s == 19:
                    pe.wait_ge(ssr_ready, 1)
                    token_factors("bc", "ss")
            values(TT * H - 1, H, HD, "pt", "pv", TT, vrow)
            ya_transposes(TT - 1)

            def out_piece(t, i):
                piece(t, i, U_OA, 2, lambda part, k, t: x_tile(part, 4 + k, t), lambda t, half: f"o{t}{half}")

            def xq_piece(t, i):
                piece(t, i, U_XQ, 4, x_tile, lambda t, half: f"qx{t}")

            def xo_piece(t, i):
                piece(t, i, U_XO, 2, o_tile, lambda t, half: f"w{t}{half}")

            def h_transposes(name, t, src):
                for half in range(2):
                    tile_transposes(f"{name}{t}{half}", src[:, half * 512:(half + 1) * 512])

            def x2_transposes(t):
                after_drain(pe, f"o{t}0")
                after_drain(pe, f"o{t}1")
                h_transposes("x2", t, hres[:, t, :])

            for t in range(TT):
                after_drain(pe, f"ya{t}")
                for i in range(4):
                    out_piece(t, i)
                if t >= 1:
                    x2_transposes(t - 1)
            x2_transposes(TT - 1)

            def x2_ready(t):
                after_drain(pe, f"x2{t}0")
                after_drain(pe, f"x2{t}1")

            for t in range(2):
                x2_ready(t)
                for i in range(4):
                    xq_piece(t, i)

            def qx_transposes(t):
                pe.wait_ge(xn_ready, NMK + t + 1)
                tile_transposes(f"qxt{t}", qk[:, t, :])

            def x_scores(s):
                t, h = s // XH, s % XH
                if h == 0:
                    after_drain(pe, f"qxt{t}")
                p = fill(pe, f"xs{s}")
                filled(mm(p[:, 0:M], qT[:, h, t * 128:(t + 1) * 128], kxT[:, h, :]), f"xs{s}")

            def xo_transposes(t):
                after_drain(pe, f"xpv{t}")
                tile_transposes(f"xo{t}", yrow[:, t, :])

            def x3_transposes(t):
                pe.wait_ge(xn_ready, NMK + TT + t + 1)
                h_transposes("x3", t, x3row[:, t % 2, :])

            after_drain(pe, "kx0")
            after_drain(pe, "kx1")
            after_drain(pe, "mv0")
            after_drain(pe, "mv1")
            qx_transposes(0)
            x_scores(0)
            for s in range(TT * XH):
                if s in (1, 6, 10):
                    qx_transposes({1: 1, 6: 2, 10: 3}[s])
                if s + 1 < TT * XH:
                    x_scores(s + 1)
                if s < 2 * XH:
                    if s % XH == 0:
                        x2_ready(s // XH + 2)
                    xq_piece(s // XH + 2, s % XH)
                else:
                    if s % XH == 0:
                        after_drain(pe, f"xo{s // XH - 2}")
                    xo_piece(s // XH - 2, s % XH)
                prob_transposes("xp", "xs", s, MT)
                if s >= 1:
                    values(s - 1, XH, XD, "xp", "xpv", MT, xv)
                if s in (6, 10, 14):
                    xo_transposes((s - 6) // 4)
            values(TT * XH - 1, XH, XD, "xp", "xpv", MT, xv)
            after_drain(pe, "xo2")
            for i in range(4):
                xo_piece(2, i)
            xo_transposes(3)
            x3_transposes(0)
            x3_transposes(1)
            after_drain(pe, "xo3")
            for i in range(4):
                xo_piece(3, i)

            def up_half(k, half):
                u, at = U_UP + k, slice(half * 256, half * 256 + 256)
                if half == 0:
                    pe.wait_ge(lo_done, u + 1)
                    fill(pe, f"f{k}")
                p = pb[uses[f"f{k}"][0]]
                for kk in range(KD):
                    last = mm3(p[:, at], w_unit(u, 0)[:, kk, :], w_unit(u, 1)[:, kk, :], xs[:, 0, kk, at],
                               xs[:, 1, kk, at], kk == 0, kk == KD - 1)
                if half == 1:
                    filled(last, f"f{k}")

            for half in range(2):
                for t in (2 * half, 2 * half + 1):
                    if half == 1:
                        x3_transposes(t)
                    after_drain(pe, f"x3{t}0")
                    after_drain(pe, f"x3{t}1")
                for k in range(4):
                    up_half(k, half)
            for k in range(4, 2 * FT):
                cols_unit(U_UP + k, KD, lambda part, kk: xs[:, part, kk, :], [f"f{k}"])
            for n in range(FT):
                u = U_DOWN + n
                pe.wait_ge(lo_done, u + 1)
                pe.wait_ge(act_lo, n + 1)
                for b in range(8):
                    t, half = b // 2, b % 2
                    p = fill(pe, f"d{b}") if n == 0 else pb[b]
                    at = slice(n % 4 * 512 + t * 128, n % 4 * 512 + (t + 1) * 128)
                    cols = slice(half * 512, (half + 1) * 512)
                    last = mm3(p[:, :], bs[:, 0, at], bs[:, 1, at], w_unit(u, 0)[:, 0, cols], w_unit(u, 1)[:, 0, cols],
                               n == 0, n == FT - 1)
                    if n == FT - 1:
                        filled(last, f"d{b}")
                if n < FT - 1:
                    last.then_inc(unit_used, 1)


INPUTS = ["x", "mem", "norm_mix", "w_in", "attn_qn", "attn_kn", "ssm_lam_re", "ssm_lam_im", "ssm_log_step",
          "ssm_b_re", "ssm_b_im", "ssm_c_re", "ssm_c_im", "ssm_d", "ssm_w_glu", "ssm_b_glu", "gnorm_ssm",
          "gnorm_attn", "w_out", "rel_bias", "norm_xattn", "norm_mem", "x_wq", "x_wkv", "x_wo", "x_qn",
          "x_kn", "norm_ffn", "ffn_w_up", "ffn_conv_w", "ffn_conv_b", "ffn_w_down"]


def kernel(**inputs):
    import concourse.bacc as bacc
    from concourse.bass_utils import run_bass_kernel_spmd

    nc = bacc.Bacc("TRN2", target_bir_lowering=False, num_devices=1)
    arrays, aps = {}, {}
    for name in INPUTS:
        a = np.ascontiguousarray(inputs[name])
        arrays[f"in_{name}"] = a
        aps[name] = nc.dram_tensor(f"in_{name}", a.shape, mybir.dt.from_np(a.dtype), kind="ExternalInput").ap()
    arrays["in_buckets"] = bucket_table()
    aps["buckets"] = nc.dram_tensor("in_buckets", (NB + 1, 384), mybir.dt.float32, kind="ExternalInput").ap()
    out = nc.dram_tensor("out_0", (1, T, D), mybir.dt.float32, kind="ExternalOutput").ap()
    layer(nc, aps, out)
    r = run_bass_kernel_spmd(nc, [arrays], core_ids=[0])
    return r.results[0]["out_0"]
```

```python
import math
from contextlib import ExitStack

import numpy as np
import concourse.bass as bass
from concourse import mybir

T = 512
TT = T // 128
D = 1024
KD = D // 128
DS = 512
G, CG, NS = 32, 16, 64
GP = G // 2
H, HD = 8, 64
M = 256
MT = M // 128
XH, XD = 4, 128
DF = 2816
FT = DF // 128
EPS = 1e-6
NEG = -1e30
NB, MAXD = 32, 128
L = 8
NC = T // L
QG = 8
NQ = G // QG
QP = QG // 2

GAINS = [("norm_xattn", 8), ("norm_mem", 8), ("norm_ffn", 8), ("gnorm_ssm", 4),
         ("gnorm_attn", 4), ("ssm_d", 4), ("ssm_b_glu", 4), ("x_qn", 1), ("x_kn", 1),
         ("attn_qn", 1), ("attn_kn", 1)]
N_GAIN = len(GAINS) + 2
COL = {}
_at = 0
for _n, _k in GAINS:
    COL[_n] = _at
    _at += _k
NG = _at

U_SSM, U_Q, U_K, U_V, U_MK, U_GLU = 0, 4, 8, 12, 16, 20
U_MV, U_OUT, U_XQ, U_XO, U_UP, U_DOWN = 22, 26, 34, 38, 42, 86
U_OA = U_OUT + 4
U_END = U_DOWN + FT


MK_AT = [0, 2, 4, 6]
GLU_AT = [8, 9, 10, 11]
MV_AT = [12, 14, 16, 19]
SOUT_AT = [23, 23, 24, 24, 25, 25, 26, 26, 27, 27, 28, 28, 29, 30, 31, 31]
XO_AT = [4, 5, 6, 8]
SPLIT_AT = {2: 20, 4: 21, 6: 22, 8: 23, 11: 24, 13: 25, 15: 26, 17: 27, 19: 28, 21: 29, 30: 30, 31: 31}
YA_AT = [13, 23, 26]


def bucket_table():
    t = np.zeros((NB + 1, 384), np.float32)
    half = NB // 2
    for y in range(384):
        dist = 255 - y
        if dist < 0:
            t[NB, y] = 1.0
            continue
        b = dist
        if dist >= half:
            b = min(half + int(math.log(dist / half) / math.log(MAXD / half) * (NB - half)), NB - 1)
        t[b, y] += 1.0
        t[NB - 1, y] -= 1.0
    return t


def layer(nc, A, out):
    f32, f32r = mybir.dt.float32, mybir.dt.float32r
    ALU, ACT, AX = mybir.AluOpType, mybir.ActivationFunctionType, mybir.AxisListType

    scr_u = nc.dram_tensor("scr_u", (DS, L, NC), f32).ap()
    scr_y = nc.dram_tensor("scr_y", (NQ, 128, QG, NC), f32).ap()
    scr_b = nc.dram_tensor("scr_b", (128 * H * 384,), f32).ap()

    ctx = ExitStack()
    with ctx:
        def sb(name, shape, dt=f32):
            return ctx.enter_context(nc.sbuf_tensor(name, shape, dt))

        def sem(name):
            return ctx.enter_context(nc.semaphore(name))

        wring = sb("wring", [128, 4, 2, 1024], f32r)
        xs = sb("xs", [128, 2, KD, T], f32r)
        bs = sb("bs", [128, 2, 2048], f32r)
        raw = sb("raw", [128, 2, 2048])
        ident = sb("ident", [128, 128])
        ones = sb("ones", [128, 1])
        lsrow = sb("lsrow", [GP, 2])
        relb = sb("relb", [NB + 1, H])
        gcol = sb("gcol", [128, NG])
        ccol = sb("ccol", [128, 4, 2 * FT])
        lam = sb("lam", [128, 3 * GP + KD])
        sp = sb("sp", [128, 24, GP])
        pw = sb("pw", [128, 2, GP, L + 1])
        nmx = sb("nmx", [128, 48])
        lsum = sb("lsum", [128, 48])
        rl = sb("rl", [128, 16])
        F = sb("F", [128, 4096 + 12416 + 2048 + 2048 + 2048 + 4096])

        def region(at, *dims):
            n = int(np.prod(dims))
            v = F[:, at:at + n]
            if len(dims) == 1:
                return v
            names = "abcd"[:len(dims)]
            return v.rearrange(f"p ({' '.join(names)}) -> p {' '.join(names)}",
                               **{k: d for k, d in zip(names, dims)})

        ph = region(0, 2, GP, NC)
        w1 = region(2048, 2, 2, 512)
        bias = region(0, H, 512)
        R0 = 4096
        ca = region(R0, 2, 2, QP * (L + 1) * CG)
        w1p = region(R0 + 2304, 2, 512)
        kt = region(R0 + 3328, QG, 128)
        toep = region(R0 + 4352, QG, 128)
        ub = region(R0 + 5376, G, NC)
        craw = region(R0 + 5376, 2, 4, 128)
        zb = region(R0 + 7424, 2, QP, NC)
        dtmp = region(R0 + 7936, 4, QP, NC)
        ptmp = region(R0 + 8960, 2, 576)
        yb = region(R0 + 10112, 512)
        bmat = region(R0 + 10112, 2, GP, CG)
        yst = region(R0 + 10624, 512)
        cmat = region(R0 + 11136, 3, GP, CG)
        bb = region(R0 + 11904, 2, GP, CG)
        pbuf = region(R0, 2, 512)
        ptb = region(R0 + 1024, 2, 512)
        yrow = region(R0 + 2048, TT, 512)
        mkrow = region(R0 + 4096, MT, 512)
        kxT = region(R0 + 5120, XH, M)
        xv = region(R0 + 6144, MT, 512)
        hres = region(R0 + 7808, TT, D)
        hff_flat = region(0, FT * T)
        R1 = R0 + 12416
        uT = region(R1, NQ, T)
        grow = region(R0 + 7936, 128)[0:NG]
        nrow = region(R0 + 8832, 128)[0:KD]
        crow = region(R0 + 8064, 2, 128)[0:88]
        prow = region(R0 + 8320, 3, 128)[0:GP]
        qk = region(R1 + 2048, TT, 512)
        sg = region(R1 + 2048, 4, 512)
        gffn = region(0, D)
        xbc = qk[:, 2, :]
        x3row = region(R1 + 4096, 2, D)
        vrow = region(R1 + 4096, TT, 512)
        mrow = region(R1 + 4096, 2048)
        R2 = R1 + 6144
        qT = region(R2, 4, T)
        kT = region(R2 + 2048, 4, T)
        xr = region(R2, TT, D)
        cv = region(R2, 4, T)
        memr = mrow.rearrange("p (t d) -> p t d", t=MT)

        ccol_flat = ccol[:, :, :].rearrange("p a b -> p (a b)")

        pb = [ctx.enter_context(nc.psum_tensor(f"pb{i}", [128, 512], f32)) for i in range(8)]

        raw_in = [sem("raw_in0"), sem("raw_in1")]
        x_in = [sem(f"x_in{t}") for t in range(TT)]
        mem_in, conv_in = sem("mem_in"), sem("conv_in")
        par_in, gain_in = sem("par_in"), sem("gain_in")
        c_in, b_in, relb_in = sem("c_in"), sem("b_in"), sem("relb_in")
        scr_out, bias_in = sem("scr_out"), sem("bias_in")
        su_out, u_in = sem("su_out"), sem("u_in")
        t_in = [sem(f"t_in{q}") for q in range(NQ)]
        sy_out = [sem(f"sy_out{q}") for q in range(NQ)]
        y_in = [sem(f"y_in{q}") for q in range(NQ)]
        h_in, gffn_in = sem("h_in"), sem("gffn_in")
        out_done = sem("out_done")
        ident_ok, zero_ok, ones_ok = sem("ident_ok"), sem("zero_ok"), sem("ones_ok")
        half_ok, far_zero = sem("half_ok"), sem("far_zero")
        step_row, relb_ok = sem("step_row"), sem("relb_ok")
        dve_step, act_step, pool_step = sem("dve_step"), sem("act_step"), sem("pool_step")
        hi_done, lo_done = sem("hi_done"), sem("lo_done")
        unit_used = sem("unit_used")
        bank_full = [sem(f"bank_full{i}") for i in range(8)]
        bank_free = [sem(f"bank_free{i}") for i in range(8)]
        act_hi, act_lo = sem("act_hi"), sem("act_lo")
        sq_done = sem("sq_done")
        ms_ready = sem("ms_ready")
        rs_ready, pow_ready = sem("rs_ready"), sem("pow_ready")
        xn_ready = sem("xn_ready")
        xr_ready, ssr_ready, x2r_ready = sem("xr_ready"), sem("ssr_ready"), sem("x2r_ready")
        stp_ready, sa_ready, mag_ready = sem("stp_ready"), sem("sa_ready"), sem("mag_ready")
        ang_ready, sin_ready = sem("ang_ready"), sem("sin_ready")
        par_ready, ph_ready = sem("par_ready"), sem("ph_ready")
        w1p_ready, ca_ready = sem("w1p_ready"), sem("ca_ready")
        z_ready, zz_ready = sem("z_ready"), sem("zz_ready")
        gelu_ready, glu_in, hb_ready = sem("gelu_ready"), sem("glu_in"), sem("hb_ready")
        y2_ready, ysq_ready, y3_ready = sem("y2_ready"), sem("ysq_ready"), sem("y3_ready")
        logit_ready, pv_done = sem("logit_ready"), sem("pv_done")
        conv_ready, gate_ready = sem("conv_ready"), sem("gate_ready")
        hff_ready, res_ready = sem("hff_ready"), sem("res_ready")

        XO_BANK, W_BANK = (0, 2, 1, 7), (0, 1, 2, 0, 3, 1, 2, 3)

        uses, fills = {}, [0] * 8

        def use(bank, name):
            uses[name] = (bank, fills[bank])
            fills[bank] += 1

        def plan():
            use(4, "lam")
            for d in range(KD):
                use(d, f"x{d}")
            use(4, "xb"); use(5, "par"); use(6, "cr"); use(7, "cm"); use(6, "relb")
            for m in range(4):
                use(m, f"u{m}")
            for i in range(4):
                use(4 + i, f"m{i}")

            def sa(q):
                use(4, f"w1r{q}"); use(5, f"w1i{q}"); use(6, f"ka{q}"); use(7, f"kb{q}")

            def sbq(q):
                use(4, f"vr{q}"); use(5, f"vi{q}")
            for p in "qkv":
                for t in range(TT):
                    use(t, f"{p}{t}")
            sa(0); sbq(0); sa(1); use(6, "ye0"); use(7, "yo0"); sbq(1)
            for t in range(TT):
                use(4 + t, f"qt{t}")
            sa(2); use(6, "ye1"); use(7, "yo1"); sbq(2); sa(3); use(6, "ye2"); use(7, "yo2"); sbq(3)
            for t in range(TT):
                use(4 + t, f"kt{t}")
            use(6, "ye3"); use(7, "yo3")
            for s in range(TT * H):
                use(3 + s % 3, f"sc{s}"); use(6, f"pt{s}")
            for t in range(TT):
                use(7, f"pv{t}")
            use(0, "mk0"); use(1, "mk1")
            use(2, "z0"); use(0, "z1"); use(1, "z2"); use(2, "z3")
            use(2, "ya0"); use(2, "ss"); use(2, "bc"); use(2, "ya1")
            use(0, "mv0"); use(1, "mv1"); use(0, "kx0"); use(1, "kx1")
            for t in range(TT):
                for half in range(2):
                    use((2 * t + half) % 3, f"g{t}{half}")
                if t == 1:
                    use(2, "ya2")
            use(6, "ya3")
            for t in range(TT):
                for half in range(2):
                    use((2 * t + half) % 4, f"o{t}{half}")
                    use(4 + (2 * t + half) % 4, f"x2{t}{half}")
            for t in range(TT):
                use(t % 3, f"qx{t}"); use(min(t, 2), f"qxt{t}")
            for s in range(TT * XH):
                use(3 + s % 3, f"xs{s}"); use(6, f"xp{s}")
            for t in range(TT):
                use(7, f"xpv{t}"); use(XO_BANK[t], f"xo{t}")
                for half in range(2):
                    use(W_BANK[2 * t + half], f"w{t}{half}")
            for t in range(TT):
                for half in range(2):
                    use(4 + (2 * t + half) % 4, f"x3{t}{half}")
            for j in range(2 * FT):
                use(j % 4, f"f{j}")
            for b in range(8):
                use(b, f"d{b}")
        plan()

        DONE = {m: f"u{m}" for m in range(4)}
        DONE.update({U_Q + 3: "q3", U_K + 3: "k3", U_V + 3: "v3", U_MK + 3: "mk1", U_MV + 3: "mv1",
                     U_GLU: "z1", U_GLU + 1: "z3", U_OUT + 1: "g30", U_OUT + 3: "g31",
                     U_OA + 1: "o30", U_OA + 3: "o31", U_XQ + 3: "qx3", U_XO + 1: "w30", U_XO + 3: "w31"})
        DONE.update({U_UP + j: f"f{j}" for j in range(2 * FT)})

        def wait_unit(eng, u, r=0):
            if u in DONE:
                bank, n = uses[DONE[u]]
                eng.wait_ge(bank_full[bank], r + (n + 1))
            else:
                eng.wait_ge(unit_used, r * 4 + sum(v not in DONE for v in range(u + 1)))

        def fill(pe, name, r=0):
            bank, n = uses[name]
            if n > 0:
                pe.wait_ge(bank_free[bank], r + n)
            return pb[bank]

        def filled(ins, name):
            ins.then_inc(bank_full[uses[name][0]], 1)

        def read(eng, name, r=0):
            bank, n = uses[name]
            eng.wait_ge(bank_full[bank], r + (n + 1))
            return pb[bank]

        def drained(ins, name):
            ins.then_inc(bank_free[uses[name][0]], 1)

        def after_drain(eng, name, r=0):
            bank, n = uses[name]
            eng.wait_ge(bank_free[bank], r + (n + 1))

        def wait_values(eng, s, heads, bank, before):
            if s % heads == heads - 1:
                read(eng, f"{bank}{s // heads}")
            else:
                eng.wait_ge(pv_done, before + s + 1 - s // heads)

        def pt_evac(eng, copy, s):
            if s >= 2:
                wait_values(eng, s - 2, H, "pv", 0)
            n = (s // H + 1) * 128
            drained(copy(ptb[:, s % 2, 0:n], read(eng, f"pt{s}")[:, 0:n]), f"pt{s}")

        def xp_evac(eng, copy, s):
            if s >= 2:
                wait_values(eng, s - 2, XH, "xpv", TT * (H - 1))
            drained(copy(ptb[:, s % 2, 0:M], read(eng, f"xp{s}")[:, 0:M]), f"xp{s}")

        def to_tokens(a):
            return a.rearrange("p (k i) -> p i k", i=L)

        w_in = A["w_in"][0].rearrange("(k p) n -> p k n", p=128)
        w_kv = A["x_wkv"][0].rearrange("(k p) n -> p k n", p=128)
        w_glu = A["ssm_w_glu"][0].rearrange("(k p) n -> p k n", p=128)
        w_out = A["w_out"][0].rearrange("(k p) n -> p k n", p=128)
        w_xq = A["x_wq"][0].rearrange("(k p) n -> p k n", p=128)
        w_xo = A["x_wo"][0].rearrange("(k p) n -> p k n", p=128)
        w_up = A["ffn_w_up"][0].rearrange("(k p) n -> p k n", p=128)
        w_dn = A["ffn_w_down"][0].rearrange("(k p) n -> p k n", p=128)

        def chunk_src(c, r=0):
            u = 2 * c
            if u < U_Q:
                return w_in[:, :, 256 * c:256 * c + 256]
            if u < U_MK:
                p, j = (u - U_Q) // 4, (u - U_Q) // 2 % 2
                return w_in[:, 4 * j:4 * j + 4, DS * (p + 1):DS * (p + 2)]
            if u < U_GLU:
                j = (u - U_MK) // 2
                return w_kv[:, 4 * j:4 * j + 4, 0:512]
            if u < U_MV:
                return w_glu
            if u < U_OUT:
                j = (u - U_MV) // 2
                return w_kv[:, 4 * j:4 * j + 4, 512:1024]
            if u < U_XQ:
                j, p = (u - U_OUT) // 4, (u - U_OUT) // 2 % 2
                return w_out[:, 4 * j:4 * j + 4, 512 * p:512 * p + 512]
            if u < U_XO:
                j = (u - U_XQ) // 2
                return w_xq[:, 4 * j:4 * j + 4, :]
            if u < U_UP:
                p = (u - U_XO) // 2
                return w_xo[:, :, 512 * p:512 * p + 512]
            if u < U_DOWN:
                i, p = (u - U_UP) // 4, (u - U_UP) // 2 % 2
                return w_up[:, :, bass.ds(r * 256 + (DF * p + 256 * i), 256)]
            return w_dn[:, bass.ds(r * 4 + (u - U_DOWN), 2), :]

        def unit_dims(u):
            if u < U_Q or U_UP <= u < U_DOWN:
                return 8, 128
            if U_GLU <= u < U_MV:
                return 4, 256
            if u >= U_DOWN:
                return 1, 1024
            return 2, 512

        def raw_unit(u):
            r = raw[:, u // 2 % 2, :]
            a, b = unit_dims(u)
            if b in (128, 256):
                v = r.rearrange("p (k n) -> p k n", k=a)
                return v[:, :, (u % 2) * b:(u % 2) * b + b]
            return r[:, (u % 2) * 1024:(u % 2) * 1024 + 1024].rearrange("p (k n) -> p k n", k=a)

        def w_unit(u, part):
            a, b = unit_dims(u)
            return wring[:, u % 4, part, :].rearrange("p (k n) -> p k n", k=a)

        def load_chunk(eng, c, r=0):
            if c >= 2:
                eng.wait_ge(hi_done, r * 4 + 2 * (c - 1))
                eng.wait_ge(lo_done, r * 4 + 2 * (c - 1))
            src = chunk_src(c, r)
            eng.dma_start(raw[:, c % 2, :].rearrange("p (k n) -> p k n", k=src.shape[1]), src)\
               .then_inc(raw_in[c % 2], 16)

        def unit_gain(u):
            if U_OA <= u < U_XQ:
                return COL["gnorm_attn"] + 2 * ((u - U_OA) % 2)
            if U_XQ <= u < U_XO:
                return COL["norm_xattn"] + 2 * (u - U_XQ)
            return None

        def split_hi(act, u, r=0):
            act.wait_ge(raw_in[u // 2 % 2], r * 16 + 16 * (u // 4 + 1))
            if u >= 4:
                wait_unit(act, u - 4, r)
            g = unit_gain(u)
            if g is None:
                ins = nc.scalar.activation(w_unit(u, 0), raw_unit(u), ACT.Copy)
            else:
                for k in range(2):
                    ins = nc.scalar.activation(w_unit(u, 0)[:, k, :], raw_unit(u)[:, k, :], ACT.Copy,
                                               scale=gcol[:, g + k:g + k + 1])
            ins.then_inc(hi_done, 1)

        def split_lo(dve, u, r=0):
            dve.wait_ge(hi_done, r * 4 + (u + 1))
            g = unit_gain(u)
            if g is None:
                ins = nc.vector.tensor_tensor(w_unit(u, 1), raw_unit(u), w_unit(u, 0).bitcast(f32), ALU.subtract)
            else:
                for k in range(2):
                    ins = nc.vector.scalar_tensor_tensor(
                        out=w_unit(u, 1)[:, k, :], in0=raw_unit(u)[:, k, :], scalar=gcol[:, g + k:g + k + 1],
                        in1=w_unit(u, 0)[:, k, :].bitcast(f32), op0=ALU.mult, op1=ALU.subtract)
            ins.then_inc(lo_done, 1)

        def split_next(eng, split, i, j):
            if isinstance(i, int) and i == FT // 2 - 1:
                split(eng, U_DOWN + j)
            else:
                split(eng, U_UP + 4 + j, i)

        def mm3(ps, lh, ll, rh, rl_, first, last):
            nc.tensor.matmul(ps, lh, rh, start=first, stop=False)
            nc.tensor.matmul(ps, lh, rl_, start=False, stop=False)
            return nc.tensor.matmul(ps, ll, rh, start=False, stop=last)

        EV = [("x", TT, D), ("mem", MT, D), ("q", TT * H, HD), ("k", TT * H, HD), ("mk", MT * XH, XD),
              ("ss", TT, DS), ("ya", TT, DS), ("x2", TT, D)]
        EV += [(f"qx{t}", XH, XD) for t in range(TT)] + [(f"x3{t}", 1, D) for t in range(TT)]
        EVN = {n: i for i, (n, _, _) in enumerate(EV)}
        EVC, at = {}, 0
        for n, k, _ in EV:
            EVC[n] = at
            at += k
        sq = sb("sq", [128, at])
        ms = sb("ms", [128, at])
        rs = sb("rs", [128, at])
        rt = sb("rt", [128, 2, 32])

        def ev(t, name):
            return t[:, EVC[name]:EVC[name] + EV[EVN[name]][1]]

        junk = qk[:, 0:2, :].rearrange("p a b -> p (a b)")
        junk_ya, junk_late = region(R0 + 11904, 512), region(R1, 1024)
        sqr_s5, sqr_late = region(R0 + 7936, 512), region(R0 + 7168, 512)
        mhalf = sb("mhalf", [128, 8])
        hbglu = sb("hbglu", [128, 4])
        n_sq = [0]

        def row_square(act, event, t, row):
            if n_sq[0] > 0:
                act.wait_ge(sq_done, n_sq[0])
            n_sq[0] += 1
            c = EVC[event] + t
            to = {"x": junk, "me": junk, "ya": junk_ya}.get(event[0:2], junk_late)
            nc.scalar.activation(to[:, 0:row.shape[1]], row, ACT.Square, accum_out=sq[:, c:c + 1])\
                .then_inc(sq_done, 1)

        block = ctx.enter_context(nc.Block())

        @block.sync
        def _(sync):
            lam_rows = [A[n][0].rearrange("(a b) n -> a (b n)", b=2) for n in ("ssm_lam_re", "ssm_lam_im")]
            sync.dma_start(prow[:, 0, :], lam_rows[0]).then_inc(par_in, 16)
            sync.dma_start(prow[:, 1, :], lam_rows[1]).then_inc(par_in, 16)
            sync.dma_start(lsrow[:, :], A["ssm_log_step"][0].rearrange("(a b) -> a b", b=2)).then_inc(par_in, 16)
            sync.dma_start(nrow[:, :], A["norm_mix"][0].rearrange("(a n) -> a n", n=128)).then_inc(par_in, 16)
            for t in range(TT):
                sync.dma_start(xr[:, t, :], A["x"][0, t * 128:(t + 1) * 128, :]).then_inc(x_in[t], 16)
            load_chunk(sync, 0)
            load_chunk(sync, 1)
            for i, part in enumerate(("ssm_c_re", "ssm_c_im")):
                for half in range(2):
                    sync.dma_start(craw[:, i, :, half * NS:(half + 1) * NS],
                                   A[part][0].rearrange("(a g) c n -> (g c) a n", a=4)).then_inc(c_in, 16)
            sync.dma_start(relb[0:NB, :], A["rel_bias"]).then_inc(relb_in, 16)
            sync.dma_start(qk[0:NB + 1, 3, 0:384], A["buckets"]).then_inc(relb_in, 16)
            n_gain = 0
            for name, k in GAINS:
                r = COL[name]
                src = A[name][0]
                if name in ("attn_qn", "attn_kn"):
                    for i in range(2):
                        sync.dma_start(grow[r:r + 1, i * HD:(i + 1) * HD], src.rearrange("(a n) -> a n", a=1))\
                            .then_inc(gain_in, 16)
                        n_gain += 1
                else:
                    sync.dma_start(grow[r:r + k, :], src.rearrange("(a n) -> a n", n=128)).then_inc(gain_in, 16)
                    n_gain += 1
            assert n_gain == N_GAIN
            for t in range(MT):
                sync.dma_start(memr[:, t, :], A["mem"][0, t * 128:(t + 1) * 128, :]).then_inc(mem_in, 16)
            cw = A["ffn_conv_w"][0].rearrange("w o (a n) -> w (o a) n", n=128)
            sync.dma_start(crow[0:44, 0, :], cw[0]).then_inc(conv_in, 16)
            sync.dma_start(crow[44:88, 0, :], cw[1]).then_inc(conv_in, 16)
            sync.dma_start(crow[0:44, 1, :], cw[2]).then_inc(conv_in, 16)
            sync.dma_start(crow[44:88, 1, :], A["ffn_conv_b"][0].rearrange("(a n) -> a n", n=128)).then_inc(conv_in, 16)
            load_chunk(sync, 2)
            load_chunk(sync, 3)

            def u_write(q):
                after_drain(sync, f"u{q}")
                sync.dma_start(scr_u[q * 128:(q + 1) * 128].rearrange("p i k -> p (i k)"), uT[:, q, :]).then_inc(su_out, 16)

            def u_read():
                sync.wait_ge(su_out, 16 * NQ)
                after_drain(sync, "cm")
                v = scr_u.rearrange("(g c) i k -> i c g k", c=CG)
                for d in range(L):
                    sync.dma_start(ub[d * CG:(d + 1) * CG, :, :], v[L - 1 - d]).then_inc(u_in, 16)

            def t_load(q):
                after_drain(sync, f"ka{q}")
                after_drain(sync, f"kb{q}")
                if q == 0:
                    sync.wait_ge(zero_ok, 1)
                else:
                    after_drain(sync, f"yo{q - 1}")
                for d in range(L):
                    sync.dma_start(toep[d * CG:(d + 1) * CG, :, (L - 1 - d) * CG:],
                                   kt[0:CG, :, 0:(d + 1) * CG]).then_inc(t_in[q], 16)

            def y_back(q):
                after_drain(sync, f"yo{q}")
                sync.dma_start(scr_y[q].rearrange("p g k -> p (g k)"), yb).then_inc(sy_out[q], 16)
                sync.wait_ge(sy_out[q], 16)
                if q >= 1:
                    sync.wait_ge(zz_ready, q)
                v = scr_y[q].rearrange("(j c) g k -> g c j k", c=CG)
                for g in range(QG):
                    sync.dma_start(yst[g * CG:(g + 1) * CG, :].rearrange("p (j k) -> p j k", j=L), v[g])\
                        .then_inc(y_in[q], 16)

            for q in range(NQ):
                u_write(q)
            u_read()
            load_chunk(sync, 4)
            load_chunk(sync, 5)
            after_drain(sync, "relb")
            sync.dma_start(scr_b.rearrange("(p h y) -> h p y", p=128, h=H),
                           yst[0:H, 0:384].unsqueeze(1).to_broadcast([H, 128, 384])).then_inc(scr_out, 16)
            t_load(0)
            load_chunk(sync, 6)
            sync.wait_ge(scr_out, 16)
            y_back(0)
            t_load(1)
            load_chunk(sync, 7)
            load_chunk(sync, 8)
            y_back(1)
            t_load(2)
            load_chunk(sync, 9)
            y_back(2)
            t_load(3)
            load_chunk(sync, 10)
            sync.wait_ge(z_ready, NQ)
            skew = bass.AP(tensor=scr_b.tensor, offset=127,
                           ap=[[H * 384 - 1, 128], [384, H], [1, 256]])
            sync.dma_start(bias[:, :, 256:512], skew).then_inc(bias_in, 16)
            y_back(3)
            load_chunk(sync, 11)
            sync.wait_ge(zz_ready, NQ)
            for t in range(TT):
                sync.dma_start(hres[:, t, :], A["x"][0, t * 128:(t + 1) * 128, :]).then_inc(h_in, 16)
            for c in range(12, U_UP // 2):
                load_chunk(sync, c)
                if c == U_XQ // 2 + 1:
                    sync.wait_ge(logit_ready, TT * H)
                    sync.dma_start(gffn, A["norm_ffn"].to_broadcast([128, D])).then_inc(gffn_in, 16)
            with sync.Fori(0, FT // 2) as i:
                load_chunk(sync, U_UP // 2, i)
                load_chunk(sync, U_UP // 2 + 1, i)
            with sync.Fori(0, FT // 4) as i:
                load_chunk(sync, U_DOWN // 2, i)
                load_chunk(sync, U_DOWN // 2 + 1, i)
            load_chunk(sync, U_END // 2 - 1)
            for t in range(TT):
                for half in range(2):
                    sync.wait_ge(res_ready, 2 * t + half + 1)
                    sync.dma_start(out[0, t * 128:(t + 1) * 128, half * 512:half * 512 + 512],
                                   hres[:, t, half * 512:half * 512 + 512]).then_inc(out_done, 16)
            sync.wait_ge(out_done, 16 * 2 * TT)

        @block.gpsimd
        def _(pool):
            n_step = [0]

            def link(ins):
                n_step[0] += 1
                ins.then_inc(pool_step, 1)
                pool.wait_ge(pool_step, n_step[0])

            def mul(o, a, b):
                return nc.gpsimd.tensor_tensor(o, a, b, ALU.mult)

            def cmul(o_re, o_im, a_re, a_im, b_re, b_im, t1, t2, sign=ALU.add):
                mul(t1, a_re, b_re)
                link(mul(t2, a_im, b_im))
                link(nc.gpsimd.tensor_tensor(o_re, t1, t2, ALU.subtract))
                mul(t1, a_re, b_im)
                link(mul(t2, a_im, b_re))
                return nc.gpsimd.tensor_tensor(o_im, t1, t2, sign)

            link(nc.gpsimd.memset(ident[:, :], 0.0))
            nc.gpsimd.affine_select(out=ident[:, :], in_=ident[:, :], compare_op=ALU.not_equal,
                                    fill=1.0, base=0, pattern=[[-1, 128]], channel_multiplier=1)\
                .then_inc(ident_ok, 1)
            for i, part in enumerate(("ssm_b_re", "ssm_b_im")):
                pool.dma_start(bmat[:, i], A[part][0].rearrange("(a b) n c -> (b n) a c", b=2)).then_inc(b_in, 16)
            nc.gpsimd.memset(toep[:, :, :], 0.0).then_inc(zero_ok, 1)
            nc.gpsimd.memset(pw[:, 0, :, 0:1], 1.0)
            nc.gpsimd.memset(pw[:, 1, :, 0:1], 0.0)
            nc.gpsimd.memset(ph[:, 0, :, 0:1], 1.0)
            link(nc.gpsimd.memset(ph[:, 1, :, 0:1], 0.0))

            def view(t, *dims):
                n = int(np.prod(dims))
                names = "abcd"[:len(dims)]
                return t[:, 0:n].rearrange(f"p ({' '.join(names)}) -> p {' '.join(names)}",
                                           **{k: d for k, d in zip(names, dims)})

            def powers(tab, top):
                m = 1
                while m < top:
                    k = min(m, top - m)
                    t1, t2 = view(ptmp[:, 0, :], GP, k), view(ptmp[:, 1, :], GP, k)
                    b = [tab[:, i, :, m:m + 1].to_broadcast([128, GP, k]) for i in range(2)]
                    link(cmul(tab[:, 0, :, m + 1:m + 1 + k], tab[:, 1, :, m + 1:m + 1 + k],
                              tab[:, 0, :, 1:1 + k], tab[:, 1, :, 1:1 + k], b[0], b[1], t1, t2))
                    m *= 2

            pool.wait_ge(par_ready, 1)
            pool.wait_ge(b_in, 32)
            t1, t2 = view(ptmp[:, 0, :], GP, CG), view(ptmp[:, 1, :], GP, CG)
            fb = [sp[:, i, :].unsqueeze(2).to_broadcast([128, GP, CG]) for i in (0, 1)]
            link(cmul(bb[:, 0], bb[:, 1], fb[0], fb[1], bmat[:, 0], bmat[:, 1], t1, t2))
            powers(pw, L)

            def quarter(q):
                g0 = q * QP
                if q >= 1:
                    bank, n = uses[f"w1i{q - 1}"]
                    pool.wait_ge(bank_full[bank], n + 1)
                shape = [128, QP, L, CG]
                t1, t2 = view(ptmp[:, 0, :], QP, L, CG), view(ptmp[:, 1, :], QP, L, CG)
                p = [pw[:, i, g0:g0 + QP, 0:L].unsqueeze(3).to_broadcast(shape) for i in range(2)]
                b = [bb[:, i, g0:g0 + QP, :].unsqueeze(2).to_broadcast(shape) for i in range(2)]
                o = [view(w1p[:, i, :], QP, L, CG) for i in range(2)]
                cmul(o[0], o[1], p[0], p[1], b[0], b[1], t1, t2).then_inc(w1p_ready, 1)
                pool.wait_ge(w1p_ready, q + 1)
                if q == 0:
                    after_drain(pool, "cr")
                    after_drain(pool, "cm")
                if q >= 2:
                    after_drain(pool, f"yo{q - 2}")
                shape = [128, QP, L + 1, CG]
                t1, t2 = view(ptmp[:, 0, :], QP, L + 1, CG), view(ptmp[:, 1, :], QP, L + 1, CG)
                p = [pw[:, i, g0:g0 + QP, :].unsqueeze(3).to_broadcast(shape) for i in range(2)]
                c_re, c_im, nc_re = [cmat[:, i, g0:g0 + QP, :].unsqueeze(2).to_broadcast(shape)
                                     for i in range(3)]
                o = [view(ca[:, q % 2, i, :], QP, L + 1, CG) for i in range(2)]
                mul(t1, c_re, p[0])
                link(mul(t2, c_im, p[1]))
                link(nc.gpsimd.tensor_tensor(o[0], t1, t2, ALU.subtract))
                mul(t1, nc_re, p[1])
                link(mul(t2, c_im, p[0]))
                nc.gpsimd.tensor_tensor(o[1], t1, t2, ALU.subtract).then_inc(ca_ready, 1)
                pool.wait_ge(ca_ready, q + 1)

            quarter(0)
            powers(ph, NC - 1)
            nc.gpsimd.memset(rt[:, 1, 31:32], 0.0).then_inc(ph_ready, 1)
            for q in range(1, NQ):
                quarter(q)

            nc.gpsimd.memset(mhalf[:, :], -0.5).then_inc(half_ok, 1)
            pool.wait_ge(half_ok, 1)
            after_drain(pool, "v3")
            for q in range(NQ):
                pool.wait_ge(gelu_ready, q + 1)
                link(nc.gpsimd.tensor_copy(xs[:, 0, 4 + q, :], uT[:, q, :]))
                nc.gpsimd.tensor_tensor(xs[:, 1, 4 + q, :], uT[:, q, :], xs[:, 0, 4 + q, :].bitcast(f32), ALU.subtract)\
                    .then_inc(glu_in, 1)
            for i in range(EVN["mk"], len(EV)):
                name, w, _ = EV[i]
                pool.wait_ge(ms_ready, i + 1)
                nc.gpsimd.tensor_tensor(ev(rs, name), ev(ms, name), mhalf[:, 0:w], ALU.pow).then_inc(pow_ready, 1)

        @block.scalar
        def _(act):
            n_step = [0]

            def link(ins):
                n_step[0] += 1
                ins.then_inc(act_step, 1)
                act.wait_ge(act_step, n_step[0])

            def A_(o, i, f, **k):
                return nc.scalar.activation(o, i, f, **k)

            def inv_root(name):
                act.wait_ge(ms_ready, EVN[name] + 1)
                if EVN[name] > 0:
                    act.wait_ge(rs_ready, EVN[name])
                w = EV[EVN[name]][1]
                link(A_(rt[:, 0, 0:w], ev(ms, name), ACT.Ln))
                A_(ev(rs, name), rt[:, 0, 0:w], ACT.Exp, scale=-0.5).then_inc(rs_ready, 1)

            def act_split(name, dst, gain=1.0):
                A_(dst, read(act, name)[:, :], ACT.Copy, scale=gain).then_inc(act_hi, 1)

            def x_square(t):
                act.wait_ge(x_in[t], 16)
                row_square(act, "x", t, xr[:, t, :])

            after_drain(act, "lam")
            A_(sp[:, 2, :], lam[:, 2 * GP:3 * GP], ACT.Exp).then_inc(stp_ready, 1)
            x_square(0)
            act.wait_ge(sa_ready, 1)
            A_(sp[:, 5, :], sp[:, 3, :], ACT.Exp)
            A_(sp[:, 6, :], sp[:, 3, :], ACT.Exp, scale=float(L)).then_inc(mag_ready, 1)
            act.wait_ge(ang_ready, 1)
            A_(sp[:, 8, :], sp[:, 7, :], ACT.Sin)
            A_(sp[:, 10, :], sp[:, 9, :], ACT.Sin).then_inc(sin_ready, 1)
            for t in range(1, TT):
                x_square(t)
            for d in range(KD):
                act_split(f"x{d}", xs[:, 0, d, :], lam[:, 3 * GP + d:3 * GP + d + 1])
                if d == 3:
                    split_hi(act, 0)
            split_hi(act, 1)
            inv_root("x")
            split_hi(act, 2)
            split_hi(act, 3)
            p = read(act, "par")
            A_(gcol[:, :], p[:, 0:NG], ACT.Copy)
            drained(A_(ccol[:, :, :], p[:, 64:64 + 176].rearrange("p (a b) -> p a b", a=4), ACT.Copy), "par")
            for i, name in enumerate(("cr", "cm")):
                p = read(act, name)
                for half in range(2):
                    rows = slice(half * NS, (half + 1) * NS)
                    src = p[rows, :].rearrange("p (a b c) -> p a b c", b=2, c=CG)[:, :, half, :]
                    ins = A_(cmat[rows, i], src, ACT.Copy)
                    if i == 0:
                        ins = A_(cmat[rows, 2], src, ACT.Copy, scale=-1.0)
                drained(ins, name)
            p = read(act, "relb")
            drained(A_(yst[0:H, 0:384], p[0:H, 0:384], ACT.Copy), "relb")
            after_drain(act, "par")
            act.wait_ge(mem_in, 16 * MT)
            for t in range(MT):
                row_square(act, "mem", t, memr[:, t, :])
            inv_root("mem")
            for m in range(4):
                split_hi(act, U_Q + m)
            for i in range(4):
                p = read(act, f"m{i}")
                for j in range(2):
                    c = COL["norm_mem"] + 2 * i + j
                    A_(bs[:, 0, i * 512 + j * M:i * 512 + (j + 1) * M], p[:, j * M:(j + 1) * M], ACT.Copy,
                       scale=gcol[:, c:c + 1]).then_inc(act_hi, 1)

            def evac(name, dst, src=lambda p: p[:, :]):
                drained(A_(dst, src(read(act, name)), ACT.Copy), name)

            def weights_in(q):
                if q >= 2:
                    read(act, f"vi{q - 2}")
                evac(f"w1i{q}", w1[:, q % 2, 1, :])
                if q >= 1:
                    act.wait_ge(t_in[q - 1], 16 * L)
                for b, n in enumerate("ab"):
                    evac(f"k{n}{q}", kt[0:CG].rearrange("p (a b) n -> p a b n", b=2)[:, :, b, :],
                         lambda p: p[0:CG, :].rearrange("p (a n) -> p a n", a=QP))

            def y_out(q):
                if q >= 1:
                    act.wait_ge(sy_out[q - 1], 16)
                for b, n in enumerate("eo"):
                    drained(A_(yb.rearrange("p (a b k) -> p a b k", b=2, k=NC)[:, :, b, :],
                               read(act, f"y{n}{q}")[:, 0:QP * NC].rearrange("p (a k) -> p a k", a=QP), ACT.Copy),
                            f"y{n}{q}")

            def rows(name, dst):
                for t in range(TT):
                    c = EVC["x"] + t
                    drained(A_(dst[:, t, :], read(act, f"{name}{t}")[:, :], ACT.Copy, scale=rs[:, c:c + 1]), f"{name}{t}")

            split_hi(act, 8)
            split_hi(act, 9)
            weights_in(0)
            split_hi(act, 10)
            after_drain(act, "u3")
            rows("q", qk)
            split_hi(act, 11)
            weights_in(1)
            inv_root("q")
            split_hi(act, 12)
            y_out(0)
            split_hi(act, 13)
            weights_in(2)
            split_hi(act, 14)
            y_out(1)
            for t in range(TT):
                read(act, f"qt{t}")
            rows("k", qk)
            split_hi(act, 15)
            weights_in(3)
            inv_root("k")
            split_hi(act, 16)
            y_out(2)
            split_hi(act, 17)
            split_hi(act, 18)
            y_out(3)

            def gelu(q):
                act.wait_ge(zz_ready, q + 1)
                A_(uT[:, q, :], uT[:, q, :], ACT.Gelu_apprx_tanh).then_inc(gelu_ready, 1)

            for q in range(3):
                gelu(q)
            rows("v", vrow)
            split_hi(act, 19)

            def tile_hi(name, dst):
                A_(dst, read(act, name)[:, :].rearrange("p (a n) -> p a n", a=4), ACT.Copy).then_inc(act_hi, 1)

            def ya_hi(t):
                tile_hi(f"ya{t}", xs[:, 0, 4:8, t * 128:(t + 1) * 128])

            def ya_square(t):
                after_drain(act, f"pv{t}")
                row_square(act, "ya", t, yrow[:, t, :])

            def probabilities(s):
                n = (s // H + 1) * 128
                if s >= 2:
                    read(act, f"pt{s - 2}")
                p = read(act, f"sc{s}")
                act.wait_ge(logit_ready, s + 1)
                drained(A_(pbuf[:, s % 2, 0:n], p[:, 0:n], ACT.Exp, scale=-1.0, bias=nmx[:, s:s + 1],
                           accum_out=lsum[:, s:s + 1]), f"sc{s}")

            probabilities(0)
            for s in range(TT * H):
                if s % 2 == 1:
                    pt_evac(act, lambda o, i: A_(o, i, ACT.Copy), s - 1)
                if s + 1 < TT * H:
                    probabilities(s + 1)
                if s in SPLIT_AT:
                    split_hi(act, SPLIT_AT[s])
                if s == 5:
                    gelu(3)
                if s == 7:
                    evac("mk0", mkrow[:, 0, :])
                    evac("mk1", mkrow[:, 1, :])
                if s - 1 in GLU_AT:
                    m = GLU_AT.index(s - 1)
                    if m == 0:
                        act.wait_ge(hb_ready, 1)
                    drained(A_(sg[:, m, :], read(act, f"z{m}")[:, :], ACT.Tanh, scale=0.5, bias=hbglu[:, m:m + 1]), f"z{m}")
                if s - 3 in GLU_AT:
                    c = GLU_AT.index(s - 3)
                    act.wait_ge(y2_ready, c + 1)
                    A_(sg[:, c, :], uT[:, c, :], ACT.Square).then_inc(ysq_ready, 1)
                if s in YA_AT:
                    ya_square(YA_AT.index(s))
                if s - 1 in YA_AT:
                    ya_hi(YA_AT.index(s - 1))
                if s == 20:
                    evac("mv0", xv[:, 0, :])
                    evac("mv1", xv[:, 1, :])
                if s == 22:
                    for i in range(2):
                        drained(A_(kxT[:, 2 * i:2 * i + 2, :].rearrange("p h m -> p (h m)"), read(act, f"kx{i}")[:, :],
                                   ACT.Copy, scale=gcol[:, COL["x_kn"]:COL["x_kn"] + 1]), f"kx{i}")
                if s in (20, 21):
                    for c in (2 * (s - 20), 2 * (s - 20) + 1):
                        act.wait_ge(y3_ready, c + 1)
                        g = COL["gnorm_ssm"] + c
                        A_(to_tokens(xs[:, 0, c, :]), uT[:, c, :].rearrange("p (i k) -> p i k", i=L),
                           ACT.Copy, scale=gcol[:, g:g + 1]).then_inc(act_hi, 1)
            split_hi(act, U_OA + 2)
            ya_square(TT - 1)
            split_hi(act, U_OA + 3)
            ya_hi(TT - 1)

            def x_hi(name, t):
                for half in range(2):
                    tile_hi(f"{name}{t}{half}", xs[:, 0, 4 * half:4 * half + 4, t * 128:(t + 1) * 128])

            def h_square(name, last_add, event, i, t):
                after_drain(act, f"{last_add}{t}1")
                row_square(act, event, i, hres[:, t, :])

            for t in range(TT):
                if t == TT - 1:
                    split_hi(act, U_XQ)
                    split_hi(act, U_XQ + 1)
                    split_hi(act, U_XQ + 2)
                h_square("x2", "o", "x2", t, t)
                if t >= 1:
                    x_hi("x2", t - 1)
            split_hi(act, U_XQ + 3)
            x_hi("x2", TT - 1)
            act.wait_ge(x2r_ready, 1)

            def qx_rows(t):
                c = EVC["x2"] + t
                drained(A_(qk[:, t, :], read(act, f"qx{t}")[:, :], ACT.Copy, scale=rs[:, c:c + 1]), f"qx{t}")

            def xo_hi(t):
                tile_hi(f"xo{t}", bs[:, 0, :].rearrange("p (a n) -> p a n", a=4)[:, :, t * 128:(t + 1) * 128])

            qx_rows(0)
            qx_rows(1)

            def x_probabilities(s):
                if s >= 2:
                    read(act, f"xp{s - 2}")
                p = read(act, f"xs{s}")
                act.wait_ge(logit_ready, TT * H + s + 1)
                drained(A_(pbuf[:, s % 2, 0:M], p[:, 0:M], ACT.Exp, bias=nmx[:, 32 + s:33 + s],
                           accum_out=lsum[:, 32 + s:33 + s]), f"xs{s}")

            x_probabilities(0)
            for s in range(TT * XH):
                if s % 2 == 1:
                    xp_evac(act, lambda o, i: A_(o, i, ACT.Copy), s - 1)
                if s + 1 < TT * XH:
                    x_probabilities(s + 1)
                if s in (2, 6):
                    qx_rows(2 + s // 6)
                if s in (7, 11, 15):
                    xo_hi((s - 7) // 4)
                if s in XO_AT:
                    split_hi(act, U_XO + XO_AT.index(s))
                if s == 13:
                    h_square("x3", "w", "x30", 0, 0)
            xo_hi(TT - 1)
            h_square("x3", "w", "x31", 0, 1)
            x_hi("x3", 0)
            split_hi(act, U_UP)
            x_hi("x3", 1)
            h_square("x3", "w", "x32", 0, 2)
            split_hi(act, U_UP + 1)
            split_hi(act, U_UP + 2)
            h_square("x3", "w", "x33", 0, 3)
            split_hi(act, U_UP + 3)
            x_hi("x3", 2)
            x_hi("x3", 3)
            def up_round(i, first=False, split=None):
                for j in range(4):
                    p = read(act, f"f{j}", i)
                    if not first:
                        act.wait_ge(hff_ready, i * 2 + (j % 2 - 1))
                    tap, shift = (ccol_flat[:, bass.ds(i * 2 + (c * 2 * FT + j % 2 + FT * (j // 2)), 1)] for c in (2, 3))
                    A_(cv[:, j, :], p[:, :], ACT.Identity, scale=tap, bias=shift).then_inc(conv_ready, 1)
                    split_next(act, split_hi, i, j)
                    if j < 2:
                        after_drain(act, f"f{j}", i)
                        A_(cv[:, j, :], cv[:, j, :], ACT.Silu).then_inc(gate_ready, 1)

            def down_hi(n, r=0):
                act.wait_ge(hff_ready, r * 4 + (n + 1))
                if n >= 4:
                    wait_unit(act, U_DOWN + n - 4, r)
                A_(bs[:, 0, n % 4 * 512:n % 4 * 512 + 512], hff_flat[:, bass.ds(r * (4 * T) + n * T, T)], ACT.Copy)\
                    .then_inc(act_hi, 1)

            up_round(0, first=True)
            with act.Fori(1, FT // 2 - 1) as i:
                up_round(i)
            for n in range(4):
                down_hi(n)
            up_round(FT // 2 - 1)
            with act.Fori(0, FT // 4 - 1) as r:
                for n in range(4, 8):
                    split_hi(act, U_DOWN + n, r)
                    down_hi(n, r)
            for n in range(FT // 4 * 4, FT):
                split_hi(act, U_DOWN + n)
                down_hi(n)

        @block.vector
        def _(dve):
            n_step, n_hi = [0], [0]

            def link(ins):
                n_step[0] += 1
                ins.then_inc(dve_step, 1)
                dve.wait_ge(dve_step, n_step[0])

            V = nc.vector

            def tt(o, a, b, op):
                return V.tensor_tensor(o, a, b, op)

            def ts(o, a, s1, s2, o1, o2):
                return V.tensor_scalar(o, a, s1, s2, o1, o2)

            def stt(o, a, s1, b, o1, o2):
                return V.scalar_tensor_tensor(out=o, in0=a, scalar=s1, in1=b, op0=o1, op1=o2)

            def lo_of(src, hi, lo, g=1.0):
                n_hi[0] += 1
                dve.wait_ge(act_hi, n_hi[0])
                return stt(lo, src, g, hi.bitcast(f32), ALU.mult, ALU.subtract)

            def mean_sq(name):
                n = EV[EVN[name]][2]
                ts(ev(ms, name), ev(sq, name), 1.0 / n, EPS, ALU.mult, ALU.add).then_inc(ms_ready, 1)

            def root(name, ready=None):
                w = EV[EVN[name]][1]
                if EVN[name] < EVN["mk"]:
                    dve.wait_ge(rs_ready, EVN[name] + 1)
                else:
                    dve.wait_ge(pow_ready, EVN[name] - EVN["mk"] + 1)
                r, t = ev(rs, name), rt[:, 1, 0:w]
                link(tt(t, r, r, ALU.mult))
                link(tt(t, t, ev(ms, name), ALU.mult))
                link(ts(t, t, -0.5, 1.5, ALU.mult, ALU.add))
                last = tt(r, r, t, ALU.mult)
                if ready is None:
                    link(last)
                else:
                    last.then_inc(ready, 1)

            def scale_rows(name, dst, src, tiles):
                for t in range(tiles):
                    c = EVC[name] + t
                    V.tensor_scalar_mul(dst[:, t, :], src[:, t, :], rs[:, c:c + 1]).then_inc(xn_ready, 1)

            def head_event(name, src, tiles, heads, pre):
                for t in tiles:
                    after_drain(dve, f"{pre}{t}")
                    sqr = sqr_s5 if name in "qk" else sqr_late
                    at = t - tiles[0]
                    link(tt(sqr, src[:, t, :], src[:, t, :], ALU.mult))
                    c = EVC[name] + at * heads
                    link(V.reduce_sum(sq[:, c:c + heads], sqr.rearrange("p (h n) -> p h n", h=heads), AX.X))
                mean_sq(name)

            def head_rows(name, src, tiles, heads, width):
                root(name)
                for t in tiles:
                    c = EVC[name] + (t - tiles[0]) * heads
                    v = src[:, t, :].rearrange("p (h n) -> p h n", h=heads)
                    tt(v, v, rs[:, c:c + heads].unsqueeze(2).to_broadcast([128, heads, width]), ALU.mult)\
                        .then_inc(xn_ready, 1)

            V.memset(ones[:, :], 1.0).then_inc(ones_ok, 1)
            V.memset(relb[NB:NB + 1, :], NEG).then_inc(relb_ok, 1)
            dve.wait_ge(par_in, 64)
            V.tensor_copy(prow[:, 2, :].rearrange("p (b n) -> p b n", b=2),
                          lsrow[:, :].unsqueeze(2).to_broadcast([GP, 2, NS])).then_inc(step_row, 1)
            p = read(dve, "lam")
            drained(V.tensor_copy(lam[:, :], p[:, 0:3 * GP + KD]), "lam")
            after_drain(dve, "lam")
            c = lambda i: sp[:, i, :]
            dve.wait_ge(stp_ready, 1)
            link(V.tensor_scalar_min(c(11), lam[:, 0:GP], -1e-4))
            tt(c(3), c(11), c(2), ALU.mult).then_inc(sa_ready, 1)
            link(tt(c(4), lam[:, GP:2 * GP], c(2), ALU.mult))
            MAGIC = 12582912.0
            C1 = 6.28125
            C2 = round((2 * math.pi - C1) * 2 ** 22) / 2 ** 22
            C3 = 2 * math.pi - C1 - C2
            TOP = 3.141592
            link(ts(c(12), c(4), 1 / (2 * math.pi), MAGIC, ALU.mult, ALU.add))
            link(V.tensor_scalar_sub(c(12), c(12), MAGIC))
            link(stt(c(7), c(12), -C1, c(4), ALU.mult, ALU.add))
            link(stt(c(7), c(12), -C2, c(7), ALU.mult, ALU.add))
            link(stt(c(7), c(12), -C3, c(7), ALU.mult, ALU.add))
            link(ts(c(7), c(7), TOP, -TOP, ALU.min, ALU.max))
            link(V.tensor_scalar_mul(c(13), c(7), -1.0))
            link(tt(c(13), c(13), c(7), ALU.max))
            ts(c(9), c(13), -1.0, math.pi / 2, ALU.mult, ALU.add).then_inc(ang_ready, 1)
            dve.wait_ge(sin_ready, 1)
            dve.wait_ge(mag_ready, 1)
            tt(pw[:, 0, :, 1], c(5), c(10), ALU.mult)
            tt(pw[:, 1, :, 1], c(5), c(8), ALU.mult)
            tt(c(12), c(11), c(11), ALU.mult)
            link(tt(c(13), lam[:, GP:2 * GP], lam[:, GP:2 * GP], ALU.mult))
            link(tt(c(12), c(12), c(13), ALU.add))
            link(V.reciprocal(c(12), c(12)))
            link(V.tensor_scalar_add(c(14), pw[:, 0, :, 1], -1.0))
            tt(c(15), c(14), c(11), ALU.mult)
            tt(c(16), pw[:, 1, :, 1], lam[:, GP:2 * GP], ALU.mult)
            tt(c(17), pw[:, 1, :, 1], c(11), ALU.mult)
            link(tt(c(18), c(14), lam[:, GP:2 * GP], ALU.mult))
            tt(c(15), c(15), c(16), ALU.add)
            link(tt(c(17), c(17), c(18), ALU.subtract))
            tt(c(0), c(15), c(12), ALU.mult)
            link(tt(c(1), c(17), c(12), ALU.mult))
            a_, b_ = c(10), c(8)
            for i in range(3):
                n0, n1 = (ph[:, 0, :, 1], ph[:, 1, :, 1]) if i == 2 else (c(19 + 2 * i), c(20 + 2 * i))
                tt(c(14), a_, a_, ALU.mult)
                tt(c(15), b_, b_, ALU.mult)
                link(tt(c(16), a_, b_, ALU.mult))
                tt(n0, c(14), c(15), ALU.subtract)
                last = V.tensor_scalar_mul(n1, c(16), 2.0)
                if i < 2:
                    link(last)
                else:
                    last.then_inc(par_ready, 1)
                a_, b_ = n0, n1
            for d in range(KD):
                g = lam[:, 3 * GP + d:3 * GP + d + 1]
                p = read(dve, f"x{d}")
                drained(lo_of(p[:, :], xs[:, 0, d, :], xs[:, 1, d, :], g), f"x{d}")
                if d == 3:
                    split_lo(dve, 0)
            split_lo(dve, 1)
            dve.wait_ge(sq_done, TT)
            mean_sq("x")
            root("x", xr_ready)
            split_lo(dve, 2)
            p = read(dve, "xb")
            drained(V.tensor_copy(xbc, p[:, :]), "xb")
            after_drain(dve, "xb")
            by_step = lambda a: a.rearrange("p (k i) -> p i k", i=L)

            def u_evac(m):
                p = read(dve, f"u{m}")
                drained(tt(uT[:, m, :].rearrange("p (i k) -> p i k", i=L), by_step(p[:, :]), by_step(xbc), ALU.mult),
                        f"u{m}")

            u_evac(0)
            split_lo(dve, 3)
            u_evac(1)
            after_drain(dve, "par")
            dve.wait_ge(sq_done, TT + MT)
            mean_sq("mem")
            root("mem")
            scale_rows("mem", memr, memr, MT)
            b = COL["ssm_b_glu"]
            V.tensor_scalar_mul(hbglu[:, :], gcol[:, b:b + 4], 0.5).then_inc(hb_ready, 1)
            for m in range(4):
                split_lo(dve, U_Q + m)
                if m in (0, 1):
                    u_evac(2 + m)
            for i in range(4):
                p = read(dve, f"m{i}")
                dve.wait_ge(act_hi, n_hi[0] + 2)
                for j in range(2):
                    cc = COL["norm_mem"] + 2 * i + j
                    at = slice(i * 512 + j * M, i * 512 + (j + 1) * M)
                    ins = lo_of(p[:, j * M:(j + 1) * M], bs[:, 0, at], bs[:, 1, at], gcol[:, cc:cc + 1])
                drained(ins, f"m{i}")

            def weights_in(q):
                if q >= 2:
                    read(dve, f"vr{q - 2}")
                drained(V.tensor_copy(w1[:, q % 2, 0, :], read(dve, f"w1r{q}")[:, :]), f"w1r{q}")

            def scan(q):
                if q == 0:
                    dve.wait_ge(ph_ready, 1)
                else:
                    dve.wait_ge(z_ready, q)
                if q >= 1:
                    read(dve, f"yo{q - 1}")
                vr = read(dve, f"vr{q}")[:, 0:QP * NC].rearrange("p (g k) -> p g k", g=QP)
                vi = read(dve, f"vi{q}")[:, 0:QP * NC].rearrange("p (g k) -> p g k", g=QP)
                co, si = (ph[:, i, q * QP:(q + 1) * QP, :] for i in range(2))
                t = [dtmp[:, i] for i in range(4)]
                zr, zi = zb[:, 0], zb[:, 1]
                tt(t[0], vr, co, ALU.mult)
                drained(tt(t[3], vr, si, ALU.mult), f"vr{q}")
                tt(t[1], vi, si, ALU.mult)
                drained(tt(t[2], vi, co, ALU.mult), f"vi{q}")
                after_drain(dve, f"vr{q}")
                after_drain(dve, f"vi{q}")
                tt(zr, t[0], t[1], ALU.add)
                link(tt(zi, t[2], t[3], ALU.subtract))
                for g in range(QP):
                    decay = sp[:, 6, q * QP + g:q * QP + g + 1].to_broadcast([128, NC])
                    V.tensor_tensor_scan(t[0][:, g, :], decay, zr[:, g, :], 0.0, ALU.mult, ALU.add)
                    last = V.tensor_tensor_scan(t[1][:, g, :], decay, zi[:, g, :], 0.0, ALU.mult, ALU.add)
                link(last)
                tt(t[2], t[0], co, ALU.mult)
                link(tt(t[3], t[1], si, ALU.mult))
                link(tt(zr, t[2], t[3], ALU.subtract))
                tt(t[2], t[0], si, ALU.mult)
                link(tt(t[3], t[1], co, ALU.mult))
                tt(zi, t[2], t[3], ALU.add).then_inc(z_ready, 1)

            def skip_in(q):
                dve.wait_ge(y_in[q], 16 * QG)
                g = gcol[:, COL["ssm_d"] + q:COL["ssm_d"] + q + 1]
                stt(uT[:, q, :], uT[:, q, :], g, yst, ALU.mult, ALU.add).then_inc(zz_ready, 1)

            def transposed(pre, dst, gain, scale, tiles=range(TT)):
                for t in tiles:
                    p = read(dve, f"{pre}{t}")
                    drained(ts(dst[:, :, t * 128:(t + 1) * 128], p[:, :].rearrange("p (a b) -> p a b", a=4),
                               gcol[:, COL[gain]:COL[gain] + 1], scale, ALU.mult, ALU.mult), f"{pre}{t}")

            split_lo(dve, 8)
            split_lo(dve, 9)
            weights_in(0)
            split_lo(dve, 10)
            scan(0)
            head_event("q", qk, range(TT), H, "q")
            split_lo(dve, 11)
            weights_in(1)
            head_rows("q", qk, range(TT), H, HD)
            split_lo(dve, 12)
            scan(1)
            split_lo(dve, 13)
            transposed("qt", qT, "attn_qn", HD ** -0.5)
            weights_in(2)
            skip_in(0)
            split_lo(dve, 14)
            scan(2)
            head_event("k", qk, range(TT), H, "k")
            split_lo(dve, 15)
            weights_in(3)
            head_rows("k", qk, range(TT), H, HD)
            skip_in(1)
            split_lo(dve, 16)
            scan(3)
            split_lo(dve, 17)
            transposed("kt", kT, "attn_kn", 1.0)
            skip_in(2)
            split_lo(dve, 18)
            V.memset(bias[:, :, 0:256], 0.0).then_inc(far_zero, 1)
            split_lo(dve, 19)
            dve.wait_ge(far_zero, 1)
            dve.wait_ge(bias_in, 16)

            def normalise(bank, l0, heads, width, t):
                p = read(dve, bank)
                link(V.reciprocal(rl[:, 0:heads], lsum[:, l0:l0 + heads]))
                drained(tt(yrow[:, t, :].rearrange("p (h n) -> p h n", h=heads),
                           p[:, :].rearrange("p (h n) -> p h n", h=heads),
                           rl[:, 0:heads].unsqueeze(2).to_broadcast([128, heads, width]), ALU.mult), bank)
                after_drain(dve, bank)

            def tile_lo(name, hi, lo, last=True):
                ins = lo_of(read(dve, name)[:, :].rearrange("p (a n) -> p a n", a=4), hi, lo)
                drained(ins, name)

            def ya_lo(t):
                at = slice(t * 128, (t + 1) * 128)
                tile_lo(f"ya{t}", xs[:, 0, 4:8, at], xs[:, 1, 4:8, at])

            def residual(name, t, half, factor=1.0):
                o = hres[:, t, half * 512:(half + 1) * 512]
                drained(stt(o, read(dve, name)[:, :], factor, o, ALU.mult, ALU.add), name)

            def logits(s):
                h, n = s % H, (s // H + 1) * 128
                p = read(dve, f"sc{s}")
                V.tensor_tensor_reduce(out=p[:, 0:n], in0=p[:, 0:n], in1=bias[:, h, 512 - n:512], scale=-1.0,
                                       scalar=3.0e38, op0=ALU.add, op1=ALU.min,
                                       accum_out=nmx[:, s:s + 1]).then_inc(logit_ready, 1)

            logits(0)
            for s in range(TT * H):
                if s + 1 < TT * H:
                    logits(s + 1)
                if s in (9, 17, 25):
                    qd = (s - 9) // 8
                    normalise(f"pv{qd}", H * qd, H, HD, qd)
                if s >= 2 and s % 2 == 0:
                    pt_evac(dve, V.tensor_copy, s - 1)
                if s == 4:
                    skip_in(3)
                if s == 8:
                    head_event("mk", mkrow, range(MT), XH, "mk")
                if s == 10:
                    head_rows("mk", mkrow, range(MT), XH, XD)
                if s - 1 in YA_AT:
                    ya_lo(YA_AT.index(s - 1))
                if s - 2 in GLU_AT:
                    m = GLU_AT.index(s - 2)
                    after_drain(dve, f"z{m}")
                    link(ts(sg[:, m, :], sg[:, m, :], 0.5, 0.5, ALU.mult, ALU.add))
                    tt(uT[:, m, :], uT[:, m, :], sg[:, m, :], ALU.mult).then_inc(y2_ready, 1)
                if s == 16:
                    p = read(dve, "ss")
                    drained(V.tensor_copy(ev(sq, "ss"), p[:, 0:TT]), "ss")
                    after_drain(dve, "ss")
                    mean_sq("ss")
                if s == 17:
                    root("ss", ssr_ready)
                if s in (19, 20):
                    p = read(dve, "bc")
                    for cc in (2 * (s - 19), 2 * (s - 19) + 1):
                        tt(uT[:, cc, :], uT[:, cc, :], p[:, :], ALU.mult).then_inc(y3_ready, 1)
                if s in (21, 22):
                    for cc in (2 * (s - 21), 2 * (s - 21) + 1):
                        g = gcol[:, COL["gnorm_ssm"] + cc:COL["gnorm_ssm"] + cc + 1]
                        dve.wait_ge(y3_ready, cc + 1)
                        ins = lo_of(uT[:, cc, :].rearrange("p (i k) -> p i k", i=L), to_tokens(xs[:, 0, cc, :]),
                                    to_tokens(xs[:, 1, cc, :]), g)
                        if cc == 3:
                            drained(ins, "bc")
                if s == 23:
                    dve.wait_ge(h_in, 16 * TT)
                for n in range(2 * TT):
                    if s == SOUT_AT[2 * n + 1] + 1:
                        residual(f"g{n // 2}{n % 2}", n // 2, n % 2)
                if s - 1 in SPLIT_AT:
                    split_lo(dve, SPLIT_AT[s - 1])
            pt_evac(dve, V.tensor_copy, TT * H - 1)
            split_lo(dve, U_OA + 1)
            normalise(f"pv{TT - 1}", H * (TT - 1), H, HD, TT - 1)
            split_lo(dve, U_OA + 2)
            residual("g31", TT - 1, 1)
            split_lo(dve, U_OA + 3)
            ya_lo(TT - 1)
            dve.wait_ge(sq_done, TT + MT + TT)
            mean_sq("ya")
            root("ya")

            def x_lo(name, t):
                for half in range(2):
                    at = (slice(4 * half, 4 * half + 4), slice(t * 128, (t + 1) * 128))
                    tile_lo(f"{name}{t}{half}", xs[:, 0, at[0], at[1]], xs[:, 1, at[0], at[1]])

            for half in range(2):
                for t in range(TT):
                    after_drain(dve, f"g{t}{half}")
            for t in range(TT):
                for half in range(2):
                    c = EVC["ya"] + t
                    if t == TT - 1 and half == 0:
                        split_lo(dve, U_XQ)
                    residual(f"o{t}{half}", t, half, rs[:, c:c + 1])
                if t == TT - 1:
                    split_lo(dve, U_XQ + 1)
                    split_lo(dve, U_XQ + 2)
                if t >= 1:
                    x_lo("x2", t - 1)
            dve.wait_ge(sq_done, TT + MT + TT + TT)
            mean_sq("x2")
            split_lo(dve, U_XQ + 3)
            root("x2", x2r_ready)
            x_lo("x2", TT - 1)

            def qx_event(t):
                head_event(f"qx{t}", qk, [t], XH, "qx")

            def qx_rows(t):
                head_rows(f"qx{t}", qk, [t], XH, XD)

            def xo_lo(t):
                v = [bs[:, i, :].rearrange("p (a n) -> p a n", a=4)[:, :, t * 128:(t + 1) * 128] for i in range(2)]
                tile_lo(f"xo{t}", v[0], v[1])

            def w_residual(t):
                for half in range(2):
                    if t == 0:
                        after_drain(dve, f"o{t}{half}")
                    residual(f"w{t}{half}", t, half)

            def x3_mean(t):
                dve.wait_ge(sq_done, 3 * TT + MT + t + 1)
                mean_sq(f"x3{t}")

            def x3_rows(t):
                root(f"x3{t}")
                if t == 0:
                    dve.wait_ge(gffn_in, 16)
                c = EVC[f"x3{t}"]
                stt(x3row[:, t % 2, :], hres[:, t, :], rs[:, c:c + 1], gffn, ALU.mult, ALU.mult).then_inc(xn_ready, 1)

            qx_event(0)
            qx_rows(0)
            qx_event(1)
            transposed("qxt", qT, "x_qn", XD ** -0.5, [0])
            qx_rows(1)
            def row_max(s):
                p = read(dve, f"xs{s}")
                V.tensor_reduce(nmx[:, 32 + s:33 + s], p[:, 0:M], AX.X, ALU.max, negate=True)\
                    .then_inc(logit_ready, 1)

            row_max(0)
            for s in range(TT * XH):
                if s + 1 < TT * XH:
                    row_max(s + 1)
                if s in (5, 9, 13):
                    t = (s - 5) // 4
                    normalise(f"xpv{t}", 32 + XH * t, XH, XD, t)
                if s >= 2 and s % 2 == 0:
                    xp_evac(dve, V.tensor_copy, s - 1)
                if s in (1, 5, 9):
                    transposed("qxt", qT, "x_qn", XD ** -0.5, [1 + s // 4])
                if s in (3, 7):
                    qx_event(2 + s // 4)
                if s in (4, 8):
                    qx_rows(1 + s // 4)
                if s in (7, 11, 15):
                    xo_lo((s - 7) // 4)
                if s - 1 in XO_AT:
                    split_lo(dve, U_XO + XO_AT.index(s - 1))
                if s == 13:
                    w_residual(0)
                if s == 14:
                    x3_mean(0)
            xp_evac(dve, V.tensor_copy, TT * XH - 1)
            normalise(f"xpv{TT - 1}", 32 + XH * (TT - 1), XH, XD, TT - 1)
            x3_rows(0)
            w_residual(1)
            x3_mean(1)
            xo_lo(TT - 1)
            x3_rows(1)
            w_residual(2)
            x_lo("x3", 0)
            split_lo(dve, U_UP)
            x_lo("x3", 1)
            x3_mean(2)
            split_lo(dve, U_UP + 1)
            w_residual(3)
            x3_rows(2)
            split_lo(dve, U_UP + 2)
            x3_mean(3)
            split_lo(dve, U_UP + 3)
            x3_rows(3)
            x_lo("x3", 2)
            x_lo("x3", 3)
            before_up = n_step[0]

            def up_round(i):
                for j in range(4):
                    p = read(dve, f"f{j}", i)
                    dve.wait_ge(conv_ready, i * 4 + (j + 1))
                    o = cv[:, j, :]
                    tap = [ccol_flat[:, bass.ds(i * 2 + (c * 2 * FT + j % 2 + FT * (j // 2)), 1)] for c in (0, 1)]
                    stt(o[:, 1:], p[:, 0:T - 1], tap[1], o[:, 1:], ALU.mult, ALU.add).then_inc(dve_step, 1)
                    dve.wait_ge(dve_step, i * 4 + (before_up + j + 1))
                    drained(stt(o[:, 2:], p[:, 0:T - 2], tap[0], o[:, 2:], ALU.mult, ALU.add), f"f{j}")
                    split_next(dve, split_lo, i, j)
                    if j >= 2:
                        after_drain(dve, f"f{j}", i)
                        dve.wait_ge(gate_ready, i * 2 + (j - 1))
                        tt(hff_flat[:, bass.ds(i * (2 * T) + (j - 2) * T, T)], cv[:, j - 2, :], o, ALU.mult)\
                            .then_inc(hff_ready, 1)

            before_down = n_hi[0]

            def down_lo(n, r=0):
                at = slice(n % 4 * 512, n % 4 * 512 + 512)
                dve.wait_ge(act_hi, r * 4 + (before_down + n + 1))
                tt(bs[:, 1, at], hff_flat[:, bass.ds(r * (4 * T) + n * T, T)], bs[:, 0, at].bitcast(f32), ALU.subtract)\
                    .then_inc(act_lo, 1)

            with dve.Fori(0, FT // 2 - 1) as i:
                up_round(i)
            for n in range(4):
                down_lo(n)
            up_round(FT // 2 - 1)
            with dve.Fori(0, FT // 4 - 1) as r:
                for n in range(4, 8):
                    split_lo(dve, U_DOWN + n, r)
                    down_lo(n, r)
            for n in range(FT // 4 * 4, FT):
                split_lo(dve, U_DOWN + n)
                down_lo(n)
            for b in range(8):
                t, half = b // 2, b % 2
                o = hres[:, t, half * 512:(half + 1) * 512]
                tt(o, o, read(dve, f"d{b}")[:, :], ALU.add).then_inc(res_ready, 1)

        @block.tensor
        def _(pe):
            def mm(o, l, r, start=True, stop=True):
                return nc.tensor.matmul(o, l, r, start=start, stop=stop)

            def tr(o, i):
                return nc.tensor.transpose(o, i, ident[0:i.shape[0], 0:i.shape[0]])

            def used(ins, u):
                if u in DONE:
                    filled(ins, DONE[u])
                else:
                    ins.then_inc(unit_used, 1)

            def cols_unit(u, kts, xhi, bank_names):
                pe.wait_ge(lo_done, u + 1)
                wh, wl = w_unit(u, 0), w_unit(u, 1)
                for i, name in enumerate(bank_names):
                    p = fill(pe, name)
                    for k in range(kts):
                        at = slice(i * 128, (i + 1) * 128)
                        last = mm3(p[:, :], wh[:, k, at], wl[:, k, at], xhi(0, k), xhi(1, k), k == 0, k == kts - 1)
                    filled(last, name)

            def rows_unit(u, u0, units, act_tile, tiles, names):
                pe.wait_ge(lo_done, u + 1)
                j = u - u0
                for t in range(tiles):
                    if j == 0:
                        fill(pe, names[t])
                    p = pb[uses[names[t]][0]]
                    for k in range(2):
                        kk = 2 * j + k
                        last = mm3(p[:, :], act_tile(0, kk, t), act_tile(1, kk, t), w_unit(u, 0)[:, k, :],
                                   w_unit(u, 1)[:, k, :], kk == 0, kk == 2 * units - 1)
                    if j == units - 1:
                        filled(last, names[t])
                if j < units - 1:
                    last.then_inc(unit_used, 1)

            x_tile = lambda part, k, t: xs[:, part, k, t * 128:(t + 1) * 128]
            m_tile = lambda part, k, t: bs[:, part, k * M + t * 128:k * M + (t + 1) * 128]
            o_tile = lambda part, k, t: bs[:, part, k * 512 + t * 128:k * 512 + (t + 1) * 128]
            names = lambda pre, n: [f"{pre}{t}" for t in range(n)]

            def proj(u, u0, pre):
                rows_unit(u, u0, 4, x_tile, TT, names(pre, TT))

            pe.wait_ge(ident_ok, 1)
            pe.wait_ge(par_in, 64)
            pe.wait_ge(step_row, 1)
            p = fill(pe, "lam")
            for i in range(3):
                tr(p[:, i * GP:(i + 1) * GP], prow[:, i, :])
            filled(tr(p[:, 3 * GP:3 * GP + KD], nrow[:, :]), "lam")
            for t in range(TT):
                pe.wait_ge(x_in[t], 16)
                for d in range(KD):
                    p = fill(pe, f"x{d}") if t == 0 else pb[d]
                    last = tr(p[:, t * 128:(t + 1) * 128], xr[:, t, d * 128:(d + 1) * 128])
                    if t == TT - 1:
                        filled(last, f"x{d}")
            pe.wait_ge(lo_done, 1)
            p = fill(pe, "u0")
            for d in range(KD):
                after_drain(pe, f"x{d}")
                last = mm3(p[:, :], w_unit(0, 0)[:, d, :], w_unit(0, 1)[:, d, :], xs[:, 0, d, :], xs[:, 1, d, :],
                           d == 0, d == KD - 1)
            filled(last, "u0")

            def u_unit(m):
                cols_unit(U_SSM + m, KD, lambda part, k: xs[:, part, k, :], [f"u{m}"])

            def token_factors(name, event):
                p = fill(pe, name)
                for t in range(TT):
                    cc = EVC[event] + t
                    last = mm(p[:, t * 128:(t + 1) * 128], rs[:, cc:cc + 1].to_broadcast([128, 128]), ident[:, :])
                filled(last, name)

            u_unit(1)
            pe.wait_ge(xr_ready, 1)
            token_factors("xb", "x")
            pe.wait_ge(gain_in, 16 * N_GAIN)
            pe.wait_ge(conv_in, 16 * 4)
            p = fill(pe, "par")
            tr(p[:, 0:NG], grow[:, :])
            tr(p[:, 64:152], crow[:, 0, :])
            filled(tr(p[:, 152:240], crow[:, 1, :]), "par")
            pe.wait_ge(c_in, 16 * 4)
            for i, name in enumerate(("cr", "cm")):
                p = fill(pe, name)
                for a in range(4):
                    last = tr(p[:, a * 128:(a + 1) * 128], craw[:, i, a, :])
                filled(last, name)
            pe.wait_ge(relb_in, 32)
            pe.wait_ge(relb_ok, 1)
            p = fill(pe, "relb")
            filled(mm(p[0:H, 0:384], relb[:, :], qk[0:NB + 1, 3, 0:384]), "relb")

            def transposes(pre, count, base, src, tiles=TT):
                pe.wait_ge(xn_ready, base)
                for d in range(count):
                    p = fill(pe, f"{pre}{d}")
                    for t in range(tiles):
                        last = tr(p[:, t * 128:(t + 1) * 128], src(d, t))
                    filled(last, f"{pre}{d}")

            u_unit(2)
            u_unit(3)
            transposes("m", 4, MT, lambda i, j: memr[:, j % 2, (2 * i + j // 2) * 128:(2 * i + j // 2 + 1) * 128])

            def weights_in(q):
                pe.wait_ge(w1p_ready, q + 1)
                for i, n in enumerate("ri"):
                    p = fill(pe, f"w1{n}{q}")
                    for g in range(QP):
                        last = tr(p[:, g * 128:(g + 1) * 128], w1p[:, i, g * 128:(g + 1) * 128])
                    filled(last, f"w1{n}{q}")
                pe.wait_ge(ca_ready, q + 1)
                p = [fill(pe, f"k{n}{q}") for n in "ab"]
                for a in range(QP):
                    at = slice(a * (L + 1) * CG, a * (L + 1) * CG + L * CG)
                    for part in range(2):
                        for b in range(2):
                            rows = slice(b * NS, (b + 1) * NS)
                            last = mm(p[b][0:CG, a * 128:(a + 1) * 128], bb[rows, part, q * QP + a, :],
                                      ca[rows, q % 2, part, at], part == 0, part == 1)
                            if a == QP - 1 and part == 1:
                                filled(last, f"k{'ab'[b]}{q}")

            def states_in(q):
                pe.wait_ge(u_in, 16 * L)
                after_drain(pe, f"w1r{q}")
                after_drain(pe, f"w1i{q}")
                for i, n in enumerate("ri"):
                    p = fill(pe, f"v{n}{q}")
                    for g in range(QG):
                        rows, gp = slice(g % 2 * NS, g % 2 * NS + NS), g // 2
                        last = mm(p[rows, gp * NC:(gp + 1) * NC],
                                  w1[:, q % 2, i, gp * 128 + g % 2 * NS:gp * 128 + g % 2 * NS + NS],
                                  ub[:, q * QG + g, :])
                    filled(last, f"v{n}{q}")

            def outputs(q):
                pe.wait_ge(t_in[q], 16 * L)
                pe.wait_ge(z_ready, q + 1)
                p = [fill(pe, f"y{n}{q}") for n in "eo"]
                for a in range(QP):
                    for b in range(2):
                        g = 2 * a + b
                        mm(p[b][:, a * NC:(a + 1) * NC], toep[:, g, :], ub[:, q * QG + g, :], True, False)
                    at = slice((a * (L + 1) + 1) * CG, (a + 1) * (L + 1) * CG)
                    for part in range(2):
                        for b in range(2):
                            rows = slice(b * NS, (b + 1) * NS)
                            last = mm(p[b][:, a * NC + 1:(a + 1) * NC], ca[rows, q % 2, part, at],
                                      zb[rows, part, a, 0:NC - 1], False, part == 1)
                            if a == QP - 1 and part == 1:
                                filled(last, f"y{'eo'[b]}{q}")

            def head_transposes(pre, base, src, tiles=TT):
                for t in range(tiles):
                    pe.wait_ge(xn_ready, base + t + 1)
                    p = fill(pe, f"{pre}{t}")
                    for a in range(4):
                        last = tr(p[:, a * 128:(a + 1) * 128], src[:, t, a * 128:(a + 1) * 128])
                    filled(last, f"{pre}{t}")

            proj(4, U_Q, "q")
            proj(5, U_Q, "q")
            weights_in(0)
            proj(6, U_Q, "q")
            states_in(0)
            proj(7, U_Q, "q")
            weights_in(1)
            proj(8, U_K, "k")
            outputs(0)
            states_in(1)
            proj(9, U_K, "k")
            N0 = MT
            head_transposes("qt", N0, qk)
            weights_in(2)
            proj(10, U_K, "k")
            outputs(1)
            states_in(2)
            proj(11, U_K, "k")
            weights_in(3)
            proj(12, U_V, "v")
            outputs(2)
            states_in(3)
            proj(13, U_V, "v")
            head_transposes("kt", N0 + TT, qk)
            proj(14, U_V, "v")
            outputs(3)
            proj(15, U_V, "v")

            def scores(s):
                qt, h = s // H, s % H
                rows = slice(h % 2 * HD, h % 2 * HD + HD)
                p = fill(pe, f"sc{s}")
                n = (qt + 1) * 128
                filled(mm(p[:, 0:n], qT[rows, h // 2, qt * 128:(qt + 1) * 128], kT[rows, h // 2, 0:n]), f"sc{s}")

            def prob_transposes(pre, sc, s, tiles):
                after_drain(pe, f"{sc}{s}")
                p = fill(pe, f"{pre}{s}")
                for a in range(tiles):
                    last = tr(p[:, a * 128:(a + 1) * 128], pbuf[:, s % 2, a * 128:(a + 1) * 128])
                filled(last, f"{pre}{s}")

            def values(s, heads, width, pt, bank, tiles, v):
                t, h = s // heads, s % heads
                after_drain(pe, f"{pt}{s}")
                p = fill(pe, f"{bank}{t}") if h == 0 else pb[uses[f"{bank}{t}"][0]]
                for a in range(tiles):
                    last = mm(p[:, h * width:(h + 1) * width], ptb[:, s % 2, a * 128:(a + 1) * 128],
                              v[:, a, h * width:(h + 1) * width], a == 0, a == tiles - 1)
                if h == heads - 1:
                    filled(last, f"{bank}{t}")
                else:
                    last.then_inc(pv_done, 1)

            for t in range(TT):
                after_drain(pe, f"qt{t}")
                after_drain(pe, f"kt{t}")
                after_drain(pe, f"v{t}")
            NMK = N0 + 2 * TT + MT

            def glu_tile(m):
                u, at = U_GLU + m // 2, slice(m % 2 * 128, m % 2 * 128 + 128)
                pe.wait_ge(lo_done, u + 1)
                p = fill(pe, f"z{m}")
                for k in range(4):
                    last = mm3(p[:, :], w_unit(u, 0)[:, k, at], w_unit(u, 1)[:, k, at], xs[:, 0, 4 + k, :],
                               xs[:, 1, 4 + k, :], k == 0, k == 3)
                filled(last, f"z{m}")

            def piece(t, i, u0, units, act_tile, name):
                u, (half, j) = u0 + i, divmod(i, units)
                if t == 0:
                    pe.wait_ge(lo_done, u + 1)
                p = fill(pe, name(t, half)) if j == 0 else pb[uses[name(t, half)][0]]
                for k in range(2):
                    kk = 2 * j + k
                    last = mm3(p[:, :], act_tile(0, kk, t), act_tile(1, kk, t), w_unit(u, 0)[:, k, :],
                               w_unit(u, 1)[:, k, :], kk == 0, kk == 2 * units - 1)
                if j == units - 1:
                    filled(last, name(t, half))
                elif t == TT - 1:
                    last.then_inc(unit_used, 1)

            def sout_piece(n):
                piece(n // 4, n % 4, U_OUT, 2, x_tile, lambda t, half: f"g{t}{half}")

            def tile_transposes(name, src):
                p = fill(pe, name)
                for a in range(4):
                    last = tr(p[:, a * 128:(a + 1) * 128], src[:, a * 128:(a + 1) * 128])
                filled(last, name)

            def ya_transposes(t):
                after_drain(pe, f"pv{t}")
                tile_transposes(f"ya{t}", yrow[:, t, :])

            scores(0)
            scores(1)
            for s in range(TT * H):
                if s + 2 < TT * H:
                    scores(s + 2)
                if s in MK_AT:
                    rows_unit(U_MK + MK_AT.index(s), U_MK, 4, m_tile, MT, names("mk", MT))
                if s in GLU_AT:
                    if s == GLU_AT[0]:
                        pe.wait_ge(glu_in, NQ)
                    glu_tile(GLU_AT.index(s))
                if s in MV_AT:
                    rows_unit(U_MV + MV_AT.index(s), U_MV, 4, m_tile, MT, names("mv", MT))
                if s == SOUT_AT[0]:
                    after_drain(pe, "bc")
                for n in range(4 * TT):
                    if SOUT_AT[n] == s:
                        sout_piece(n)
                prob_transposes("pt", "sc", s, s // H + 1)
                if s >= 1:
                    values(s - 1, H, HD, "pt", "pv", (s - 1) // H + 1, vrow)
                if s in YA_AT:
                    ya_transposes(YA_AT.index(s))
                if s == 15:
                    pe.wait_ge(ones_ok, 1)
                    pe.wait_ge(ysq_ready, 4)
                    p = fill(pe, "ss")
                    for t in range(TT):
                        for c in range(4):
                            last = mm(p[:, t:t + 1], sg[:, c, t * 128:(t + 1) * 128], ones[:, 0:1], c == 0, c == 3)
                    filled(last, "ss")
                if s == 21:
                    pe.wait_ge(xn_ready, NMK)
                    for i in range(2):
                        p = fill(pe, f"kx{i}")
                        for h in range(2):
                            for t in range(MT):
                                last = tr(p[:, h * M + t * 128:h * M + (t + 1) * 128],
                                          mkrow[:, t, (2 * i + h) * XD:(2 * i + h + 1) * XD])
                        filled(last, f"kx{i}")
                if s == 18:
                    pe.wait_ge(ssr_ready, 1)
                    token_factors("bc", "ss")
            values(TT * H - 1, H, HD, "pt", "pv", TT, vrow)

            def out_piece(t, i):
                piece(t, i, U_OA, 2, lambda part, k, t: x_tile(part, 4 + k, t), lambda t, half: f"o{t}{half}")

            def xq_piece(t, i):
                piece(t, i, U_XQ, 4, x_tile, lambda t, half: f"qx{t}")

            def xo_piece(t, i):
                piece(t, i, U_XO, 2, o_tile, lambda t, half: f"w{t}{half}")

            def h_transposes(name, t, src):
                for half in range(2):
                    tile_transposes(f"{name}{t}{half}", src[:, half * 512:(half + 1) * 512])

            def x2_transposes(t):
                after_drain(pe, f"o{t}0")
                after_drain(pe, f"o{t}1")
                h_transposes("x2", t, hres[:, t, :])

            for t in range(TT):
                if t == 1:
                    ya_transposes(TT - 1)
                after_drain(pe, f"ya{t}")
                for i in range(4):
                    out_piece(t, i)
                if t >= 1:
                    x2_transposes(t - 1)
            def x2_ready(t):
                after_drain(pe, f"x2{t}0")
                after_drain(pe, f"x2{t}1")

            for t in range(2):
                x2_ready(t)
                for i in range(4):
                    xq_piece(t, i)
                if t == 0:
                    x2_transposes(TT - 1)

            def qx_transposes(t):
                pe.wait_ge(xn_ready, NMK + t + 1)
                tile_transposes(f"qxt{t}", qk[:, t, :])

            def x_scores(s):
                t, h = s // XH, s % XH
                if h == 0:
                    after_drain(pe, f"qxt{t}")
                p = fill(pe, f"xs{s}")
                filled(mm(p[:, 0:M], qT[:, h, t * 128:(t + 1) * 128], kxT[:, h, :]), f"xs{s}")

            def xo_transposes(t):
                after_drain(pe, f"xpv{t}")
                tile_transposes(f"xo{t}", yrow[:, t, :])

            def x3_transposes(t):
                pe.wait_ge(xn_ready, NMK + TT + t + 1)
                h_transposes("x3", t, x3row[:, t % 2, :])

            after_drain(pe, "kx0")
            after_drain(pe, "kx1")
            after_drain(pe, "mv0")
            after_drain(pe, "mv1")
            qx_transposes(0)
            x2_ready(2)
            xq_piece(2, 0)
            xq_piece(2, 1)
            x_scores(0)
            x_scores(1)
            for s in range(TT * XH):
                if s in (1, 5, 9):
                    qx_transposes(1 + s // 4)
                if s + 2 < TT * XH:
                    x_scores(s + 2)
                if s < 2 * XH - 2:
                    if s == 2:
                        x2_ready(3)
                    xq_piece((s + 2) // XH + 2, (s + 2) % XH)
                elif s >= 2 * XH:
                    if s % XH == 0:
                        after_drain(pe, f"xo{s // XH - 2}")
                    xo_piece(s // XH - 2, s % XH)
                prob_transposes("xp", "xs", s, MT)
                if s >= 1:
                    values(s - 1, XH, XD, "xp", "xpv", MT, xv)
                if s in (6, 10, 14):
                    xo_transposes((s - 6) // 4)
            values(TT * XH - 1, XH, XD, "xp", "xpv", MT, xv)
            after_drain(pe, "xo2")
            for i in range(4):
                xo_piece(2, i)
                if i == 1:
                    xo_transposes(3)
            x3_transposes(0)
            after_drain(pe, "xo3")
            for i in range(4):
                xo_piece(3, i)
                if i == 1:
                    x3_transposes(1)

            def up_half(k, half):
                u, at = U_UP + k, slice(half * 256, half * 256 + 256)
                if half == 0:
                    pe.wait_ge(lo_done, u + 1)
                    fill(pe, f"f{k}")
                p = pb[uses[f"f{k}"][0]]
                for kk in range(KD):
                    last = mm3(p[:, at], w_unit(u, 0)[:, kk, :], w_unit(u, 1)[:, kk, :], xs[:, 0, kk, at],
                               xs[:, 1, kk, at], kk == 0, kk == KD - 1)
                if half == 1:
                    filled(last, f"f{k}")

            for half in range(2):
                for t in (2 * half, 2 * half + 1):
                    after_drain(pe, f"x3{t}0")
                    after_drain(pe, f"x3{t}1")
                for k in range(4):
                    up_half(k, half)
                    if half == 0 and k in (1, 2):
                        x3_transposes(1 + k)
            with pe.Fori(1, FT // 2) as i:
                for j in range(4):
                    pe.wait_ge(lo_done, i * 4 + (U_UP + j + 1))
                    p = fill(pe, f"f{j}", i)
                    for kk in range(KD):
                        last = mm3(p[:, :], w_unit(U_UP + j, 0)[:, kk, :], w_unit(U_UP + j, 1)[:, kk, :],
                                   xs[:, 0, kk, :], xs[:, 1, kk, :], kk == 0, kk == KD - 1)
                    filled(last, f"f{j}")
            def down_unit(n, r=0):
                u = U_DOWN + n
                pe.wait_ge(lo_done, r * 4 + (u + 1))
                pe.wait_ge(act_lo, r * 4 + (n + 1))
                for b in range(8):
                    t, half = b // 2, b % 2
                    p = fill(pe, f"d{b}") if n == 0 else pb[b]
                    at = slice(n % 4 * 512 + t * 128, n % 4 * 512 + (t + 1) * 128)
                    cols = slice(half * 512, (half + 1) * 512)
                    last = mm3(p[:, :], bs[:, 0, at], bs[:, 1, at], w_unit(u, 0)[:, 0, cols], w_unit(u, 1)[:, 0, cols],
                               n == 0, n == FT - 1)
                    if n == FT - 1:
                        filled(last, f"d{b}")
                if n < FT - 1:
                    last.then_inc(unit_used, 1)

            down_unit(0)
            with pe.Fori(0, (FT - 2) // 4) as r:
                for n in range(1, 5):
                    down_unit(n, r)
            down_unit(FT - 1)


INPUTS = ["x", "mem", "norm_mix", "w_in", "attn_qn", "attn_kn", "ssm_lam_re", "ssm_lam_im", "ssm_log_step",
          "ssm_b_re", "ssm_b_im", "ssm_c_re", "ssm_c_im", "ssm_d", "ssm_w_glu", "ssm_b_glu", "gnorm_ssm",
          "gnorm_attn", "w_out", "rel_bias", "norm_xattn", "norm_mem", "x_wq", "x_wkv", "x_wo", "x_qn",
          "x_kn", "norm_ffn", "ffn_w_up", "ffn_conv_w", "ffn_conv_b", "ffn_w_down"]


def kernel(**inputs):
    import concourse.bacc as bacc
    from concourse.bass_utils import run_bass_kernel_spmd

    nc = bacc.Bacc("TRN2", target_bir_lowering=False, num_devices=1)
    arrays, aps = {}, {}
    for name in INPUTS:
        a = np.ascontiguousarray(inputs[name])
        arrays[f"in_{name}"] = a
        aps[name] = nc.dram_tensor(f"in_{name}", a.shape, mybir.dt.from_np(a.dtype), kind="ExternalInput").ap()
    arrays["in_buckets"] = bucket_table()
    aps["buckets"] = nc.dram_tensor("in_buckets", (NB + 1, 384), mybir.dt.float32, kind="ExternalInput").ap()
    out = nc.dram_tensor("out_0", (1, T, D), mybir.dt.float32, kind="ExternalOutput").ap()
    layer(nc, aps, out)
    r = run_bass_kernel_spmd(nc, [arrays], core_ids=[0])
    return r.results[0]["out_0"]
```
